# Optimizing a Trainium2 kernel written in Bass

```python
import jax, jax.numpy as jnp
from jax import lax
import numpy as np

D_MODEL = 2048
BATCH = 1
SEQ = 256
DEPTH = 1

CHUNK = 64
N_META = 16
MIX_DIM = D_MODEL
MLA_HEADS = 8
D_NOPE = 128
D_ROPE = 64
D_QK = D_NOPE + D_ROPE
D_V = 128
Q_RANK = 384
KV_RANK = 512
ROPE_THETA = 10000.0
ATTN_DIM = MLA_HEADS * D_V
Q_BLOCK = 128
CONV_DIM = MIX_DIM - ATTN_DIM
CONV_WIDTH = 3
IN_DIM = Q_RANK + KV_RANK + D_ROPE + 3 * CONV_DIM
PEER_HEADS = 8
N_KEYS = 128
N_EXPERTS = N_KEYS * N_KEYS
D_KEY = 256
D_HALF = D_KEY // 2
PEER_TOPK = 16
PEER_BLOCK = 128
DEEPNORM_ALPHA = (2.0 * DEPTH) ** 0.25
DEEPNORM_BETA = (8.0 * DEPTH) ** -0.25
EPS = 1e-5
NEG_INF = -1e30

kernel_name = "hybrid_mla_shortconv_peer_deepnorm"

def layer_norm(x, g, b):
    xf = x.astype(jnp.float32)
    mu = jnp.mean(xf, axis=-1, keepdims=True)
    var = jnp.mean(jnp.square(xf - mu), axis=-1, keepdims=True)
    return ((xf - mu) * lax.rsqrt(var + EPS) * g.astype(jnp.float32) + b.astype(jnp.float32)).astype(x.dtype)

def rms_norm(x, g):
    xf = x.astype(jnp.float32)
    r = lax.rsqrt(jnp.mean(jnp.square(xf), axis=-1, keepdims=True) + EPS)
    return (xf * r * g.astype(jnp.float32)).astype(x.dtype)

def rope_tables(n_pos, dtype):
    inv = 1.0 / (ROPE_THETA ** (jnp.arange(0, D_ROPE, 2, dtype=jnp.float32) / D_ROPE))
    ang = jnp.arange(n_pos, dtype=jnp.float32)[:, None] * inv[None, :]
    return jnp.cos(ang).astype(dtype), jnp.sin(ang).astype(dtype)

def apply_rope(x, cos, sin):
    x1, x2 = jnp.split(x, 2, axis=-1)
    return jnp.concatenate([x1 * cos - x2 * sin, x1 * sin + x2 * cos], axis=-1)

def chunk_ids(n_pos):
    p = jnp.arange(n_pos)
    return jnp.where(p < N_META, 0, (p - N_META) // CHUNK + 1)

def mla_scores(qn, qr, kn, kr):
    s = jnp.einsum('bqhd,bkhd->bhqk', qn, kn) + jnp.einsum('bqhd,bkd->bhqk', qr, kr)
    return s.astype(jnp.float32)

def mla_attention(c_q, c_kv, k_rope, q_norm_g, kv_norm_g, w_uq, w_ukv, cos, sin):
    B, L, _ = c_q.shape
    n_real = L - N_META
    q = (rms_norm(c_q, q_norm_g) @ w_uq).reshape(B, L, MLA_HEADS, D_QK)
    kv = (rms_norm(c_kv, kv_norm_g) @ w_ukv).reshape(B, L, MLA_HEADS, D_NOPE + D_V)
    k_nope, v = kv[..., :D_NOPE], kv[..., D_NOPE:]
    scale = D_QK ** -0.5
    q_nope = q[..., :D_NOPE] * scale
    q_rot = apply_rope(q[..., D_NOPE:], cos[:, None, :], sin[:, None, :]) * scale
    k_rot = apply_rope(k_rope, cos, sin)
    kchunk = chunk_ids(L)

    s_meta = mla_scores(q_nope[:, :N_META], q_rot[:, :N_META], k_nope[:, :N_META], k_rot[:, :N_META])
    p_meta = jax.nn.softmax(s_meta, axis=-1).astype(v.dtype)
    o_meta = jnp.einsum('bhqk,bkhd->bqhd', p_meta, v[:, :N_META])

    n_blk = n_real // Q_BLOCK
    def to_blocks(t):
        return t[:, N_META:].reshape(B, n_blk, Q_BLOCK, *t.shape[2:]).swapaxes(0, 1)

    def attend_block(args):
        qn_b, qr_b, blk = args
        s = mla_scores(qn_b, qr_b, k_nope, k_rot)
        qchunk = (blk * Q_BLOCK + jnp.arange(Q_BLOCK)) // CHUNK + 1
        visible = kchunk[None, :] <= qchunk[:, None]
        p = jax.nn.softmax(jnp.where(visible[None, None], s, NEG_INF), axis=-1).astype(v.dtype)
        return jnp.einsum('bhqk,bkhd->bqhd', p, v)

    o_real = lax.map(attend_block, (to_blocks(q_nope), to_blocks(q_rot), jnp.arange(n_blk)))
    o_real = o_real.swapaxes(0, 1).reshape(B, n_real, MLA_HEADS, D_V)
    o = jnp.concatenate([o_meta, o_real], axis=1)
    return o.reshape(B, L, ATTN_DIM)

def short_conv(b_gate, c_gate, h, conv_w):
    L = h.shape[1]
    u = jnp.pad(c_gate * h, ((0, 0), (CONV_WIDTH - 1, 0), (0, 0)))
    y = sum(u[:, j:j + L] * conv_w[j] for j in range(CONV_WIDTH))
    return b_gate * y

def peer_ffn(x, w_query, sub_keys, expert_u, expert_v):
    T = x.shape[0]
    n_blk = -(-T // PEER_BLOCK)
    xp = jnp.pad(x, ((0, n_blk * PEER_BLOCK - T), (0, 0))).reshape(n_blk, PEER_BLOCK, D_MODEL)

    def block(xb):
        q = (xb @ w_query).reshape(PEER_BLOCK, PEER_HEADS, 2, D_HALF)
        s = jnp.einsum('thcd,ckd->thck', q, sub_keys).astype(jnp.float32)
        top_s, top_i = lax.top_k(s, PEER_TOPK)
        cand = top_s[:, :, 0, :, None] + top_s[:, :, 1, None, :]
        cand = cand.reshape(PEER_BLOCK, PEER_HEADS, PEER_TOPK * PEER_TOPK)
        best_s, best_c = lax.top_k(cand, PEER_TOPK)
        i1 = jnp.take_along_axis(top_i[:, :, 0], best_c // PEER_TOPK, axis=-1)
        i2 = jnp.take_along_axis(top_i[:, :, 1], best_c % PEER_TOPK, axis=-1)
        idx = i1 * N_KEYS + i2
        g = jax.nn.softmax(best_s, axis=-1)
        u = expert_u[idx]
        a = jax.nn.gelu(jnp.einsum('thkd,td->thk', u, xb).astype(jnp.float32), approximate=False)
        w = (g * a).astype(xb.dtype)
        return jnp.einsum('thk,thkd->td', w, expert_v[idx])

    return lax.map(block, xp).reshape(n_blk * PEER_BLOCK, D_MODEL)[:T]

def setup_inputs(seed: int = 0) -> dict:
    key = jax.random.key(seed)
    ks = jax.random.split(key, 24)
    f32 = jnp.float32
    def nrm(k, shape, scale):
        return jax.random.normal(k, shape, f32) * scale
    def gain(k, shape):
        return 1.0 + 0.02 * jax.random.normal(k, shape, f32)
    return {
        "x": nrm(ks[0], (BATCH, SEQ, D_MODEL), 1.0),
        "meta_tokens": nrm(ks[1], (N_META, D_MODEL), 1.0),
        "ln0_g": gain(ks[2], (D_MODEL,)),
        "ln0_b": nrm(ks[3], (D_MODEL,), 0.02),
        "w_in": nrm(ks[4], (DEPTH, D_MODEL, IN_DIM), D_MODEL ** -0.5),
        "q_norm_g": gain(ks[5], (DEPTH, Q_RANK)),
        "kv_norm_g": gain(ks[6], (DEPTH, KV_RANK)),
        "w_uq": nrm(ks[7], (DEPTH, Q_RANK, MLA_HEADS * D_QK), Q_RANK ** -0.5),
        "w_ukv": nrm(ks[8], (DEPTH, KV_RANK, MLA_HEADS * (D_NOPE + D_V)), KV_RANK ** -0.5),
        "conv_w": nrm(ks[9], (DEPTH, CONV_WIDTH, CONV_DIM), CONV_WIDTH ** -0.5),
        "attn_out_g": gain(ks[10], (DEPTH, ATTN_DIM)),
        "conv_out_g": gain(ks[11], (DEPTH, CONV_DIM)),
        "w_o": nrm(ks[12], (DEPTH, MIX_DIM, D_MODEL), MIX_DIM ** -0.5 * DEEPNORM_BETA),
        "ln1_g": gain(ks[13], (DEPTH, D_MODEL)),
        "ln1_b": nrm(ks[14], (DEPTH, D_MODEL), 0.02),
        "peer_w_query": nrm(ks[15], (DEPTH, D_MODEL, PEER_HEADS * D_KEY), D_MODEL ** -0.5),
        "peer_sub_keys": nrm(ks[16], (DEPTH, 2, N_KEYS, D_HALF), D_HALF ** -0.5),
        "peer_u": nrm(ks[17], (DEPTH, N_EXPERTS, D_MODEL), D_MODEL ** -0.5),
        "peer_v": nrm(ks[18], (DEPTH, N_EXPERTS, D_MODEL), DEEPNORM_BETA),
        "ln2_g": gain(ks[19], (DEPTH, D_MODEL)),
        "ln2_b": nrm(ks[20], (DEPTH, D_MODEL), 0.02),
    }

def reference(x, meta_tokens, ln0_g, ln0_b, w_in, q_norm_g, kv_norm_g, w_uq, w_ukv, conv_w,
              attn_out_g, conv_out_g, w_o, ln1_g, ln1_b, peer_w_query, peer_sub_keys,
              peer_u, peer_v, ln2_g, ln2_b):
    B = x.shape[0]
    meta = jnp.broadcast_to(meta_tokens[None].astype(x.dtype), (B, N_META, D_MODEL))
    h = layer_norm(jnp.concatenate([meta, x], axis=1), ln0_g, ln0_b)
    L = h.shape[1]
    cos, sin = rope_tables(L, h.dtype)
    splits = np.cumsum([Q_RANK, KV_RANK, D_ROPE, CONV_DIM, CONV_DIM]).tolist()
    for layer in range(DEPTH):
        proj = h @ w_in[layer]
        c_q, c_kv, k_rope, b_gate, c_gate, h_conv = jnp.split(proj, splits, axis=-1)
        o_attn = mla_attention(c_q, c_kv, k_rope, q_norm_g[layer], kv_norm_g[layer],
                               w_uq[layer], w_ukv[layer], cos, sin)
        o_conv = short_conv(b_gate, c_gate, h_conv, conv_w[layer])
        mixed = jnp.concatenate([rms_norm(o_attn, attn_out_g[layer]),
                                 rms_norm(o_conv, conv_out_g[layer])], axis=-1) @ w_o[layer]
        h = layer_norm(DEEPNORM_ALPHA * h + mixed, ln1_g[layer], ln1_b[layer])
        f = peer_ffn(h.reshape(B * L, D_MODEL), peer_w_query[layer], peer_sub_keys[layer],
                     peer_u[layer], peer_v[layer]).reshape(B, L, D_MODEL)
        h = layer_norm(DEEPNORM_ALPHA * h + f, ln2_g[layer], ln2_b[layer])
    return h[:, N_META:]


_drawn_inputs = setup_inputs


def setup_inputs(seed=0):
    import zlib

    import numpy as np

    out = dict(_drawn_inputs(seed))
    spreads = {}
    factors = {}
    for name, (base, spread) in spreads.items():
        noise = np.random.default_rng([zlib.crc32(name.encode()), seed]).standard_normal(out[name].shape)
        drawn = base * np.exp(spread * noise) if base else spread * noise
        out[name] = __import__('jax').numpy.asarray(drawn.astype(out[name].dtype))
    for name, factor in factors.items():
        out[name] = (out[name] * factor).astype(out[name].dtype)
    return out
```

```python
from contextlib import ExitStack

import numpy as np

import concourse.bass as bass
from concourse import mybir

ALU = mybir.AluOpType
ACT = mybir.ActivationFunctionType
AX = mybir.AxisListType
F32 = mybir.dt.float32
U32 = mybir.dt.uint32

P = 128
D = 2048
KT = D // P
SEQ = 256
TT = SEQ // P
META = 16
L = META + SEQ
HEADS = 8
D_NOPE, D_ROPE, D_V = 128, 64, 128
D_QK = D_NOPE + D_ROPE
Q_RANK, KV_RANK = 384, 512
QT, KVT = Q_RANK // P, KV_RANK // P
CONV_DIM = 1024
CT = CONV_DIM // P
AT = HEADS * D_V // P
CONV_W = 3
CHUNK = 64
OFF_KR = Q_RANK + KV_RANK
OFF_B = OFF_KR + D_ROPE
OFF_C = OFF_B + CONV_DIM
OFF_H = OFF_C + CONV_DIM
N_KEYS = 128
TOPK = 16
ROWS = 2 * TOPK
RING = 8
ALPHA = 2.0 ** 0.25
EPS = 1e-5
SCALE = float(D_QK) ** -0.5
NEG = -1e30
THETA = 10000.0

C_ID, C_FOLD, C_ONES, C_ROPE = 0, 128, 256, 384
C_MASKQ = C_ROPE + L
C_MASKK = C_MASKQ + P
C_IOTA = C_MASKK + L
C_W = C_IOTA + TOPK

G_Q, G_KV, G_ATT, G_CONV, G_CW = 0, QT, QT + KVT, QT + KVT + AT, QT + KVT + AT + CT
G_N = G_CW + CONV_W * CT


def constants():
    c = np.zeros((P, C_W), np.float32)
    r = np.arange(P)
    c[:, C_ID:C_ID + P] = np.eye(P)
    c[:, C_FOLD:C_FOLD + P] = (r[:, None] % D_ROPE) == (r[None, :] % D_ROPE)
    c[:, C_ONES:C_ONES + P] = 1.0
    inv = (1.0 / (np.float32(THETA) ** (np.arange(0, D_ROPE, 2, dtype=np.float32) / D_ROPE))).astype(np.float32)
    ang = np.arange(L, dtype=np.float32)[None, :] * inv[:, None]
    cos, sin = np.cos(ang), np.sin(ang)
    c[:, C_ROPE:C_ROPE + L] = np.concatenate([cos, cos, -sin, sin])
    c[0, C_MASKQ:C_MASKQ + CHUNK] = 1.0
    c[0, C_MASKK + L - CHUNK:C_MASKK + L] = NEG
    c[:, C_IOTA:C_IOTA + TOPK] = np.arange(TOPK)
    return c


def build(nc, x, meta_tokens, ln0_g, ln0_b, w_in, q_norm_g, kv_norm_g, w_uq, w_ukv, conv_w, attn_out_g,
          conv_out_g, w_o, ln1_g, ln1_b, peer_w_query, peer_sub_keys, peer_u, peer_v, ln2_g, ln2_b,
          const_block, out):
    ctx = ExitStack()

    def sb(name, shape, dt=F32):
        return ctx.enter_context(nc.sbuf_tensor(name, shape, dt))

    def sem(name):
        return ctx.enter_context(nc.semaphore(name))

    with ctx:
        cst = sb("cst", [P, C_W])
        ring = sb("ring", [P, RING, D])
        hres = sb("hres", [P, TT, D])
        hT = sb("hT", [P, KT, L])
        gb = sb("gb", [P, 2, D])
        grows = sb("grows", [G_N, P])
        gains = sb("gains", [P, G_N])
        sk = sb("sk", [P, 2, P])
        skT = sb("skT", [P, 2, P])
        cq = sb("cq", [P, QT, SEQ])
        ckv = sb("ckv", [P, KVT, L])
        kr2 = sb("kr2", [P, L])
        krot = sb("krot", [P, L])
        sq = sb("sq", [P, 8, L])
        rs = sb("rs", [P, 4, L])
        stats = sb("stats", [P, 3, 4, 6])
        mv = sb("mv", [P, 3, 2])
        rstd = sb("rstd", [P, 3, 2])
        cgate = sb("cgate", [P, L])
        ubuf = sb("ubuf", [P, L])
        ybuf = sb("ybuf", [P, SEQ])
        mixT = sb("mixT", [P, AT + CT, SEQ])
        qn = sb("qn", [P, 2, SEQ])
        qrot = sb("qrot", [P, 2, SEQ])
        kn = sb("kn", [P, 2, L])
        vt = sb("vt", [P, 2, 3, P])
        pr = sb("pr", [P, 2, P + META + L])
        pT = sb("pT", [P, 2, 3, P])
        pTm = sb("pTm", [META, 2, 2, P])
        smx = sb("smx", [P, 2, 8])
        moT = sb("moT", [P, 2, SEQ])
        scores = sb("scores", [P, TT * HEADS + 1, 2, N_KEYS])
        acc = mixT[:, :, :].rearrange("p (t k) n -> p t (k n)", t=TT)
        sc = sb("sc", [P, 2, N_KEYS])
        sc2 = sb("sc2", [P, 2, N_KEYS])
        tv = sb("tv", [P, 2, TOPK])
        ti = sb("ti", [P, 2, TOPK], U32)
        tif = sb("tif", [P, 2, TOPK])
        cand = sb("cand", [P, TOPK * TOPK])
        cand2 = sb("cand2", [P, TOPK * TOPK])
        bv = sb("bv", [P, TOPK])
        bi = sb("bi", [P, TOPK], U32)
        bhl = sb("bhl", [P, 2, TOPK], U32)
        bhlf = sb("bhlf", [P, 2, TOPK])
        hot = sb("hot", [P, 2, TOPK, TOPK])
        isel = sb("isel", [P, 2, TOPK])
        idx = sb("idx", [P, 2, TOPK], U32)
        gex = sb("gex", [P, TOPK])
        gsm = sb("gsm", [P, 4])
        gate = sb("gate", [P, 2, TOPK])
        dots = sb("dots", [P, 2, TOPK])
        gel = sb("gel", [P, 2, TOPK])
        wgt = sb("wgt", [P, 2, TOPK])

        ps = [ctx.enter_context(nc.psum_tensor(f"ps{i}", [P, 512], F32)) for i in range(8)]

        ident = cst[:, C_ID:C_ID + P]
        ones = cst[:, C_ONES:C_ONES + P]
        rope = cst[:, C_ROPE:C_ROPE + L]
        wslot = [ring[:, s, :].rearrange("p (k n) -> p k n", k=KT) for s in range(RING)]
        metab = ring[0:META, RING - 1, :]

        consts_loaded = sem("consts_loaded")
        x_loaded = [sem(f"x_loaded{b}") for b in range(3)]
        gb_loaded = sem("gb_loaded")
        small_loaded = sem("small_loaded")
        w_loaded = [sem(f"w_loaded{s}") for s in range(3)]
        kr_loaded = sem("kr_loaded")
        att_w_loaded = [sem(f"att_w_loaded{b}") for b in range(2)]
        wo_loaded = [sem(f"wo_loaded{b}") for b in range(2)]
        wq_loaded = [sem(f"wq_loaded{b}") for b in range(2)]
        dve_step = sem("dve_step")
        var_ready = sem("var_ready")
        std_ready = sem("std_ready")
        h_ready = sem("h_ready")
        turned = sem("turned")
        turn_copied = sem("turn_copied")
        gains_turned = sem("gains_turned")
        gains_copied = sem("gains_copied")
        proj_done = sem("proj_done")
        bank_freed = [sem(f"bank_freed{b}") for b in range(3)]
        low_copied = sem("low_copied")
        squared = sem("squared")
        sums_ready = sem("sums_ready")
        ms_ready = sem("ms_ready")
        rms_ready = sem("rms_ready")
        normed = sem("normed")
        rr_ready = sem("rr_ready")
        kr2_ready = sem("kr2_ready")
        folded = sem("folded")
        krot_ready = sem("krot_ready")
        conv_step = sem("conv_step")
        qkv_done = sem("qkv_done")
        act_evac = sem("act_evac")
        dve_evac = sem("dve_evac")
        scored = sem("scored")
        att_step = sem("att_step")
        exped = sem("exped")
        p_ready = sem("p_ready")
        p_turned = sem("p_turned")
        pT_copied = sem("pT_copied")
        pTm_copied = sem("pTm_copied")
        pv_done = sem("pv_done")
        o_copied = sem("o_copied")
        wo_done = sem("wo_done")
        mo_copied = sem("mo_copied")
        mo_turned = sem("mo_turned")
        res_added = sem("res_added")
        wq_done = sem("wq_done")
        pq_copied = sem("pq_copied")
        keys_done = sem("keys_done")
        scores_kept = sem("scores_kept")
        pad_cleared = sem("pad_cleared")
        pick_step = sem("pick_step")
        pick_passed = sem("pick_passed")
        gather_passed = sem("gather_passed")
        idx_ready = sem("idx_ready")
        shifted = sem("shifted")
        gexp_ready = sem("gexp_ready")
        slots_free = sem("slots_free")
        row_landed = [sem(f"row_landed{s}") for s in range(RING)]
        gelu_ready = sem("gelu_ready")
        weight_ready = sem("weight_ready")
        acc_started = sem("acc_started")
        out_ready = sem("out_ready")
        stored = sem("stored")

        def win_block(slot, col):
            return wslot[slot], w_in[0].rearrange("(k p) n -> p k n", p=P)[:, :, bass.ds(col, P)]

        FIRST = QT + KVT + 1
        KR_TILE = FIRST - 1
        fills = [len([n for n in range(KR_TILE) if n % 3 == s]) for s in range(3)]
        uses = [len([n for n in range(FIRST) if n % 3 == s]) for s in range(3)]
        SC, SH, SB = FIRST % 3, (FIRST + 1) % 3, (FIRST + 2) % 3

        block = ctx.enter_context(nc.Block())

        @block.sync
        def _(sp):
            sp.dma_start(hres[:, 0, :], x[0, 0:P, :]).then_inc(x_loaded[0], 16)
            sp.dma_start(hres[:, 1, :], x[0, P:SEQ, :]).then_inc(x_loaded[1], 16)
            sp.dma_start(metab, meta_tokens[:, :]).then_inc(x_loaded[2], 16)
            sp.dma_start(cst[:, :], const_block[:, :]).then_inc(consts_loaded, 16)
            for n in range(FIRST):
                if n >= 3:
                    sp.wait_ge(proj_done, n - 2)
                if n < KR_TILE:
                    dst, src = win_block(n % 3, n * P)
                    sp.dma_start(dst, src).then_inc(w_loaded[n % 3], 16)
                else:
                    wv = w_in[0].rearrange("(k p) n -> p k n", p=P)
                    half = D_ROPE // 2
                    for to, frm, w in ((0, 0, D_ROPE), (D_ROPE, half, half), (D_ROPE + half, 0, half)):
                        sp.dma_start(wslot[n % 3][:, :, to:to + w],
                                     wv[:, :, OFF_KR + frm:OFF_KR + frm + w]).then_inc(kr_loaded, 16)
            with sp.Fori(0, CT) as i:
                for k, (slot, off) in enumerate(((SC, OFF_C), (SH, OFF_H), (SB, OFF_B))):
                    sp.wait_ge(proj_done, i * 3 + (FIRST + k - 2))
                    dst, src = win_block(slot, i * P + off)
                    sp.dma_start(dst, src).then_inc(w_loaded[slot], 16)
            with sp.Fori(0, KT // 2) as i:
                for b in range(2):
                    sp.wait_ge(wo_done, i * 2 + b) if b else sp.wait_ge(wo_done, i * 2)
                    sp.dma_start(wslot[3 + b], w_o[0].rearrange("(k p) n -> p k n", p=P)[
                        :, :, bass.ds(i * 2 * P + b * P, P)]).then_inc(wo_loaded[b], 16)
            sp.wait_ge(proj_done, FIRST + 3 * CT)
            with sp.Fori(0, HEADS) as i:
                for b in range(2):
                    sp.wait_ge(wq_done, i * 2 + b) if b else sp.wait_ge(wq_done, i * 2)
                    sp.dma_start(wslot[b], peer_w_query[0].rearrange("(k p) n -> p k n", p=P)[
                        :, :, bass.ds(i * 2 * P + b * P, P)]).then_inc(wq_loaded[b], 16)
            for t in range(TT):
                sp.wait_ge(out_ready, t + 1)
                sp.dma_start(out[0, t * P:(t + 1) * P, :], acc[:, t, :]).then_inc(stored, 16)
            sp.wait_ge(stored, 16 * TT)

        @block.gpsimd
        def _(pool):
            def load_gb(g, b):
                pool.dma_start(gb[:, 0, :], g.partition_broadcast(P)).then_inc(gb_loaded, 16)
                pool.dma_start(gb[:, 1, :], b.partition_broadcast(P)).then_inc(gb_loaded, 16)

            load_gb(ln0_g, ln0_b)
            for at, rows, src in ((G_Q, QT, q_norm_g[0]), (G_KV, KVT, kv_norm_g[0]), (G_ATT, AT, attn_out_g[0]),
                                  (G_CONV, CT, conv_out_g[0])):
                pool.dma_start(grows[at:at + rows, :], src.rearrange("(k p) -> k p", p=P)).then_inc(small_loaded, 16)
            pool.dma_start(grows[G_CW:G_N, :], conv_w[0].rearrange("j (k p) -> (j k) p", p=P)).then_inc(small_loaded, 16)
            pool.dma_start(sk[:, :, :], peer_sub_keys[0].rearrange("c k d -> k c d")).then_inc(small_loaded, 16)
            pool.memset(scores[:, TT * HEADS, :, :], 0.0).then_inc(pad_cleared, 1)

            def load_head(h, slot, wait):
                if wait is not None:
                    pool.wait_ge(qkv_done, wait)
                uq = ring[:, 5 + slot, 0:QT * 2 * P].rearrange("p (k n) -> p k n", k=QT)
                ukv = ring[:, 5 + slot, QT * 2 * P:(QT + KVT) * 2 * P].rearrange("p (k n) -> p k n", k=KVT)
                srcq = w_uq[0].rearrange("(k p) n -> p k n", p=P)
                half = D_ROPE // 2
                for to, frm, w in ((0, 0, D_QK), (D_QK, D_NOPE + half, half), (D_QK + half, D_NOPE, half)):
                    pool.dma_start(uq[:, :, to:to + w], srcq[:, :, bass.ds(h * D_QK + frm, w)]
                                   ).then_inc(att_w_loaded[slot], 16)
                pool.dma_start(ukv, w_ukv[0].rearrange("(k p) n -> p k n", p=P)[
                    :, :, bass.ds(h * (D_NOPE + D_V), D_NOPE + D_V)]).then_inc(att_w_loaded[slot], 16)

            load_head(0, 0, None)
            load_head(1, 1, None)
            pool.wait_ge(h_ready, 3)
            load_gb(ln1_g[0], ln1_b[0])
            with pool.Fori(1, HEADS // 2) as i:
                load_head(i * 2, 0, i * 6 - 3)
                load_head(i * 2 + 1, 1, i * 6)
            pool.wait_ge(h_ready, 5)
            load_gb(ln2_g[0], ln2_b[0])

            for t in range(TT):
                with pool.Fori(0, HEADS // 2) as i:
                    for b in range(2):
                        q = i * 2 + (t * HEADS + b)
                        pool.wait_ge(idx_ready, q + 1)
                        for m in range(ROWS):
                            table = peer_u if m < TOPK else peer_v
                            pool.wait_ge(slots_free, q * ROWS + (m + 1))
                            pool.sem_inc(gather_passed, 1)
                            pool.indirect_dma_start(
                                out=ring[:, m % RING, :], out_offset=None, in_=table[0],
                                in_offset=bass.IndirectOffsetOnAxis(ap=idx[:, b, m % TOPK:m % TOPK + 1], axis=0),
                            ).then_inc(row_landed[m % RING], 16)

        @block.tensor
        def _(pe):
            def mm(o, lhsT, rhs, k, n):
                return nc.tensor.matmul(o, lhsT, rhs, start=(k == 0), stop=(k == n - 1))

            pe.wait_ge(consts_loaded, 16)
            pe.wait_ge(small_loaded, 16 * 6)
            nc.tensor.transpose(ps[7][:, 256:256 + G_N], grows[:, :], ident[0:G_N, 0:G_N]).then_inc(gains_turned, 1)
            for c in range(2):
                nc.tensor.transpose(ps[7][:, c * P:(c + 1) * P], sk[:, c, :], ident).then_inc(gains_turned, 1)

            turns = [0]

            def turn(t, copied):
                for g in range(KT // 4):
                    n = turns[0]
                    turns[0] += 1
                    if n >= 4:
                        pe.wait_ge(turn_copied, n - 3 + copied)
                    for j in range(4):
                        k = 4 * g + j
                        last = nc.tensor.transpose(ps[3 + n % 4][:, j * P:(j + 1) * P],
                                                   hres[:, t, k * P:(k + 1) * P], ident)
                    last.then_inc(turned, 1)

            for t in range(TT):
                pe.wait_ge(h_ready, t + 1)
                turn(t, 0)
            pe.wait_ge(h_ready, 3)
            pe.wait_ge(turn_copied, 5)
            for k in range(KT):
                last = nc.tensor.transpose(ps[3][:, k * META:(k + 1) * META], metab[:, k * P:(k + 1) * P],
                                           ident[0:META, 0:META])
            last.then_inc(turned, 1)

            pe.wait_ge(turn_copied, 9)

            def project(bank, slot, first):
                for k in range(KT):
                    last = mm(ps[bank][:, 0:L - first], wslot[slot][:, k, :], hT[:, k, first:L], k, KT)
                last.then_inc(proj_done, 1)

            for n in range(FIRST):
                if n < KR_TILE:
                    pe.wait_ge(w_loaded[n % 3], 16 * (n // 3 + 1))
                else:
                    pe.wait_ge(kr_loaded, 48)
                if n >= 3:
                    pe.wait_ge(bank_freed[n % 3], n // 3)
                project(n % 3, n % 3, META if n < QT else 0)

            pe.wait_ge(squared, QT)
            for k in range(QT):
                last = mm(ps[3][:, 0:SEQ], ones, sq[:, k, 0:SEQ], k, QT)
            last.then_inc(sums_ready, 1)
            pe.wait_ge(squared, QT + KVT)
            for k in range(KVT):
                last = mm(ps[4][:, 0:L], ones, sq[:, QT + k, :], k, KVT)
            last.then_inc(sums_ready, 1)
            pe.wait_ge(kr2_ready, 1)
            nc.tensor.matmul(ps[5][:, 0:L], cst[:, C_FOLD:C_FOLD + P], kr2[:, :], start=True, stop=True
                             ).then_inc(folded, 1)

            with pe.Fori(0, CT) as i:
                for k, slot in enumerate((SC, SH, SB)):
                    pe.wait_ge(w_loaded[slot], i * 16 + 16 * (fills[slot] + 1))
                    pe.wait_ge(bank_freed[slot], i + uses[slot])
                    project(slot, slot, META if k == 2 else 0)

            pe.wait_ge(squared, QT + KVT + 1)
            for k in range(CT):
                last = mm(ps[7][:, 0:SEQ], ones, sq[:, k, 0:SEQ], k, CT)
            last.then_inc(sums_ready, 1)

            wk = P + META

            def qkv(h, b, i):
                pe.wait_ge(att_w_loaded[b], i * 64 + 64)
                if not isinstance(h, int) or h > 0:
                    pe.wait_ge(act_evac, h * 2)
                    pe.wait_ge(dve_evac, h * 3)
                uq = ring[:, 5 + b, 0:QT * 2 * P].rearrange("p (k n) -> p k n", k=QT)
                ukv = ring[:, 5 + b, QT * 2 * P:(QT + KVT) * 2 * P].rearrange("p (k n) -> p k n", k=KVT)
                for half in range(2):
                    for k in range(QT):
                        last = mm(ps[7 * half][:, 0:SEQ], uq[:, k, half * P:(half + 1) * P],
                                  cq[:, k, :], k, QT)
                last.then_inc(qkv_done, 1)
                for k in range(KVT):
                    last = mm(ps[1][:, 0:L], ukv[:, k, 0:P], ckv[:, k, :], k, KVT)
                last.then_inc(qkv_done, 1)
                for blk, (c0, w) in enumerate(((META, P), (META + P, P), (0, META))):
                    for k in range(KVT):
                        last = mm(ps[2][0:w, blk * P:(blk + 1) * P], ckv[:, k, c0:c0 + w],
                                  ukv[:, k, P:2 * P], k, KVT)
                last.then_inc(qkv_done, 1)

            def score(h, b):
                pe.wait_ge(act_evac, h * 2 + 2)
                pe.wait_ge(dve_evac, h * 3 + 1)
                if not isinstance(h, int) or h > 0:
                    pe.wait_ge(exped, h * 2)
                for t in range(TT):
                    o = ps[3][:, 0:wk] if t == 0 else ps[3][:, wk:wk + L]
                    w = wk if t == 0 else L
                    mm(o, qn[:, b, t * P:(t + 1) * P], kn[:, b, 0:w], 0, 3)
                    mm(o, qrot[:, b, t * P:(t + 1) * P], krot[:, 0:w], 1, 3)
                    mm(o, cst[0:1, C_MASKQ:C_MASKQ + P], cst[0:1, C_MASKK + L - w:C_MASKK + L], 2, 3
                       ).then_inc(scored, 1)

            def attend(h, b):
                pe.wait_ge(p_ready, h * 2 + 2)
                pe.wait_ge(pT_copied, h)
                pe.wait_ge(pTm_copied, h)
                for n, c0 in enumerate((META, wk + META, wk + META + P)):
                    last = nc.tensor.transpose(ps[4][:, n * P:(n + 1) * P], pr[:, b, c0:c0 + P], ident)
                last.then_inc(p_turned, 1)
                for n, c0 in enumerate((0, wk)):
                    last = nc.tensor.transpose(ps[5][0:META, n * P:(n + 1) * P], pr[:, b, c0:c0 + META], ident)
                last.then_inc(p_turned, 1)
                pe.wait_ge(pT_copied, h + 1)
                pe.wait_ge(pTm_copied, h + 1)
                pe.wait_ge(dve_evac, h * 3 + 3)
                pe.wait_ge(o_copied, h)
                mm(ps[6][:, 0:P], vt[:, b, 0, :], pT[:, b, 0, :], 0, 2)
                mm(ps[6][:, 0:P], vt[0:META, b, 2, :], pTm[:, b, 0, :], 1, 2)
                mm(ps[6][:, P:SEQ], vt[:, b, 0, :], pT[:, b, 1, :], 0, 3)
                mm(ps[6][:, P:SEQ], vt[:, b, 1, :], pT[:, b, 2, :], 1, 3)
                mm(ps[6][:, P:SEQ], vt[0:META, b, 2, :], pTm[:, b, 1, :], 2, 3).then_inc(pv_done, 1)

            pe.wait_ge(normed, 2)
            pe.wait_ge(krot_ready, 1)
            pe.wait_ge(ms_ready, 3)
            pe.wait_ge(bank_freed[SB], uses[SB] + CT)
            pe.wait_ge(bank_freed[SH], uses[SH] + CT)
            pe.wait_ge(bank_freed[SC], uses[SC] + CT)

            def pair(i, last):
                h = i * 2
                score(h, 0)
                qkv(h + 1, 1, i)
                attend(h, 0)
                score(h + 1, 1)
                if not last:
                    qkv(h + 2, 0, i + 1)
                attend(h + 1, 1)

            qkv(0, 0, 0)
            with pe.Fori(0, HEADS // 2 - 1) as i:
                pair(i, False)
            pair(HEADS // 2 - 1, True)
            pe.wait_ge(squared, QT + KVT + 2)
            for k in range(AT):
                last = mm(ps[7][:, 0:SEQ], ones, sq[:, k, 0:SEQ], k, AT)
            last.then_inc(sums_ready, 1)

            pe.wait_ge(normed, 4)
            with pe.Fori(0, KT // 2) as i:
                for b in range(2):
                    pe.wait_ge(wo_loaded[b], i * 16 + 16)
                    pe.wait_ge(mo_copied, i * 2 + b)
                    for k in range(KT):
                        last = mm(ps[b][:, 0:SEQ], wslot[3 + b][:, k, :], mixT[:, k, :], k, KT)
                    last.then_inc(wo_done, 1)
                for b in range(2):
                    pe.wait_ge(mo_copied, i * 2 + (b + 1))
                    pe.wait_ge(res_added, i * 2 + b)
                    for t in range(TT):
                        last = nc.tensor.transpose(ps[4 + b][:, t * P:(t + 1) * P], moT[:, b, t * P:(t + 1) * P], ident)
                    last.then_inc(mo_turned, 1)

            pe.wait_ge(turn_copied, 9)
            pe.wait_ge(res_added, KT)
            turns[0] = 0
            for t in range(TT):
                pe.wait_ge(h_ready, 4 + t)
                turn(t, 9)
            pe.wait_ge(turn_copied, 17)
            pe.wait_ge(mo_copied, KT)
            pe.wait_ge(gains_copied, 2)
            with pe.Fori(0, HEADS) as i:
                for b in range(2):
                    pe.wait_ge(wq_loaded[b], i * 16 + 16)
                    pe.wait_ge(pq_copied, i * 2 + b)
                    for k in range(KT):
                        last = mm(ps[b][:, 0:SEQ], wslot[b][:, k, :], hT[:, k, 0:SEQ], k, KT)
                    last.then_inc(wq_done, 1)
                for b in range(2):
                    pe.wait_ge(pq_copied, i * 2 + (b + 1))
                    pe.wait_ge(scores_kept, i * 2 + b)
                    for t in range(TT):
                        last = nc.tensor.matmul(ps[4 + b][:, t * P:(t + 1) * P], moT[:, b, t * P:(t + 1) * P],
                                                skT[:, b, :], start=True, stop=True)
                    last.then_inc(keys_done, 1)
            pe.sem_inc(slots_free, RING)

        @block.scalar
        def _(act):
            def std(n, w):
                act.wait_ge(var_ready, n)
                nc.scalar.activation(rstd[:, 0:w, 0], mv[:, 0:w, 1], ACT.Sqrt).then_inc(std_ready, 1)

            def keep_turned(n, base):
                t, g = n // 4, n % 4
                act.wait_ge(turned, base + n + 1)
                nc.scalar.copy(hT[:, 4 * g:4 * g + 4, (META if base == 0 else 0) + t * P:][:, :, 0:P],
                               ps[3 + n % 4][:, :].rearrange("p (k n) -> p k n", k=4)).then_inc(turn_copied, 1)

            act.wait_ge(gains_turned, 3)
            nc.scalar.copy(gains[:, :], ps[7][:, 256:256 + G_N]).then_inc(gains_copied, 1)
            nc.scalar.copy(skT[:, :, :], ps[7][:, 0:2 * P].rearrange("p (c n) -> p c n", c=2)).then_inc(gains_copied, 1)
            std(1, 3)
            for n in range(8):
                keep_turned(n, 0)
            act.wait_ge(turned, 9)
            nc.scalar.copy(hT[:, :, 0:META], ps[3][:, 0:KT * META].rearrange("p (k n) -> p k n", k=KT)
                           ).then_inc(turn_copied, 1)

            for n in range(KR_TILE):
                act.wait_ge(proj_done, n + 1)
                w = SEQ if n < QT else L
                dst = cq[:, n, :] if n < QT else ckv[:, n - QT, :]
                nc.scalar.copy(dst, ps[n % 3][:, 0:w]).then_inc(low_copied, 1)
                nc.scalar.activation(sq[:, n, 0:w], ps[n % 3][:, 0:w], ACT.Square).then_inc(squared, 1)
                act.wait_ge(squared, n + 1)
                act.sem_inc(bank_freed[n % 3], 1)

            def rms(n, w):
                act.wait_ge(ms_ready, n + 1)
                nc.scalar.activation(rs[:, n, 0:w], rs[:, n, 0:w], ACT.Sqrt).then_inc(rms_ready, 1)

            rms(0, SEQ)
            rms(1, L)
            act.wait_ge(folded, 1)
            nc.scalar.copy(krot[:, :], ps[5][:, 0:L]).then_inc(krot_ready, 1)

            with act.Fori(0, CT) as i:
                act.wait_ge(proj_done, i * 3 + (FIRST + 1))
                act.wait_ge(bank_freed[SH], i + uses[SH])
                nc.scalar.copy(cgate[:, :], ps[SC][:, 0:L]).then_inc(bank_freed[SC], 1)
            act.wait_ge(bank_freed[SB], uses[SB] + CT)
            act.wait_ge(sums_ready, 2)
            nc.scalar.activation(sq[:, :, 0:SEQ], mixT[:, AT:AT + CT, :], ACT.Square).then_inc(squared, 1)
            rms(2, SEQ)

            def head(h, b):
                act.wait_ge(qkv_done, h * 3 + 1)
                nc.scalar.copy(qn[:, b, :], ps[0][:, 0:SEQ]).then_inc(act_evac, 1)
                act.wait_ge(qkv_done, h * 3 + 2)
                nc.scalar.copy(kn[:, b, :], ps[1][:, 0:L]).then_inc(act_evac, 1)

            def softmax_exp(h, b):
                for t in range(TT):
                    lo, w = (0, wk) if t == 0 else (wk, L)
                    act.wait_ge(shifted, h * 2 + 2)
                    nc.scalar.activation(pr[:, b, lo:lo + w], ps[3][:, lo:lo + w], ACT.Exp,
                                         bias=smx[:, b, 2 + t:3 + t], scale=SCALE,
                                         accum_out=smx[:, b, 4 + t:5 + t]).then_inc(exped, 1)

            def output(h, b):
                act.wait_ge(p_turned, h * 2 + 1)
                nc.scalar.copy(pT[:, b, :, :], ps[4][:, 0:3 * P].rearrange("p (k n) -> p k n", k=3)
                               ).then_inc(pT_copied, 1)
                act.wait_ge(pv_done, h + 1)
                nc.scalar.copy(mixT[:, bass.ds(h, 1), :], ps[6][:, 0:SEQ].unsqueeze(1)).then_inc(o_copied, 1)

            def pair(i, last):
                h = i * 2
                softmax_exp(h, 0)
                head(h + 1, 1)
                output(h, 0)
                softmax_exp(h + 1, 1)
                if not last:
                    head(h + 2, 0)
                output(h + 1, 1)

            wk = P + META
            head(0, 0)
            with act.Fori(0, HEADS // 2 - 1) as i:
                pair(i, False)
            pair(HEADS // 2 - 1, True)
            act.wait_ge(sums_ready, 3)
            act.wait_ge(o_copied, HEADS)
            nc.scalar.activation(sq[:, :, 0:SEQ], mixT[:, 0:AT, :], ACT.Square).then_inc(squared, 1)
            rms(3, SEQ)

            with act.Fori(0, KT // 2) as i:
                for b in range(2):
                    act.wait_ge(wo_done, i * 2 + (b + 1))
                    act.wait_ge(mo_turned, i * 2 + b) if b else act.wait_ge(mo_turned, i * 2)
                    nc.scalar.copy(moT[:, b, :], ps[b][:, 0:SEQ]).then_inc(mo_copied, 1)
            std(2, 2)
            for n in range(8):
                keep_turned(n, 9)
            act.wait_ge(mo_turned, KT)
            with act.Fori(0, HEADS) as i:
                for b in range(2):
                    act.wait_ge(wq_done, i * 2 + (b + 1))
                    act.wait_ge(keys_done, i * 2 + b) if b else act.wait_ge(keys_done, i * 2)
                    nc.scalar.copy(moT[:, b, :], ps[b][:, 0:SEQ]).then_inc(pq_copied, 1)

            def gate_exp(q):
                act.wait_ge(shifted, 2 * HEADS + 1 + q)
                nc.scalar.activation(gex[:, :], bv[:, :], ACT.Exp, bias=gsm[:, 0:1],
                                     accum_out=gsm[:, 1:2]).then_inc(gexp_ready, 1)

            gate_exp(0)
            for t in range(TT):
                with act.Fori(0, HEADS // 2) as i:
                    for b in range(2):
                        q = i * 2 + (t * HEADS + b)
                        gate_exp(q + 1)
                        act.wait_ge(slots_free, q * ROWS + (RING + TOPK))
                        nc.scalar.activation(gel[:, b, :], dots[:, b, :], ACT.Gelu).then_inc(gelu_ready, 1)
                std(3 + t, 1)

        @block.vector
        def _(dve):
            steps = [0]

            def link(ins):
                steps[0] += 1
                ins.then_inc(dve_step, 1)
                dve.wait_ge(dve_step, steps[0])

            def layer_stats(blocks, signal):
                for s, (xb, p) in enumerate(blocks):
                    for j in range(4):
                        link(nc.vector.bn_stats(stats[0:p, s, j, :], xb[:, j * 512:(j + 1) * 512]))
                    link(nc.vector.bn_aggr(mv[0:p, s, :], stats[0:p, s, :, :].rearrange("p j s -> p (j s)")))
                w = len(blocks)
                nc.vector.tensor_scalar(mv[:, 0:w, 1], mv[:, 0:w, 1], EPS, None, ALU.add).then_inc(var_ready, 1)
                dve.wait_ge(std_ready, signal)
                link(nc.vector.reciprocal(rstd[:, 0:w, 1], rstd[:, 0:w, 0]))

            def layer_apply(s, xb, p, done):
                link(nc.vector.tensor_scalar(xb, xb, mv[0:p, s, 0:1], rstd[0:p, s, 1:2], ALU.subtract, ALU.mult))
                link(nc.vector.tensor_tensor(xb, xb, gb[0:p, 0, :], ALU.mult))
                nc.vector.tensor_tensor(xb, xb, gb[0:p, 1, :], ALU.add).then_inc(done, 1)

            link(nc.vector.memset(mv[:, :, :], 1.0))
            blocks = [(hres[:, 0, :], P), (hres[:, 1, :], P), (metab, META)]
            for s in range(3):
                dve.wait_ge(x_loaded[s], 16)
            layer_stats(blocks, 1)
            dve.wait_ge(gb_loaded, 32)
            for s, (xb, p) in enumerate(blocks):
                layer_apply(s, xb, p, h_ready)

            dve.wait_ge(consts_loaded, 16)
            dve.wait_ge(proj_done, FIRST)
            nc.vector.tensor_tensor(kr2[:, :], ps[KR_TILE % 3][:, 0:L], rope, ALU.mult).then_inc(kr2_ready, 1)
            dve.wait_ge(kr2_ready, 1)
            dve.sem_inc(bank_freed[KR_TILE % 3], 1)

            def rms_scale(n, bank, w, dim, tiles, gain):
                dve.wait_ge(sums_ready, n + 1)
                nc.vector.tensor_scalar(rs[:, n, 0:w], ps[bank][:, 0:w], 1.0 / dim, EPS, ALU.mult, ALU.add
                                        ).then_inc(ms_ready, 1)
                dve.wait_ge(rms_ready, n + 1)
                link(nc.vector.reciprocal(rs[:, n, 0:w], rs[:, n, 0:w]))
                for k, tile in enumerate(tiles):
                    last = nc.vector.scalar_tensor_tensor(out=tile, in0=tile, scalar=gains[:, gain + k:gain + k + 1],
                                                          in1=rs[:, n, 0:w], op0=ALU.mult, op1=ALU.mult)
                last.then_inc(normed, 1)

            dve.wait_ge(low_copied, QT + KVT)
            dve.wait_ge(gains_copied, 2)
            rms_scale(0, 3, SEQ, Q_RANK, [cq[:, k, :] for k in range(QT)], G_Q)
            rms_scale(1, 4, L, KV_RANK, [ckv[:, k, :] for k in range(KVT)], G_KV)

            with dve.Fori(0, CT) as i:
                dve.wait_ge(proj_done, i * 3 + (FIRST + 2))
                dve.wait_ge(bank_freed[SC], i + (uses[SC] + 1))
                nc.vector.tensor_tensor(ubuf[:, :], ps[SH][:, 0:L], cgate[:, :], ALU.mult).then_inc(bank_freed[SH], 1)
                dve.wait_ge(bank_freed[SH], i + (uses[SH] + 1))
                lo = META - CONV_W + 1
                nc.vector.tensor_scalar(ybuf[:, :], ubuf[:, lo:lo + SEQ], gains[:, bass.ds(i + G_CW, 1)], None,
                                        ALU.mult).then_inc(conv_step, 1)
                for j in range(1, CONV_W):
                    dve.wait_ge(conv_step, i * CONV_W + j)
                    nc.vector.scalar_tensor_tensor(out=ybuf[:, :], in0=ubuf[:, lo + j:lo + j + SEQ],
                                                   scalar=gains[:, bass.ds(i + (G_CW + j * CT), 1)], in1=ybuf[:, :],
                                                   op0=ALU.mult, op1=ALU.add).then_inc(conv_step, 1)
                dve.wait_ge(conv_step, i * CONV_W + CONV_W)
                dve.wait_ge(proj_done, i * 3 + (FIRST + 3))
                nc.vector.tensor_tensor(mixT[:, bass.ds(i + AT, 1), :], ps[SB][:, 0:SEQ].unsqueeze(1),
                                        ybuf[:, :].unsqueeze(1), ALU.mult).then_inc(bank_freed[SB], 1)
            dve.wait_ge(bank_freed[SB], uses[SB] + CT)
            dve.wait_ge(squared, QT + KVT + 1)
            rms_scale(2, 7, SEQ, CONV_DIM, [mixT[:, AT + k, :] for k in range(CT)], G_CONV)

            wk = P + META

            def head(h, b):
                dve.wait_ge(qkv_done, h * 3 + 1)
                nc.vector.tensor_tensor(qrot[:, b, :], ps[7][:, 0:SEQ], rope[:, META:L], ALU.mult
                                        ).then_inc(dve_evac, 1)
                dve.wait_ge(qkv_done, h * 3 + 3)
                nc.vector.tensor_copy(vt[:, b, 0:2, :], ps[2][:, 0:2 * P].rearrange("p (k n) -> p k n", k=2)
                                      ).then_inc(dve_evac, 1)
                nc.vector.tensor_copy(vt[0:META, b, 2, :], ps[2][0:META, 2 * P:3 * P]).then_inc(dve_evac, 1)

            def softmax(h, b):
                dve.wait_ge(scored, h * 2 + 2)
                for t in range(TT):
                    lo, w = (0, wk) if t == 0 else (wk, L)
                    nc.vector.tensor_reduce(smx[:, b, t:t + 1], ps[3][:, lo:lo + w], AX.X, ALU.max
                                            ).then_inc(att_step, 1)
                    dve.wait_ge(att_step, h * 4 + (t + 1))
                    nc.vector.tensor_scalar(smx[:, b, 2 + t:3 + t], smx[:, b, t:t + 1], -SCALE, None, ALU.mult
                                            ).then_inc(shifted, 1)
                for t in range(TT):
                    lo, w = (0, wk) if t == 0 else (wk, L)
                    dve.wait_ge(exped, h * 2 + (t + 1))
                    nc.vector.reciprocal(smx[:, b, 6 + t:7 + t], smx[:, b, 4 + t:5 + t]).then_inc(att_step, 1)
                    dve.wait_ge(att_step, h * 4 + (t + 3))
                    nc.vector.tensor_scalar(pr[:, b, lo:lo + w], pr[:, b, lo:lo + w], smx[:, b, 6 + t:7 + t], None,
                                            ALU.mult).then_inc(p_ready, 1)

            def turned_meta(h, b):
                dve.wait_ge(p_turned, h * 2 + 2)
                nc.vector.tensor_copy(pTm[:, b, :, :], ps[5][0:META, 0:2 * P].rearrange("p (k n) -> p k n", k=2)
                                      ).then_inc(pTm_copied, 1)

            def pair(i, last):
                h = i * 2
                softmax(h, 0)
                head(h + 1, 1)
                turned_meta(h, 0)
                softmax(h + 1, 1)
                if not last:
                    head(h + 2, 0)
                turned_meta(h + 1, 1)

            head(0, 0)
            with dve.Fori(0, HEADS // 2 - 1) as i:
                pair(i, False)
            pair(HEADS // 2 - 1, True)
            dve.wait_ge(o_copied, HEADS)
            dve.wait_ge(squared, QT + KVT + 2)
            rms_scale(3, 7, SEQ, AT * P, [mixT[:, k, :] for k in range(AT)], G_ATT)

            with dve.Fori(0, KT // 2) as i:
                for b in range(2):
                    dve.wait_ge(mo_turned, i * 2 + (b + 1))
                    cols = bass.ds(i * 2 * P + b * P, P)
                    nc.vector.scalar_tensor_tensor(
                        out=hres[:, :, cols], in0=hres[:, :, cols], scalar=ALPHA,
                        in1=ps[4 + b][:, 0:SEQ].rearrange("p (t n) -> p t n", t=TT),
                        op0=ALU.mult, op1=ALU.add).then_inc(res_added, 1)
            dve.wait_ge(res_added, KT)
            layer_stats([(hres[:, t, :], P) for t in range(TT)], 2)
            dve.wait_ge(gb_loaded, 64)
            for t in range(TT):
                layer_apply(t, hres[:, t, :], P, h_ready)
            dve.wait_ge(h_ready, 5)
            dve.wait_ge(mo_copied, KT)
            dve.wait_ge(wo_done, KT)
            for t in range(TT):
                nc.vector.tensor_scalar(acc[:, t, :], hres[:, t, :], ALPHA, None, ALU.mult).then_inc(acc_started, 1)

            by_tile = scores[:, 0:TT * HEADS, :, :].rearrange("p (t h) c k -> p t (h c k)", t=TT)
            with dve.Fori(0, HEADS) as i:
                for b in range(2):
                    dve.wait_ge(keys_done, i * 2 + (b + 1))
                    nc.vector.tensor_copy(by_tile[:, :, bass.ds(i * 2 * N_KEYS + b * N_KEYS, N_KEYS)],
                                          ps[4 + b][:, 0:SEQ].rearrange("p (t n) -> p t n", t=TT)
                                          ).then_inc(scores_kept, 1)
            dve.wait_ge(scores_kept, 2 * HEADS)
            dve.wait_ge(pad_cleared, 1)

            PICK = 30

            def pick(q, b):
                n = [0]

                def step(ins):
                    n[0] += 1
                    ins.then_inc(pick_step, 1)
                    dve.wait_ge(pick_step, q * PICK + n[0])
                    dve.sem_inc(pick_passed, 1)

                def top16(vals, inds, src, spare):
                    step(nc.vector.max(vals[:, 0:8], src))
                    step(nc.vector.max_index(inds[:, 0:8], vals[:, 0:8], src))
                    step(nc.vector.match_replace(spare, vals[:, 0:8], src, -3.0e38))
                    step(nc.vector.max(vals[:, 8:16], spare))
                    step(nc.vector.max_index(inds[:, 8:16], vals[:, 8:16], spare))

                step(nc.vector.tensor_copy(sc[:, :, :].unsqueeze(1), scores[:, bass.ds(q, 1), :, :]))
                for c in range(2):
                    top16(tv[:, c, :], ti[:, c, :], sc[:, c, :], sc2[:, c, :])
                grid = cand[:, :].rearrange("p (a b) -> p a b", a=TOPK)
                step(nc.vector.tensor_tensor(grid, tv[:, 0, :].unsqueeze(2).to_broadcast([P, TOPK, TOPK]),
                                             tv[:, 1, :].unsqueeze(1).to_broadcast([P, TOPK, TOPK]), ALU.add))
                step(nc.vector.tensor_copy(tif[:, :, :], ti[:, :, :]))
                top16(bv, bi, cand[:, :], cand2[:, :])
                nc.vector.tensor_scalar(gsm[:, 0:1], bv[:, 0:1], -1.0, None, ALU.mult).then_inc(shifted, 1)
                step(nc.vector.tensor_scalar(bhl[:, 0, :], bi[:, :], 4, None, ALU.logical_shift_right))
                step(nc.vector.tensor_scalar(bhl[:, 1, :], bi[:, :], TOPK - 1, None, ALU.bitwise_and))
                step(nc.vector.tensor_copy(bhlf[:, :, :], bhl[:, :, :]))
                full = [P, 2, TOPK, TOPK]
                iota = cst[:, C_IOTA:C_IOTA + TOPK].unsqueeze(1).to_broadcast([P, 2 * TOPK, TOPK])
                hot3 = hot[:, :, :, :].rearrange("p c k j -> p (c k) j")
                step(nc.vector.tensor_tensor(
                    hot3, iota, bhlf[:, :, :].rearrange("p c k -> p (c k)").unsqueeze(2).to_broadcast(
                        [P, 2 * TOPK, TOPK]), ALU.is_equal))
                step(nc.vector.tensor_tensor(hot[:, :, :, :], hot[:, :, :, :],
                                             tif[:, :, :].unsqueeze(2).to_broadcast(full), ALU.mult))
                step(nc.vector.tensor_reduce(isel[:, :, :].rearrange("p c k -> p (c k)"), hot3, AX.X, ALU.add))
                nc.vector.scalar_tensor_tensor(out=idx[:, b, :], in0=isel[:, 0, :], scalar=float(N_KEYS),
                                               in1=isel[:, 1, :], op0=ALU.mult, op1=ALU.add).then_inc(idx_ready, 1)
                dve.wait_ge(gexp_ready, q + 1)
                step(nc.vector.reciprocal(gsm[:, 2:3], gsm[:, 1:2]))
                step(nc.vector.tensor_scalar(gate[:, b, :], gex[:, :], gsm[:, 2:3], None, ALU.mult))
                while n[0] < PICK:
                    n[0] += 1
                    dve.sem_inc(pick_step, 1)
                assert n[0] == PICK

            pick(0, 0)
            dve.wait_ge(acc_started, TT)
            for t in range(TT):
                with dve.Fori(0, HEADS // 2) as i:
                    for b in range(2):
                        q = i * 2 + (t * HEADS + b)
                        for m in range(TOPK):
                            dve.wait_ge(row_landed[m % RING], q * (16 * ROWS // RING) + 16 * (m // RING + 1))
                            nc.vector.tensor_tensor_reduce(
                                ring[:, m % RING, :], ring[:, m % RING, :], hres[:, t, :], 1.0, 0.0,
                                ALU.mult, ALU.add, dots[:, b, m:m + 1]).then_inc(slots_free, 1)
                        pick(q + 1, 1 - b)
                        dve.wait_ge(gelu_ready, q + 1)
                        nc.vector.tensor_tensor(wgt[:, b, :], gel[:, b, :], gate[:, b, :], ALU.mult
                                                ).then_inc(weight_ready, 1)
                        dve.wait_ge(weight_ready, q + 1)
                        for m in range(TOPK, ROWS):
                            k = m - TOPK
                            dve.wait_ge(row_landed[m % RING], q * (16 * ROWS // RING) + 16 * (m // RING + 1))
                            nc.vector.scalar_tensor_tensor(
                                out=acc[:, t, :], in0=ring[:, m % RING, :], scalar=wgt[:, b, k:k + 1],
                                in1=acc[:, t, :], op0=ALU.mult, op1=ALU.add).then_inc(slots_free, 1)
                            dve.wait_ge(slots_free, q * ROWS + (RING + m + 1))
                layer_stats([(acc[:, t, :], P)], 3 + t)
                dve.wait_ge(gb_loaded, 96)
                layer_apply(0, acc[:, t, :], P, out_ready)


_INS = ["x", "meta_tokens", "ln0_g", "ln0_b", "w_in", "q_norm_g", "kv_norm_g", "w_uq", "w_ukv", "conv_w",
        "attn_out_g", "conv_out_g", "w_o", "ln1_g", "ln1_b", "peer_w_query", "peer_sub_keys", "peer_u", "peer_v",
        "ln2_g", "ln2_b"]


def kernel(**inputs):
    import concourse.bacc as bacc
    from concourse.bass_utils import run_bass_kernel_spmd

    nc = bacc.Bacc("TRN2", target_bir_lowering=False, num_devices=1)
    arrays, args = {}, []
    for name in _INS + ["const_block"]:
        a = np.ascontiguousarray(inputs[name]) if name in inputs else constants()
        arrays[f"in_{name}"] = a
        args.append(nc.dram_tensor(f"in_{name}", a.shape, mybir.dt.from_np(a.dtype), kind="ExternalInput").ap())
    args.append(nc.dram_tensor("out", (1, SEQ, D), F32, kind="ExternalOutput").ap())
    build(nc, *args)
    return run_bass_kernel_spmd(nc, [arrays], core_ids=[0]).results[0]["out"]
```

```python
from contextlib import ExitStack

import numpy as np

import concourse.bass as bass
from concourse import mybir

ALU = mybir.AluOpType
ACT = mybir.ActivationFunctionType
AX = mybir.AxisListType
F32 = mybir.dt.float32
F32R = mybir.dt.float32r
U32 = mybir.dt.uint32

P = 128
D = 2048
KT = D // P
SEQ = 256
TT = SEQ // P
META = 16
L = META + SEQ
HEADS = 8
D_NOPE, D_ROPE, D_V = 128, 64, 128
D_QK = D_NOPE + D_ROPE
Q_RANK, KV_RANK = 384, 512
QT, KVT = Q_RANK // P, KV_RANK // P
CONV_DIM = 1024
CT = CONV_DIM // P
AT = HEADS * D_V // P
CONV_W = 3
CHUNK = 64
OFF_KR = Q_RANK + KV_RANK
OFF_B = OFF_KR + D_ROPE
OFF_C = OFF_B + CONV_DIM
OFF_H = OFF_C + CONV_DIM
N_KEYS = 128
TOPK = 16
EXP_TILES = N_KEYS
PICKS = TT * HEADS
CH = 4
CK = 4 * P
ALPHA = 2.0 ** 0.25
EPS = 1e-5
SCALE = float(D_QK) ** -0.5
NEG = -1e30
THETA = 10000.0

C_ID, C_IOTA, C_KEEP = 0, P, 2 * P
C_ONES, C_FOLD, C_ROPE = C_KEEP, C_KEEP + P, C_KEEP + 2 * P
C_MASKQ = C_ROPE + L
C_MASKK = C_MASKQ + P
C_W = C_MASKK + L

G_Q, G_KV, G_ATT, G_CONV, G_CW = 0, QT, QT + KVT, QT + KVT + AT, QT + KVT + AT + CT
G_N = G_CW + CONV_W * CT


def constants():
    c = np.zeros((P, C_W), np.float32)
    r = np.arange(P)
    c[:, C_ID:C_ID + P] = np.eye(P)
    c[:, C_FOLD:C_FOLD + P] = (r[:, None] % D_ROPE) == (r[None, :] % D_ROPE)
    c[:, C_ONES:C_ONES + P] = 1.0
    inv = (1.0 / (np.float32(THETA) ** (np.arange(0, D_ROPE, 2, dtype=np.float32) / D_ROPE))).astype(np.float32)
    ang = np.arange(L, dtype=np.float32)[None, :] * inv[:, None]
    cos, sin = np.cos(ang), np.sin(ang)
    c[:, C_ROPE:C_ROPE + L] = np.concatenate([cos, cos, -sin, sin])
    c[0, C_MASKQ:C_MASKQ + CHUNK] = 1.0
    c[0, C_MASKK + L - CHUNK:C_MASKK + L] = NEG
    c[:, C_IOTA:C_IOTA + P] = np.arange(P)
    return c


class Carve:

    def __init__(self, tensor, at, end):
        self.tensor, self.at, self.end = tensor, at, end

    def take(self, n, parts=P):
        lo, self.at = self.at, self.at + n
        assert self.at <= self.end, (self.at, self.end)
        return self.tensor[0:parts, lo:lo + n]


def after(eng, sem, value):
    if not isinstance(value, int) or value > 0:
        eng.wait_ge(sem, value)


def build(nc, x, meta_tokens, ln0_g, ln0_b, w_in, q_norm_g, kv_norm_g, w_uq, w_ukv, conv_w, attn_out_g,
          conv_out_g, w_o, ln1_g, ln1_b, peer_w_query, peer_sub_keys, peer_u, peer_v, ln2_g, ln2_b,
          const_block, out):
    ctx = ExitStack()

    def sb(name, shape, dt=F32):
        return ctx.enter_context(nc.sbuf_tensor(name, shape, dt))

    def sem(name):
        return ctx.enter_context(nc.semaphore(name))

    with ctx:
        NT = 2
        STEPS = SEQ // NT
        PAIRS = EXP_TILES // 2
        PICKED_AT = 2 * PICKS
        TURNED_AT = PICKED_AT + 8
        GATES_AT = PAIRS - STEPS // (2 * CH)
        HALF = NT * P

        store = sb("store", [P, EXP_TILES * SEQ])
        by_expert = store[:, :].rearrange("p (e t) -> p e t", e=EXP_TILES)
        A_COLS = 2 * KT * L
        split = sb("split", [P, A_COLS + CH * 2 * CK], F32R)
        nat = sb("nat", [P, 2, D])
        keep = sb("keep", [P, C_KEEP])
        early = sb("early", [P, C_W - C_KEEP])[:, :]
        gains = sb("gains", [P, G_N])
        smx = sb("smx", [P, 2, 8])
        stats = sb("stats", [P, 4, 6])
        mv = sb("mv", [P, 2])
        rstd = sb("rstd", [P, 2])
        tv = sb("tv", [P, 2, TOPK])
        ti = sb("ti", [P, 2, TOPK], U32)
        tif = sb("tif", [P, 2, TOPK])
        bi = sb("bi", [P, TOPK], U32)
        bhl = sb("bhl", [P, 2, TOPK], U32)
        bhlf = sb("bhlf", [P, 2, TOPK])
        bscore = sb("bscore", [P, TOPK])
        chosen = sb("chosen", [P, 2, PICKS * TOPK])
        gate = sb("gate", [P, PICKS * TOPK])
        gsum = sb("gsum", [P, 2, PICKS])
        turnedc = sb("turnedc", [P, 3, SEQ])
        h1_spill = nc.dram_tensor("h1_spill", (P, TT * D), F32, kind="Internal").ap()

        PICK_AT = 104 * SEQ
        mixT = store[:, 112 * SEQ:].rearrange("p (k n) -> p k n", k=AT + CT)
        scores = store[:, 112 * SEQ:].rearrange("p (q c k) -> p q c k", q=PICKS, c=2)
        hot_c = Carve(store, PICK_AT, 112 * SEQ)
        sc = hot_c.take(2 * N_KEYS).rearrange("p (c k) -> p c k", c=2)
        sc2 = hot_c.take(2 * N_KEYS).rearrange("p (c k) -> p c k", c=2)
        cand, cand2 = hot_c.take(TOPK * TOPK), hot_c.take(TOPK * TOPK)
        hot = hot_c.take(2 * TOPK * TOPK).rearrange("p (c k j) -> p c k j", c=2, k=TOPK)
        carve = Carve(store, 0, PICK_AT)

        def view(n, k):
            return carve.take(n * k).rearrange("p (k n) -> p k n", k=k)

        wnat = [carve.take(D) for _ in range(4)]
        att_w = [carve.take((QT + KVT) * 2 * P) for _ in range(2)]
        metab = carve.take(D, META)
        cq, ckv = view(SEQ, QT), view(L, KVT)
        kr2, krot, cgate, ubuf, ybuf = carve.take(L), carve.take(L), carve.take(L), carve.take(L), carve.take(SEQ)
        rs = view(L, 2)
        qn, qrot, kn = view(SEQ, 2), view(SEQ, 2), view(L, 2)
        vt = carve.take(6 * P).rearrange("p (b k n) -> p b k n", b=2, k=3)
        pr = view(P + META + L, 2)
        pT = view(3 * P, 1).rearrange("p a (k n) -> p (a k) n", k=3)
        pTm = carve.take(2 * P, META).rearrange("p (k n) -> p k n", k=2)
        moT = view(SEQ, 2)
        skT = view(P, 2)
        sk = view(P, 2)
        grows = carve.take(P, G_N)
        hres = view(D, TT)
        sq_flat = store[:, PICK_AT:PICK_AT + 8 * SEQ]
        sq = sq_flat.rearrange("p (k n) -> p k n", k=8)

        gb = nat
        ident, iota = keep[:, C_ID:C_ID + P], keep[:, C_IOTA:C_IOTA + P]
        ones = early[:, C_ONES - C_KEEP:C_ONES - C_KEEP + P]
        fold = early[:, C_FOLD - C_KEEP:C_FOLD - C_KEEP + P]
        rope = early[:, C_ROPE - C_KEEP:C_ROPE - C_KEEP + L]
        maskq = early[0:1, C_MASKQ - C_KEEP:C_MASKQ - C_KEEP + P]
        maskk = early[0:1, C_MASKK - C_KEEP:C_MASKK - C_KEEP + L]

        act_hl = [split[:, s * KT * L:(s + 1) * KT * L].rearrange("p (k n) -> p k n", k=KT) for s in range(2)]
        chunk_hl = [[split[:, A_COLS + (2 * c + s) * CK:A_COLS + (2 * c + s + 1) * CK] for s in range(2)]
                    for c in range(CH)]
        v_hl = [[split[:, (2 * b + s) * D:(2 * b + s + 1) * D] for s in range(2)] for b in range(2)]
        second_rows = [early[:, b * HALF:(b + 1) * HALF] for b in range(2)]
        first_rows = [chosen[:, b, :] for b in range(2)]
        w_hl = [[split[:, 4 * D + (2 * b + s) * SEQ:4 * D + (2 * b + s + 1) * SEQ] for s in range(2)] for b in range(2)]

        ps = [ctx.enter_context(nc.psum_tensor(f"ps{i}", [P, 512], F32)) for i in range(8)]

        consts_loaded = sem("consts_loaded")
        x_loaded = [sem(f"x_loaded{b}") for b in range(3)]
        gb_loaded = sem("gb_loaded")
        small_loaded = sem("small_loaded")
        w_loaded = [sem(f"w_loaded{s}") for s in range(3)]
        kr_loaded = sem("kr_loaded")
        att_w_loaded = [sem(f"att_w_loaded{b}") for b in range(2)]
        w2_loaded = [sem(f"w2_loaded{b}") for b in range(2)]
        hi_done = sem("hi_done")
        lo_done = sem("lo_done")
        chunk_used = sem("chunk_used")
        stat_step = sem("stat_step")
        var_ready = sem("var_ready")
        std_ready = sem("std_ready")
        h_ready = sem("h_ready")
        turned = sem("turned")
        turned_hi = sem("turned_hi")
        turned_lo = sem("turned_lo")
        gains_turned = sem("gains_turned")
        gains_copied = sem("gains_copied")
        bank_freed = [sem(f"bank_freed{b}") for b in range(3)]
        low_copied = sem("low_copied")
        squared = sem("squared")
        sums_ready = sem("sums_ready")
        ms_ready = sem("ms_ready")
        rms_ready = sem("rms_ready")
        normed = sem("normed")
        kr2_ready = sem("kr2_ready")
        folded = sem("folded")
        krot_ready = sem("krot_ready")
        conv_step = sem("conv_step")
        mixed_hi = sem("mixed_hi")
        mixed_lo = sem("mixed_lo")
        qkv_done = sem("qkv_done")
        act_evac = sem("act_evac")
        dve_evac = sem("dve_evac")
        scored = sem("scored")
        att_step = sem("att_step")
        shifted = sem("shifted")
        exped = sem("exped")
        p_ready = sem("p_ready")
        p_turned = sem("p_turned")
        pT_copied = sem("pT_copied")
        pTm_copied = sem("pTm_copied")
        pv_done = sem("pv_done")
        o_copied = sem("o_copied")
        res_added = sem("res_added")
        spilled = sem("spilled")
        pq_copied = sem("pq_copied")
        keys_done = sem("keys_done")
        scores_kept = sem("scores_kept")
        pick_step = sem("pick_step")
        pick_passed = sem("pick_passed")
        gate_started = sem("gate_started")
        gate_step = sem("gate_step")
        gate_exped = sem("gate_exped")
        choice_turned = sem("choice_turned")
        choice_copied = sem("choice_copied")
        u_loaded = [sem(f"u_loaded{b}") for b in range(4)]
        u_turned = sem("u_turned")
        gelu_done = sem("gelu_done")
        second_diff = sem("second_diff")
        second_sq = sem("second_sq")
        second_hot = sem("second_hot")
        first_hot = sem("first_hot")
        gates_done = sem("gates_done")
        store_set = sem("store_set")
        store_step = sem("store_step")
        v_loaded = [sem(f"v_loaded{b}") for b in range(2)]
        v_hi = sem("v_hi")
        v_lo = sem("v_lo")
        w_lo = sem("w_lo")
        v_used = sem("v_used")
        h1_back = sem("h1_back")
        joined = sem("joined")
        out_ready = sem("out_ready")
        stored = sem("stored")

        FIRST = QT + KVT + 1
        KR_TILE = FIRST - 1
        N_IN = FIRST + 3 * CT
        fills = [len([n for n in range(KR_TILE) if n % 3 == s]) for s in range(3)]
        uses = [len([n for n in range(FIRST) if n % 3 == s]) for s in range(3)]
        SC, SH, SB = FIRST % 3, (FIRST + 1) % 3, (FIRST + 2) % 3
        C_WO = CH * N_IN
        C_WQ = C_WO + CH * KT
        C_U = C_WQ + CH * KT
        GROUPS = D // 512
        wk = P + META

        def multiplied(i, b, k):
            return i * (2 * (CH + 1)) + ((CH + 1) * (b - 2 * GATES_AT) + k)

        def step_of(i, b, c):
            return i * (2 * CH) + (CH * (b - 2 * GATES_AT) + c)

        def token_of(i, b, c):
            return i * (2 * CH * NT) + NT * (CH * (b - 2 * GATES_AT) + c)

        block = ctx.enter_context(nc.Block())

        @block.sync
        def _(sp):
            win = w_in[0].rearrange("(k p) n -> p k n", p=P)

            def tile(slot):
                return wnat[slot].rearrange("p (k n) -> p k n", k=KT)

            sp.dma_start(hres[:, 0, :], x[0, 0:P, :]).then_inc(x_loaded[0], 16)
            sp.dma_start(hres[:, 1, :], x[0, P:SEQ, :]).then_inc(x_loaded[1], 16)
            sp.dma_start(keep[:, :], const_block[:, 0:C_KEEP]).then_inc(consts_loaded, 16)
            sp.dma_start(early, const_block[:, C_KEEP:C_W]).then_inc(consts_loaded, 16)
            for n in range(FIRST):
                if n >= 3:
                    sp.wait_ge(lo_done, CH * (n - 2))
                if n < KR_TILE:
                    sp.dma_start(tile(n % 3), win[:, :, n * P:(n + 1) * P]).then_inc(w_loaded[n % 3], 16)
                else:
                    half = D_ROPE // 2
                    for to, frm, w in ((0, 0, D_ROPE), (D_ROPE, half, half), (D_ROPE + half, 0, half)):
                        sp.dma_start(tile(n % 3)[:, :, to:to + w],
                                     win[:, :, OFF_KR + frm:OFF_KR + frm + w]).then_inc(kr_loaded, 16)
            with sp.Fori(0, CT) as i:
                for k, (slot, off) in enumerate(((SC, OFF_C), (SH, OFF_H), (SB, OFF_B))):
                    sp.wait_ge(lo_done, i * (3 * CH) + CH * (FIRST + k - 2))
                    sp.dma_start(tile(slot), win[:, :, bass.ds(i * P + off, P)]).then_inc(w_loaded[slot], 16)
            wo = w_o[0].rearrange("(j k p) n -> p j k n", p=P, k=CH)
            with sp.Fori(0, GROUPS) as g:
                for j in range(4):
                    sp.wait_ge(lo_done, g * (4 * CH) + (C_WO + CH * (j - 1)))
                    sp.dma_start(wnat[2 + j % 2].rearrange("p (k n) -> p k n", k=CH),
                                 wo[:, j, :, bass.ds(g * 512, 512)]).then_inc(w2_loaded[j % 2], 16)
            wq = peer_w_query[0].rearrange("(k p) n -> p k n", p=P)
            with sp.Fori(0, HEADS) as i:
                for b in range(2):
                    sp.wait_ge(lo_done, i * (2 * CH) + (C_WQ + CH * (b - 1)))
                    sp.dma_start(tile(2 + b), wq[:, :, bass.ds(i * (2 * P) + b * P, P)]).then_inc(w2_loaded[b], 16)

            u = peer_u[0].rearrange("(e p) d -> e p d", p=P)
            sp.wait_ge(h_ready, 5)

            def load_u(i, b, s, first):
                if not first:
                    sp.wait_ge(u_turned, i * (2 * CH) + (CH * b - 2 * CH + 2 * s + 2))
                e = i * 2 + b
                src = u[bass.ds(e, 1)][0] if not isinstance(e, int) else u[e]
                sp.dma_start(nat[:, b, s * (D // 2):(s + 1) * (D // 2)], src[:, s * (D // 2):(s + 1) * (D // 2)]
                             ).then_inc(u_loaded[2 * b + s], 16)

            for b in range(2):
                for s in range(2):
                    load_u(0, b, s, True)
            sp.dma_start(h1_spill[:, :], hres.rearrange("p t n -> p (t n)")).then_inc(spilled, 16)
            with sp.Fori(1, EXP_TILES // 2) as i:
                for b in range(2):
                    for s in range(2):
                        load_u(i, b, s, False)

            v = peer_v[0].rearrange("(e p) d -> e p d", p=P)
            sp.wait_ge(u_turned, CH * EXP_TILES)
            sp.dma_start(nat[:, 0, :], v[0]).then_inc(v_loaded[0], 16)
            sp.dma_start(nat[:, 1, :], v[1]).then_inc(v_loaded[1], 16)
            with sp.Fori(1, EXP_TILES // 2) as i:
                for b in range(2):
                    sp.wait_ge(v_lo, i * 2 + (b - 1))
                    sp.wait_ge(v_hi, i * 4 + (2 * b - 2))
                    sp.dma_start(nat[:, b, :], v[bass.ds(i * 2 + b, 1)][0]).then_inc(v_loaded[b], 16)
            sp.dma_start(store[:, 0:TT * D], h1_spill[:, :]).then_inc(h1_back, 16)
            sp.dma_start(store[:, TT * D:(TT + 1) * D], ln2_g[0].partition_broadcast(P)).then_inc(h1_back, 16)
            sp.dma_start(store[:, (TT + 1) * D:(TT + 2) * D], ln2_b[0].partition_broadcast(P)).then_inc(h1_back, 16)
            for t in range(TT):
                sp.wait_ge(out_ready, t + 1)
                sp.dma_start(out[0, t * P:(t + 1) * P, :], store[:, t * D:(t + 1) * D]).then_inc(stored, 16)
            sp.wait_ge(stored, 16 * TT)

        @block.gpsimd
        def _(pool):
            def load_gb(g, b):
                pool.dma_start(gb[:, 0, :], g.partition_broadcast(P)).then_inc(gb_loaded, 16)
                pool.dma_start(gb[:, 1, :], b.partition_broadcast(P)).then_inc(gb_loaded, 16)

            load_gb(ln0_g, ln0_b)
            pool.dma_start(metab, meta_tokens[:, :]).then_inc(x_loaded[2], 16)
            for at, rows, src in ((G_Q, QT, q_norm_g[0]), (G_KV, KVT, kv_norm_g[0]), (G_ATT, AT, attn_out_g[0]),
                                  (G_CONV, CT, conv_out_g[0])):
                pool.dma_start(grows[at:at + rows, :], src.rearrange("(k p) -> k p", p=P)).then_inc(small_loaded, 16)
            pool.dma_start(grows[G_CW:G_N, :], conv_w[0].rearrange("j (k p) -> (j k) p", p=P)).then_inc(small_loaded, 16)
            pool.dma_start(sk, peer_sub_keys[0].rearrange("c k d -> k c d")).then_inc(small_loaded, 16)

            def load_head(h, slot, wait):
                if wait is not None:
                    pool.wait_ge(qkv_done, wait)
                uq = att_w[slot][:, 0:QT * 2 * P].rearrange("p (k n) -> p k n", k=QT)
                ukv = att_w[slot][:, QT * 2 * P:].rearrange("p (k n) -> p k n", k=KVT)
                srcq = w_uq[0].rearrange("(k p) n -> p k n", p=P)
                half = D_ROPE // 2
                for to, frm, w in ((0, 0, D_QK), (D_QK, D_NOPE + half, half), (D_QK + half, D_NOPE, half)):
                    pool.dma_start(uq[:, :, to:to + w], srcq[:, :, bass.ds(h * D_QK + frm, w)]
                                   ).then_inc(att_w_loaded[slot], 16)
                pool.dma_start(ukv, w_ukv[0].rearrange("(k p) n -> p k n", p=P)[
                    :, :, bass.ds(h * (D_NOPE + D_V), D_NOPE + D_V)]).then_inc(att_w_loaded[slot], 16)

            load_head(0, 0, None)
            load_head(1, 1, None)
            pool.wait_ge(h_ready, 3)
            load_gb(ln1_g[0], ln1_b[0])
            with pool.Fori(1, HEADS // 2) as i:
                load_head(i * 2, 0, i * 6 - 3)
                load_head(i * 2 + 1, 1, i * 6)

            pool.wait_ge(choice_copied, 2)
            nc.gpsimd.memset(store[:, 2 * GATES_AT * SEQ:], 1.0).then_inc(store_set, 1)

            def second_distance(i, k, first):
                if not first:
                    pool.wait_ge(gates_done, i * (2 * CH) + (k - 1))
                full = [P, NT, P]
                nc.gpsimd.tensor_tensor(
                    second_rows[k % 2].rearrange("p (t k) -> p t k", t=NT), iota.unsqueeze(1).to_broadcast(full),
                    turnedc[:, 1, bass.ds(i * (2 * CH * NT) + k * NT, NT)].unsqueeze(2).to_broadcast(full),
                    ALU.subtract).then_inc(second_diff, 1)

            for k in range(2 * CH):
                second_distance(0, k, k < 2)
            with pool.Fori(1, PAIRS - GATES_AT) as i:
                for k in range(2 * CH):
                    second_distance(i, k, False)

        @block.tensor
        def _(pe):
            def mm(o, lhsT, rhs, k, n):
                return nc.tensor.matmul(o, lhsT, rhs, start=(k == 0), stop=(k == n - 1))

            def mm3(o, stat, mov, k, n):
                nc.tensor.matmul(o, stat[0], mov[0], start=(k == 0), stop=False)
                nc.tensor.matmul(o, stat[0], mov[1], start=False, stop=False)
                return nc.tensor.matmul(o, stat[1], mov[0], start=False, stop=(k == n - 1))

            def parts(pair, cut):
                return [cut(a) for a in pair]

            pe.wait_ge(consts_loaded, 32)
            pe.wait_ge(small_loaded, 16 * 6)
            nc.tensor.transpose(ps[7][:, 256:256 + G_N], grows, ident[0:G_N, 0:G_N]).then_inc(gains_turned, 1)
            for c in range(2):
                nc.tensor.transpose(ps[7][:, c * P:(c + 1) * P], sk[:, c, :], ident).then_inc(gains_turned, 1)

            def turn(t, base):
                for g in range(KT // 4):
                    n = t * 4 + g
                    if n >= 4:
                        pe.wait_ge(turned_lo, n - 3 + base)
                    for j in range(4):
                        k = 4 * g + j
                        last = nc.tensor.transpose(ps[3 + n % 4][:, j * P:(j + 1) * P],
                                                   hres[:, t, k * P:(k + 1) * P], ident)
                    last.then_inc(turned, 1)

            for t in range(TT):
                pe.wait_ge(h_ready, t + 1)
                turn(t, 0)
            pe.wait_ge(h_ready, 3)
            pe.wait_ge(turned_lo, 5)
            for k in range(KT):
                last = nc.tensor.transpose(ps[3][:, k * META:(k + 1) * META], metab[:, k * P:(k + 1) * P],
                                           ident[0:META, 0:META])
            last.then_inc(turned, 1)

            pe.wait_ge(turned_lo, 9)

            def tile_chunks(o, chunk0, lo, hi_):
                for c in range(CH):
                    pe.wait_ge(lo_done, chunk0 + (c + 1))
                    for j in range(4):
                        k = 4 * c + j
                        last = mm3(o, parts(chunk_hl[c], lambda a: a[:, j * P:(j + 1) * P]),
                                   parts(act_hl, lambda a: a[:, k, lo:hi_]), k, KT)
                    last.then_inc(chunk_used, 1)

            def project(slot, chunk0, first):
                tile_chunks(ps[slot][:, 0:L - first], chunk0, first, L)

            def low_sums():
                pe.wait_ge(squared, QT)
                for k in range(QT):
                    last = mm(ps[3][:, 0:SEQ], ones, sq[:, k, :], k, QT)
                last.then_inc(sums_ready, 1)
                pe.wait_ge(squared, QT + KVT)
                for k in range(KVT):
                    mm(ps[4][:, META:L], ones, sq[:, QT + k, :], k, KVT)
                for k in range(KVT):
                    last = mm(ps[4][:, 0:META], ones, rs[:, 1, k * META:(k + 1) * META], k, KVT)
                last.then_inc(sums_ready, 1)
                pe.wait_ge(kr2_ready, 1)
                nc.tensor.matmul(ps[5][:, 0:L], fold, kr2, start=True, stop=True).then_inc(folded, 1)

            for n in range(FIRST):
                if n >= 3:
                    pe.wait_ge(bank_freed[n % 3], n // 3)
                project(n % 3, CH * n, META if n < QT else 0)

            def conv_tiles(i, first):
                for k, slot in enumerate((SC, SH, SB)):
                    pe.wait_ge(bank_freed[slot], i + uses[slot])
                    project(slot, i * (3 * CH) + CH * (FIRST + k), META if k == 2 else 0)
                    if first and k == 0:
                        low_sums()

            conv_tiles(0, True)
            with pe.Fori(1, CT) as i:
                conv_tiles(i, False)

            pe.wait_ge(squared, QT + KVT + 1)
            for k in range(CT):
                last = mm(ps[7][:, 0:SEQ], ones, sq[:, k, :], k, CT)
            last.then_inc(sums_ready, 1)

            def qkv(h, b, i):
                pe.wait_ge(att_w_loaded[b], i * 64 + 64)
                after(pe, act_evac, h * 2)
                after(pe, dve_evac, h * 3)
                uq = att_w[b][:, 0:QT * 2 * P].rearrange("p (k n) -> p k n", k=QT)
                ukv = att_w[b][:, QT * 2 * P:].rearrange("p (k n) -> p k n", k=KVT)
                for half in range(2):
                    for k in range(QT):
                        last = mm(ps[7 * half][:, 0:SEQ], uq[:, k, half * P:(half + 1) * P], cq[:, k, :], k, QT)
                last.then_inc(qkv_done, 1)
                for k in range(KVT):
                    last = mm(ps[1][:, 0:L], ukv[:, k, 0:P], ckv[:, k, :], k, KVT)
                last.then_inc(qkv_done, 1)
                for blk, (c0, w) in enumerate(((META, P), (META + P, P), (0, META))):
                    for k in range(KVT):
                        last = mm(ps[2][0:w, blk * P:(blk + 1) * P], ckv[:, k, c0:c0 + w],
                                  ukv[:, k, P:2 * P], k, KVT)
                last.then_inc(qkv_done, 1)

            def score(h, b):
                pe.wait_ge(act_evac, h * 2 + 2)
                pe.wait_ge(dve_evac, h * 3 + 1)
                after(pe, exped, h * 2)
                for t in range(TT):
                    o = ps[3][:, 0:wk] if t == 0 else ps[3][:, wk:wk + L]
                    w = wk if t == 0 else L
                    mm(o, qn[:, b, t * P:(t + 1) * P], kn[:, b, 0:w], 0, 3)
                    mm(o, qrot[:, b, t * P:(t + 1) * P], krot[:, 0:w], 1, 3)
                    mm(o, maskq, maskk[:, L - w:L], 2, 3).then_inc(scored, 1)

            def attend(h, b):
                pe.wait_ge(p_ready, h * 2 + 2)
                after(pe, pT_copied, h)
                after(pe, pTm_copied, h)
                for n, c0 in enumerate((META, wk + META, wk + META + P)):
                    last = nc.tensor.transpose(ps[4][:, n * P:(n + 1) * P], pr[:, b, c0:c0 + P], ident)
                last.then_inc(p_turned, 1)
                for n, c0 in enumerate((0, wk)):
                    last = nc.tensor.transpose(ps[5][0:META, n * P:(n + 1) * P], pr[:, b, c0:c0 + META], ident)
                last.then_inc(p_turned, 1)
                pe.wait_ge(pT_copied, h + 1)
                pe.wait_ge(pTm_copied, h + 1)
                pe.wait_ge(dve_evac, h * 3 + 3)
                after(pe, o_copied, h)
                mm(ps[6][:, 0:P], vt[:, b, 0, :], pT[:, 0, :], 0, 2)
                mm(ps[6][:, 0:P], vt[0:META, b, 2, :], pTm[:, 0, :], 1, 2)
                mm(ps[6][:, P:SEQ], vt[:, b, 0, :], pT[:, 1, :], 0, 3)
                mm(ps[6][:, P:SEQ], vt[:, b, 1, :], pT[:, 2, :], 1, 3)
                mm(ps[6][:, P:SEQ], vt[0:META, b, 2, :], pTm[:, 1, :], 2, 3).then_inc(pv_done, 1)

            pe.wait_ge(normed, 2)
            pe.wait_ge(krot_ready, 1)
            pe.wait_ge(ms_ready, 3)
            for slot in (SC, SH, SB):
                pe.wait_ge(bank_freed[slot], uses[slot] + CT)

            def pair(i, last):
                h = i * 2
                score(h, 0)
                qkv(h + 1, 1, i)
                attend(h, 0)
                score(h + 1, 1)
                if not last:
                    qkv(h + 2, 0, i + 1)
                attend(h + 1, 1)

            qkv(0, 0, 0)
            pair(0, False)
            with pe.Fori(1, HEADS // 2 - 1) as i:
                pair(i, False)
            pair(HEADS // 2 - 1, True)
            pe.wait_ge(squared, QT + KVT + 2)
            for k in range(AT):
                last = mm(ps[7][:, 0:SEQ], ones, sq[:, k, :], k, AT)
            last.then_inc(sums_ready, 1)

            pe.wait_ge(mixed_lo, 2)

            def out_group(g):
                after(pe, res_added, g * TT)
                for k in range(KT):
                    pe.wait_ge(lo_done, g * KT + (C_WO + k + 1))
                    c = k % CH
                    for t in range(TT):
                        last = mm3(ps[t][:, :], parts(act_hl, lambda a: a[:, k, t * P:(t + 1) * P]),
                                   parts(chunk_hl[c], lambda a: a), k, KT)
                    last.then_inc(chunk_used, 1)

            out_group(0)
            with pe.Fori(1, GROUPS) as g:
                out_group(g)

            for t in range(TT):
                pe.wait_ge(h_ready, 4 + t)
                turn(t, 9)
            pe.wait_ge(turned_lo, 17)
            pe.wait_ge(gains_copied, 2)

            def query(i, b):
                after(pe, pq_copied, i * 2 + (b - 1))
                tile_chunks(ps[6 + b][:, 0:SEQ], i * (2 * CH) + (C_WQ + CH * b), 0, SEQ)

            def key_scores(i, b):
                pe.wait_ge(pq_copied, i * 2 + (b + 1))
                after(pe, scores_kept, i * 2 + (b - 1))
                for t in range(TT):
                    last = nc.tensor.matmul(ps[4 + b][:, t * P:(t + 1) * P], moT[:, b, t * P:(t + 1) * P],
                                            skT[:, b, :], start=True, stop=True)
                last.then_inc(keys_done, 1)

            query(0, 0)
            query(0, 1)
            key_scores(0, 0)
            with pe.Fori(1, HEADS) as i:
                query(i, 0)
                key_scores(i - 1, 1)
                query(i, 1)
                key_scores(i, 0)

            def turn_u(i, b, c):
                pe.wait_ge(u_loaded[2 * b + c // 2], i * 16 + 16)
                for j in range(4):
                    last = nc.tensor.transpose(ps[c][:, j * P:(j + 1) * P], nat[:, b, (4 * c + j) * P:(4 * c + j + 1) * P],
                                               ident)
                last.then_inc(u_turned, 1)

            def gates(i, b, c, first):
                s, o = step_of(i, b, c), c % 2
                pe.wait_ge(second_hot, s + 1)
                pe.wait_ge(first_hot, s + 1)
                if not first:
                    pe.wait_ge(store_step, multiplied(i, b, c - 1 if c >= 2 else c - 2))
                for t in range(NT):
                    last = nc.tensor.matmul(ps[4 + o][:, t * P:(t + 1) * P], second_rows[o][:, t * P:(t + 1) * P],
                                            first_rows[o][:, t * P:(t + 1) * P], start=True, stop=True)
                last.then_inc(gates_done, 1)

            def dot_u(i, b, last_tile=False, with_gates=False, first=False):
                for c in range(CH):
                    pe.wait_ge(lo_done, i * (2 * CH) + (C_U + CH * b + c + 1))
                    if not last_tile:
                        turn_u(i + b, 1 - b, c)
                    if c == 0:
                        if with_gates and not first:
                            pe.wait_ge(store_step, multiplied(i - 1, b, CH + 1))
                        else:
                            after(pe, gelu_done, i * 2 + (b - 1))
                    for j in range(4):
                        k = 4 * c + j
                        last = mm3(ps[6 + b][:, 0:SEQ], parts(chunk_hl[c], lambda a: a[:, j * P:(j + 1) * P]),
                                   parts(act_hl, lambda a: a[:, k, 0:SEQ]), k, KT)
                    last.then_inc(chunk_used, 1)
                    if with_gates:
                        gates(i, b, c, first and b == 0 and c < 2)

            for c in range(CH):
                turn_u(0, 0, c)
            key_scores(HEADS - 1, 1)
            dot_u(0, 0)
            dot_u(0, 1)
            with pe.Fori(1, TURNED_AT) as i:
                dot_u(i, 0)
                dot_u(i, 1)

            pe.wait_ge(gate_step, 4)
            pe.wait_ge(scores_kept, 2 * HEADS)
            for c in range(2):
                for t in range(TT):
                    last = nc.tensor.transpose(ps[4][:, (c * TT + t) * P:(c * TT + t + 1) * P],
                                               chosen[:, c, t * P:(t + 1) * P], ident)
            last.then_inc(choice_turned, 1)
            for t in range(TT):
                last = nc.tensor.transpose(ps[5][:, t * P:(t + 1) * P], gate[:, t * P:(t + 1) * P], ident)
            last.then_inc(choice_turned, 1)

            with pe.Fori(TURNED_AT, GATES_AT) as i:
                dot_u(i, 0)
                dot_u(i, 1)
            pe.wait_ge(choice_copied, 2)
            dot_u(GATES_AT, 0, with_gates=True, first=True)
            dot_u(GATES_AT, 1, with_gates=True, first=True)
            with pe.Fori(GATES_AT + 1, PAIRS - 1) as i:
                dot_u(i, 0, with_gates=True)
                dot_u(i, 1, with_gates=True)
            dot_u(PAIRS - 1, 0, with_gates=True)
            dot_u(PAIRS - 1, 1, last_tile=True, with_gates=True)

            pe.wait_ge(store_step, multiplied(PAIRS, 0, 0))

            def times_v(i, b, first, last_tile):
                pe.wait_ge(v_lo, i * 2 + (b + 1))
                pe.wait_ge(w_lo, i * 2 + (b + 1))
                for t in range(TT):
                    for g in range(4):
                        w = parts(w_hl[b], lambda a: a[:, t * P:(t + 1) * P])
                        vv = parts(v_hl[b], lambda a: a[:, g * 512:(g + 1) * 512])
                        o = ps[4 * t + g][:, :]
                        nc.tensor.matmul(o, w[0], vv[0], start=first, stop=False)
                        nc.tensor.matmul(o, w[0], vv[1], start=False, stop=False)
                        last = nc.tensor.matmul(o, w[1], vv[0], start=False, stop=last_tile)
                last.then_inc(v_used, 1)

            times_v(0, 0, True, False)
            times_v(0, 1, False, False)
            with pe.Fori(1, EXP_TILES // 2 - 1) as i:
                times_v(i, 0, False, False)
                times_v(i, 1, False, False)
            times_v(EXP_TILES // 2 - 1, 0, False, False)
            times_v(EXP_TILES // 2 - 1, 1, False, True)

        @block.scalar
        def _(act):
            def std(n):
                act.wait_ge(var_ready, n)
                nc.scalar.activation(rstd[:, 0:1], mv[:, 1:2], ACT.Sqrt).then_inc(std_ready, 1)

            def hi_turned(n, base):
                t, g = n // 4, n % 4
                act.wait_ge(turned, base + n + 1)
                lo = (META if base == 0 else 0) + t * P
                nc.scalar.copy(act_hl[0][:, 4 * g:4 * g + 4, lo:lo + P],
                               ps[3 + n % 4][:, :].rearrange("p (k n) -> p k n", k=4)).then_inc(turned_hi, 1)

            def hi_chunks(chunk0, src, loaded, count):
                act.wait_ge(loaded, count)
                for c in range(CH):
                    after(act, chunk_used, chunk0 + (c + 1 - CH))
                    nc.scalar.copy(chunk_hl[c][0], src[:, c * CK:(c + 1) * CK]).then_inc(hi_done, 1)

            std(1)
            std(2)
            std(3)
            act.wait_ge(gains_turned, 3)
            nc.scalar.copy(gains[:, :], ps[7][:, 256:256 + G_N]).then_inc(gains_copied, 1)
            nc.scalar.copy(skT, ps[7][:, 0:2 * P].rearrange("p (c n) -> p c n", c=2)).then_inc(gains_copied, 1)
            hi_chunks(0, wnat[0], w_loaded[0], 16)
            for n in range(8):
                hi_turned(n, 0)
            act.wait_ge(turned, 9)
            nc.scalar.copy(act_hl[0][:, :, 0:META], ps[3][:, 0:KT * META].rearrange("p (k n) -> p k n", k=KT)
                           ).then_inc(turned_hi, 1)

            def hi_first(n):
                hi_chunks(CH * n, wnat[n % 3], kr_loaded if n == KR_TILE else w_loaded[n % 3],
                          48 if n == KR_TILE else 16 * (n // 3 + 1))

            for n in range(KR_TILE):
                hi_first(n + 1)
                act.wait_ge(chunk_used, CH * (n + 1))
                b = ps[n % 3]
                if n < QT:
                    nc.scalar.copy(cq[:, n, :], b[:, 0:SEQ]).then_inc(low_copied, 1)
                    nc.scalar.activation(sq[:, n, :], b[:, 0:SEQ], ACT.Square).then_inc(squared, 1)
                else:
                    k = n - QT
                    nc.scalar.copy(ckv[:, k, :], b[:, 0:L]).then_inc(low_copied, 1)
                    nc.scalar.activation(rs[:, 1, k * META:(k + 1) * META], b[:, 0:META], ACT.Square)
                    nc.scalar.activation(sq[:, n, :], b[:, META:L], ACT.Square).then_inc(squared, 1)
                act.wait_ge(squared, n + 1)
                act.sem_inc(bank_freed[n % 3], 1)

            def rms(n, w):
                s = n % 2
                act.wait_ge(ms_ready, n + 1)
                nc.scalar.activation(rs[:, s, 0:w], rs[:, s, 0:w], ACT.Sqrt).then_inc(rms_ready, 1)

            def conv_hi(i, k, slot):
                hi_chunks(i * (3 * CH) + CH * (FIRST + k), wnat[slot], w_loaded[slot], i * 16 + 16 * (fills[slot] + 1))

            def keep_c(i):
                act.wait_ge(chunk_used, i * (3 * CH) + CH * (FIRST + 1))
                act.wait_ge(bank_freed[SH], i + uses[SH])
                nc.scalar.copy(cgate, ps[SC][:, 0:L]).then_inc(bank_freed[SC], 1)

            conv_hi(0, 0, SC)
            conv_hi(0, 1, SH)
            keep_c(0)
            conv_hi(0, 2, SB)
            rms(0, SEQ)
            rms(1, L)
            act.wait_ge(folded, 1)
            nc.scalar.copy(krot, ps[5][:, 0:L]).then_inc(krot_ready, 1)
            with act.Fori(1, CT) as i:
                conv_hi(i, 0, SC)
                conv_hi(i, 1, SH)
                keep_c(i)
                conv_hi(i, 2, SB)
            act.wait_ge(bank_freed[SB], uses[SB] + CT)
            nc.scalar.activation(sq, mixT[:, AT:AT + CT, :], ACT.Square).then_inc(squared, 1)
            rms(2, SEQ)
            hi_chunks(C_WO, wnat[2], w2_loaded[0], 16)

            def head(h, b):
                act.wait_ge(qkv_done, h * 3 + 1)
                nc.scalar.copy(qn[:, b, :], ps[0][:, 0:SEQ]).then_inc(act_evac, 1)
                act.wait_ge(qkv_done, h * 3 + 2)
                nc.scalar.copy(kn[:, b, :], ps[1][:, 0:L]).then_inc(act_evac, 1)

            def softmax_exp(h, b):
                for t in range(TT):
                    lo, w = (0, wk) if t == 0 else (wk, L)
                    act.wait_ge(shifted, h * 2 + 2)
                    nc.scalar.activation(pr[:, b, lo:lo + w], ps[3][:, lo:lo + w], ACT.Exp,
                                         bias=smx[:, b, 2 + t:3 + t], scale=SCALE,
                                         accum_out=smx[:, b, 4 + t:5 + t]).then_inc(exped, 1)

            def output(h, b):
                act.wait_ge(p_turned, h * 2 + 1)
                nc.scalar.copy(pT, ps[4][:, 0:3 * P].rearrange("p (k n) -> p k n", k=3)).then_inc(pT_copied, 1)
                act.wait_ge(pv_done, h + 1)
                nc.scalar.copy(mixT[:, bass.ds(h, 1), :], ps[6][:, 0:SEQ].unsqueeze(1)).then_inc(o_copied, 1)

            def pair(i, last):
                h = i * 2
                softmax_exp(h, 0)
                head(h + 1, 1)
                output(h, 0)
                softmax_exp(h + 1, 1)
                if not last:
                    head(h + 2, 0)
                output(h + 1, 1)

            head(0, 0)
            act.wait_ge(normed, 3)
            nc.scalar.copy(act_hl[0][:, AT:AT + CT, 0:SEQ], mixT[:, AT:AT + CT, :]).then_inc(mixed_hi, 1)
            pair(0, False)
            with act.Fori(1, HEADS // 2 - 1) as i:
                pair(i, False)
            pair(HEADS // 2 - 1, True)
            act.wait_ge(o_copied, HEADS)
            nc.scalar.activation(sq, mixT[:, 0:AT, :], ACT.Square).then_inc(squared, 1)
            rms(3, SEQ)
            act.wait_ge(normed, 4)
            nc.scalar.copy(act_hl[0][:, 0:AT, 0:SEQ], mixT[:, 0:AT, :]).then_inc(mixed_hi, 1)

            def block_hi(n, j):
                hi_chunks(n * KT + (C_WO + CH * j), wnat[2 + j % 2], w2_loaded[j % 2], n * 32 + 16 * (j // 2 + 1))

            for j in (1, 2, 3):
                block_hi(0, j)
            with act.Fori(1, GROUPS) as g:
                for j in range(4):
                    block_hi(g, j)

            def query_hi(i, b):
                hi_chunks(i * (2 * CH) + (C_WQ + CH * b), wnat[2 + b], w2_loaded[b], i * 16 + (KT // 2 + 1) * 16)

            def keep_query(i, b):
                act.wait_ge(chunk_used, i * (2 * CH) + (C_WQ + CH * (b + 1)))
                after(act, keys_done, i * 2 + (b - 1))
                nc.scalar.copy(moT[:, b, :], ps[6 + b][:, 0:SEQ]).then_inc(pq_copied, 1)

            def hi_chunk_u(i, b, c):
                act.wait_ge(u_turned, i * (2 * CH) + (CH * b + c + 1))
                act.wait_ge(chunk_used, i * (2 * CH) + (C_U + CH * b + c + 1 - CH))
                nc.scalar.copy(chunk_hl[c][0], ps[c][:, :]).then_inc(hi_done, 1)

            def hi_u(i, b):
                for c in range(CH):
                    hi_chunk_u(i, b, c)

            query_hi(0, 0)
            std(4)
            std(5)
            for n in range(8):
                hi_turned(n, 9)
            query_hi(0, 1)
            keep_query(0, 0)
            with act.Fori(1, HEADS) as i:
                query_hi(i, 0)
                keep_query(i - 1, 1)
                query_hi(i, 1)
                keep_query(i, 0)
            hi_u(0, 0)
            keep_query(HEADS - 1, 1)

            def gelu(i, b, in_place=False):
                act.wait_ge(chunk_used, i * (2 * CH) + (C_U + CH * (b + 1)))
                to = ps[6 + b][:, 0:SEQ].unsqueeze(1) if in_place else by_expert[:, bass.ds(i * 2 + b, 1), :]
                nc.scalar.activation(to, ps[6 + b][:, 0:SEQ].unsqueeze(1), ACT.Gelu).then_inc(gelu_done, 1)

            def act_u(i):
                hi_u(i, 1)
                gelu(i, 0)
                hi_u(i + 1, 0)
                gelu(i, 1)

            act.wait_ge(spilled, 16)
            act_u(0)
            with act.Fori(1, PICKED_AT + 1) as i:
                act_u(i)
            act.wait_ge(gate_step, 1)
            nc.scalar.activation(gate[:, :], gate[:, :], ACT.Exp).then_inc(gate_exped, 1)
            with act.Fori(PICKED_AT + 1, TURNED_AT) as i:
                act_u(i)
            act.wait_ge(choice_turned, 1)
            nc.scalar.copy(turnedc[:, 0:2, :], ps[4][:, :].rearrange("p (c n) -> p c n", c=2)).then_inc(choice_copied, 1)
            act.wait_ge(choice_turned, 2)
            nc.scalar.copy(turnedc[:, 2, :], ps[5][:, 0:SEQ]).then_inc(choice_copied, 1)
            with act.Fori(TURNED_AT, GATES_AT) as i:
                act_u(i)

            def second_square(s, b):
                act.wait_ge(second_diff, s + 1)
                nc.scalar.activation(second_rows[b], second_rows[b], ACT.Square).then_inc(second_sq, 1)

            def second_relu(s, b):
                act.wait_ge(second_sq, s + 1)
                nc.scalar.activation(second_rows[b], second_rows[b], ACT.Relu, scale=-1.0, bias=1.0
                                     ).then_inc(second_hot, 1)

            def act_tile(i, b, last_tile=False):
                for c in range(CH):
                    s, ahead = step_of(i, b, c) + 1, not last_tile or c < CH - 1
                    if ahead:
                        second_square(s, (c + 1) % 2)
                    if not last_tile:
                        hi_chunk_u(i + b, 1 - b, c)
                    if ahead:
                        second_relu(s, (c + 1) % 2)
                gelu(i, b, in_place=True)

            second_square(0, 0)
            second_relu(0, 0)
            with act.Fori(GATES_AT, PAIRS - 1) as i:
                act_tile(i, 0)
                act_tile(i, 1)
            act_tile(PAIRS - 1, 0)
            act_tile(PAIRS - 1, 1, last_tile=True)

            def split_v(i, b):
                act.wait_ge(v_loaded[b], i * 16 + 16)
                after(act, v_used, i * 2 + (b - 1))
                nc.scalar.copy(v_hl[b][0], nat[:, b, :]).then_inc(v_hi, 1)
                if isinstance(i, int):
                    act.wait_ge(store_step, multiplied(PAIRS, 0, 0))
                nc.scalar.copy(w_hl[b][0].unsqueeze(1), by_expert[:, bass.ds(i * 2 + b, 1), :]).then_inc(v_hi, 1)

            split_v(0, 0)
            split_v(0, 1)
            with act.Fori(1, EXP_TILES // 2) as i:
                split_v(i, 0)
                split_v(i, 1)
            std(6)
            std(7)

        @block.vector
        def _(dve):
            steps = [0]

            def link(ins):
                steps[0] += 1
                ins.then_inc(stat_step, 1)
                dve.wait_ge(stat_step, steps[0])

            norms = [0]

            def layer_norm(xb, p, g, b, done):
                norms[0] += 1
                for j in range(4):
                    last = nc.vector.bn_stats(stats[0:p, j, :], xb[:, j * 512:(j + 1) * 512])
                link(last)
                link(nc.vector.bn_aggr(mv[0:p, :], stats[0:p, :, :].rearrange("p j s -> p (j s)")))
                nc.vector.tensor_scalar(mv[:, 1:2], mv[:, 1:2], EPS, None, ALU.add).then_inc(var_ready, 1)
                dve.wait_ge(std_ready, norms[0])
                link(nc.vector.reciprocal(rstd[:, 1:2], rstd[:, 0:1]))
                link(nc.vector.tensor_scalar(xb, xb, mv[0:p, 0:1], rstd[0:p, 1:2], ALU.subtract, ALU.mult))
                link(nc.vector.tensor_tensor(xb, xb, g[0:p, :], ALU.mult))
                nc.vector.tensor_tensor(xb, xb, b[0:p, :], ALU.add).then_inc(done, 1)

            def lo_part(o, src, hi):
                return nc.vector.tensor_tensor(o, src, hi.bitcast(F32), ALU.subtract)

            def lo_turned(n, base):
                t, g = n // 4, n % 4
                dve.wait_ge(turned_hi, base + n + 1)
                lo = (META if base == 0 else 0) + t * P
                lo_part(act_hl[1][:, 4 * g:4 * g + 4, lo:lo + P], ps[3 + n % 4][:, :].rearrange("p (k n) -> p k n", k=4),
                        act_hl[0][:, 4 * g:4 * g + 4, lo:lo + P]).then_inc(turned_lo, 1)

            def lo_chunks(chunk0, src):
                for c in range(CH):
                    dve.wait_ge(hi_done, chunk0 + (c + 1))
                    lo_part(chunk_hl[c][1], src[:, c * CK:(c + 1) * CK], chunk_hl[c][0]).then_inc(lo_done, 1)

            link(nc.vector.memset(mv[:, :], 1.0))
            dve.wait_ge(x_loaded[0], 16)
            dve.wait_ge(gb_loaded, 32)
            layer_norm(hres[:, 0, :], P, gb[:, 0, :], gb[:, 1, :], h_ready)
            dve.wait_ge(x_loaded[1], 16)
            layer_norm(hres[:, 1, :], P, gb[:, 0, :], gb[:, 1, :], h_ready)
            dve.wait_ge(x_loaded[2], 16)
            layer_norm(metab, META, gb[:, 0, :], gb[:, 1, :], h_ready)
            lo_chunks(0, wnat[0])
            for n in range(8):
                lo_turned(n, 0)
            dve.wait_ge(turned_hi, 9)
            lo_part(act_hl[1][:, :, 0:META], ps[3][:, 0:KT * META].rearrange("p (k n) -> p k n", k=KT),
                    act_hl[0][:, :, 0:META]).then_inc(turned_lo, 1)
            for n in range(1, FIRST):
                lo_chunks(CH * n, wnat[n % 3])

            def mean_squares(n, bank, w, dim):
                dve.wait_ge(sums_ready, n + 1)
                nc.vector.tensor_scalar(rs[:, n % 2, 0:w], ps[bank][:, 0:w], 1.0 / dim, EPS, ALU.mult, ALU.add
                                        ).then_inc(ms_ready, 1)

            def rms_scale(n, w, tiles, gain):
                dve.wait_ge(rms_ready, n + 1)
                link(nc.vector.reciprocal(rs[:, n % 2, 0:w], rs[:, n % 2, 0:w]))
                for k, tile in enumerate(tiles):
                    last = nc.vector.scalar_tensor_tensor(out=tile, in0=tile, scalar=gains[:, gain + k:gain + k + 1],
                                                          in1=rs[:, n % 2, 0:w], op0=ALU.mult, op1=ALU.mult)
                last.then_inc(normed, 1)

            def conv_lo(i, k, slot):
                lo_chunks(i * (3 * CH) + CH * (FIRST + k), wnat[slot])

            def convolve(i):
                dve.wait_ge(chunk_used, i * (3 * CH) + CH * (FIRST + 2))
                dve.wait_ge(bank_freed[SC], i + (uses[SC] + 1))
                nc.vector.tensor_tensor(ubuf, ps[SH][:, 0:L], cgate, ALU.mult).then_inc(bank_freed[SH], 1)
                dve.wait_ge(bank_freed[SH], i + (uses[SH] + 1))
                lo = META - CONV_W + 1
                nc.vector.tensor_scalar(ybuf, ubuf[:, lo:lo + SEQ], gains[:, bass.ds(i + G_CW, 1)], None,
                                        ALU.mult).then_inc(conv_step, 1)
                for j in range(1, CONV_W):
                    dve.wait_ge(conv_step, i * CONV_W + j)
                    nc.vector.scalar_tensor_tensor(out=ybuf, in0=ubuf[:, lo + j:lo + j + SEQ],
                                                   scalar=gains[:, bass.ds(i + (G_CW + j * CT), 1)], in1=ybuf,
                                                   op0=ALU.mult, op1=ALU.add).then_inc(conv_step, 1)

            def gate_conv(i):
                dve.wait_ge(conv_step, i * CONV_W + CONV_W)
                dve.wait_ge(chunk_used, i * (3 * CH) + CH * (FIRST + 3))
                nc.vector.tensor_tensor(mixT[:, bass.ds(i + AT, 1), :], ps[SB][:, 0:SEQ].unsqueeze(1),
                                        ybuf.unsqueeze(1), ALU.mult).then_inc(bank_freed[SB], 1)

            conv_lo(0, 0, SC)
            dve.wait_ge(chunk_used, CH * FIRST)
            nc.vector.tensor_tensor(kr2, ps[KR_TILE % 3][:, 0:L], rope, ALU.mult).then_inc(kr2_ready, 1)
            dve.wait_ge(kr2_ready, 1)
            dve.sem_inc(bank_freed[KR_TILE % 3], 1)
            conv_lo(0, 1, SH)
            mean_squares(0, 3, SEQ, Q_RANK)
            mean_squares(1, 4, L, KV_RANK)
            conv_lo(0, 2, SB)
            dve.wait_ge(low_copied, QT + KVT)
            dve.wait_ge(gains_copied, 2)
            rms_scale(0, SEQ, [cq[:, k, :] for k in range(QT)], G_Q)
            rms_scale(1, L, [ckv[:, k, :] for k in range(KVT)], G_KV)
            convolve(0)
            with dve.Fori(1, CT) as i:
                conv_lo(i, 0, SC)
                gate_conv(i - 1)
                conv_lo(i, 1, SH)
                conv_lo(i, 2, SB)
                convolve(i)
            gate_conv(CT - 1)
            dve.wait_ge(squared, QT + KVT + 1)
            mean_squares(2, 7, SEQ, CONV_DIM)
            rms_scale(2, SEQ, [mixT[:, AT + k, :] for k in range(CT)], G_CONV)
            lo_chunks(C_WO, wnat[2])

            def head(h, b):
                dve.wait_ge(qkv_done, h * 3 + 1)
                nc.vector.tensor_tensor(qrot[:, b, :], ps[7][:, 0:SEQ], rope[:, META:L], ALU.mult
                                        ).then_inc(dve_evac, 1)
                dve.wait_ge(qkv_done, h * 3 + 3)
                nc.vector.tensor_copy(vt[:, b, 0:2, :], ps[2][:, 0:2 * P].rearrange("p (k n) -> p k n", k=2)
                                      ).then_inc(dve_evac, 1)
                nc.vector.tensor_copy(vt[0:META, b, 2, :], ps[2][0:META, 2 * P:3 * P]).then_inc(dve_evac, 1)

            def softmax(h, b):
                dve.wait_ge(scored, h * 2 + 2)
                for t in range(TT):
                    lo, w = (0, wk) if t == 0 else (wk, L)
                    nc.vector.tensor_reduce(smx[:, b, t:t + 1], ps[3][:, lo:lo + w], AX.X, ALU.max
                                            ).then_inc(att_step, 1)
                for t in range(TT):
                    dve.wait_ge(att_step, h * 4 + (t + 1))
                    nc.vector.tensor_scalar(smx[:, b, 2 + t:3 + t], smx[:, b, t:t + 1], -SCALE, None, ALU.mult
                                            ).then_inc(shifted, 1)
                for t in range(TT):
                    lo, w = (0, wk) if t == 0 else (wk, L)
                    dve.wait_ge(exped, h * 2 + (t + 1))
                    nc.vector.reciprocal(smx[:, b, 6 + t:7 + t], smx[:, b, 4 + t:5 + t]).then_inc(att_step, 1)
                    dve.wait_ge(att_step, h * 4 + (t + 3))
                    nc.vector.tensor_scalar(pr[:, b, lo:lo + w], pr[:, b, lo:lo + w], smx[:, b, 6 + t:7 + t], None,
                                            ALU.mult).then_inc(p_ready, 1)

            def turned_meta(h):
                dve.wait_ge(p_turned, h * 2 + 2)
                nc.vector.tensor_copy(pTm, ps[5][0:META, 0:2 * P].rearrange("p (k n) -> p k n", k=2)
                                      ).then_inc(pTm_copied, 1)

            def pair(i, last):
                h = i * 2
                softmax(h, 0)
                head(h + 1, 1)
                turned_meta(h)
                softmax(h + 1, 1)
                if not last:
                    head(h + 2, 0)
                turned_meta(h + 1)

            head(0, 0)
            dve.wait_ge(mixed_hi, 1)
            lo_part(act_hl[1][:, AT:AT + CT, 0:SEQ], mixT[:, AT:AT + CT, :], act_hl[0][:, AT:AT + CT, 0:SEQ]
                    ).then_inc(mixed_lo, 1)
            pair(0, False)
            with dve.Fori(1, HEADS // 2 - 1) as i:
                pair(i, False)
            pair(HEADS // 2 - 1, True)
            dve.wait_ge(o_copied, HEADS)
            dve.wait_ge(squared, QT + KVT + 2)
            mean_squares(3, 7, SEQ, AT * P)
            rms_scale(3, SEQ, [mixT[:, k, :] for k in range(AT)], G_ATT)
            dve.wait_ge(mixed_hi, 2)
            lo_part(act_hl[1][:, 0:AT, 0:SEQ], mixT[:, 0:AT, :], act_hl[0][:, 0:AT, 0:SEQ]).then_inc(mixed_lo, 1)

            def add_residual(g):
                dve.wait_ge(chunk_used, g * KT + (C_WO + KT))
                for t in range(TT):
                    cols = bass.ds(g * 512, 512)
                    nc.vector.scalar_tensor_tensor(
                        out=hres[:, t, cols], in0=hres[:, t, cols], scalar=ALPHA, in1=ps[t][:, :],
                        op0=ALU.mult, op1=ALU.add).then_inc(res_added, 1)

            def block_lo(g, j):
                lo_chunks(g * KT + (C_WO + CH * j), wnat[2 + j % 2])

            for j in (1, 2, 3):
                block_lo(0, j)
            with dve.Fori(1, GROUPS) as g:
                block_lo(g, 0)
                add_residual(g - 1)
                for j in (1, 2, 3):
                    block_lo(g, j)
            lo_chunks(C_WQ, wnat[2])
            add_residual(GROUPS - 1)
            dve.wait_ge(res_added, TT * GROUPS)
            dve.wait_ge(gb_loaded, 64)
            for t in range(TT):
                layer_norm(hres[:, t, :], P, gb[:, 0, :], gb[:, 1, :], h_ready)
            for n in range(8):
                lo_turned(n, 9)

            def query_lo(i, b):
                lo_chunks(i * (2 * CH) + (C_WQ + CH * b), wnat[2 + b])

            by_tile = scores.rearrange("p (t h) c k -> p t (h c k)", t=TT)

            def keep_scores(i, b):
                dve.wait_ge(keys_done, i * 2 + (b + 1))
                nc.vector.tensor_copy(by_tile[:, :, bass.ds(i * (2 * N_KEYS) + b * N_KEYS, N_KEYS)],
                                      ps[4 + b][:, 0:SEQ].rearrange("p (t n) -> p t n", t=TT)
                                      ).then_inc(scores_kept, 1)

            def lo_chunk_u(i, b, c):
                dve.wait_ge(hi_done, i * (2 * CH) + (C_U + CH * b + c + 1))
                lo_part(chunk_hl[c][1], ps[c][:, :], chunk_hl[c][0]).then_inc(lo_done, 1)

            def lo_u(i, b):
                for c in range(CH):
                    lo_chunk_u(i, b, c)

            query_lo(0, 1)
            query_lo(1, 0)
            keep_scores(0, 0)
            with dve.Fori(1, HEADS - 1) as i:
                query_lo(i, 1)
                keep_scores(i - 1, 1)
                query_lo(i + 1, 0)
                keep_scores(i, 0)
            query_lo(HEADS - 1, 1)
            keep_scores(HEADS - 2, 1)
            lo_u(0, 0)
            keep_scores(HEADS - 1, 0)
            keep_scores(HEADS - 1, 1)
            dve.wait_ge(scores_kept, 2 * HEADS)

            PICK_PARTS = (6, 5, 6, 7)

            def pick(q, part):
                n = [0]

                def step(ins):
                    n[0] += 1
                    ins.then_inc(pick_step, 1)
                    dve.wait_ge(pick_step, q * sum(PICK_PARTS) + (sum(PICK_PARTS[:part]) + n[0]))
                    dve.sem_inc(pick_passed, 1)

                def top16(vals, inds, src, spare):
                    step(nc.vector.max(vals[:, 0:8], src))
                    step(nc.vector.max_index(inds[:, 0:8], vals[:, 0:8], src))
                    step(nc.vector.match_replace(spare, vals[:, 0:8], src, -3.0e38))
                    step(nc.vector.max(vals[:, 8:16], spare))
                    step(nc.vector.max_index(inds[:, 8:16], vals[:, 8:16], spare))

                if part == 0:
                    step(nc.vector.tensor_copy(sc.unsqueeze(1), scores[:, bass.ds(q, 1), :, :]))
                if part < 2:
                    c = part
                    top16(tv[:, c, :], ti[:, c, :], sc[:, c, :], sc2[:, c, :])
                    assert n[0] == PICK_PARTS[part]
                    return
                if part == 2:
                    grid = cand.rearrange("p (a b) -> p a b", a=TOPK)
                    step(nc.vector.tensor_tensor(grid, tv[:, 0, :].unsqueeze(2).to_broadcast([P, TOPK, TOPK]),
                                                 tv[:, 1, :].unsqueeze(1).to_broadcast([P, TOPK, TOPK]), ALU.add))
                    top16(bscore[:, :], bi, cand, cand2)
                    assert n[0] == PICK_PARTS[part]
                    return
                nc.vector.tensor_copy(tif[:, :, :], ti[:, :, :])
                nc.vector.tensor_copy(gate[:, bass.ds(q * TOPK, TOPK)], bscore[:, :])
                nc.vector.tensor_scalar(bhl[:, 0, :], bi[:, :], 4, None, ALU.logical_shift_right)
                step(nc.vector.tensor_scalar(bhl[:, 1, :], bi[:, :], TOPK - 1, None, ALU.bitwise_and))
                step(nc.vector.tensor_copy(bhlf[:, :, :], bhl[:, :, :]))
                hot3 = hot.rearrange("p c k j -> p (c k) j")
                both = [P, 2 * TOPK, TOPK]
                step(nc.vector.tensor_tensor(
                    hot3, iota[:, 0:TOPK].unsqueeze(1).to_broadcast(both),
                    bhlf[:, :, :].rearrange("p c k -> p (c k)").unsqueeze(2).to_broadcast(both), ALU.is_equal))
                step(nc.vector.tensor_tensor(hot, hot, tif[:, :, :].unsqueeze(2).to_broadcast([P, 2, TOPK, TOPK]),
                                             ALU.mult))
                step(nc.vector.tensor_reduce(chosen[:, :, bass.ds(q * TOPK, TOPK)], hot, AX.X, ALU.add))
                while n[0] < PICK_PARTS[part]:
                    n[0] += 1
                    dve.sem_inc(pick_step, 1)

            def picking(q):
                for n in range(4):
                    i, b = q * 2 + (n + 1) // 2, (n + 1) % 2
                    lo_chunk_u(i, b, 0)
                    lo_chunk_u(i, b, 1)
                    pick(q, n)
                    lo_chunk_u(i, b, 2)
                    lo_chunk_u(i, b, 3)

            picking(0)
            with dve.Fori(1, PICKS) as q:
                picking(q)

            def dve_u(i):
                lo_u(i, 1)
                lo_u(i + 1, 0)

            g3 = gate[:, :].rearrange("p (q k) -> p q k", k=TOPK)
            full = [P, PICKS, TOPK]
            nc.vector.tensor_copy(gsum[:, 0, :], g3[:, :, 0]).then_inc(gate_started, 1)
            dve.wait_ge(gate_started, 1)
            nc.vector.tensor_tensor(g3, g3, gsum[:, 0, :].unsqueeze(2).to_broadcast(full), ALU.subtract
                                    ).then_inc(gate_step, 1)
            with dve.Fori(PICKED_AT, PICKED_AT + 2) as i:
                dve_u(i)
            dve.wait_ge(gate_exped, 1)
            nc.vector.tensor_reduce(gsum[:, 1, :], g3, AX.X, ALU.add).then_inc(gate_step, 1)
            dve.wait_ge(gate_step, 2)
            nc.vector.reciprocal(gsum[:, 0, :], gsum[:, 1, :]).then_inc(gate_step, 1)
            dve.wait_ge(gate_step, 3)
            nc.vector.tensor_tensor(g3, g3, gsum[:, 0, :].unsqueeze(2).to_broadcast(full), ALU.mult
                                    ).then_inc(gate_step, 1)
            with dve.Fori(PICKED_AT + 2, GATES_AT) as i:
                dve_u(i)

            def hot_first(i, k):
                for t in range(NT):
                    col = bass.ds(i * (2 * CH * NT) + (k * NT + t - GATES_AT * (2 * CH * NT)), 1)
                    last = nc.vector.tensor_scalar(first_rows[k % 2][:, t * P:(t + 1) * P],
                                                   iota, turnedc[:, 0, col], turnedc[:, 2, col],
                                                   ALU.is_equal, ALU.mult)
                last.then_inc(first_hot, 1)

            def apply_gates(i, b, c):
                after(dve, store_step, multiplied(i, b, c))
                cols = by_expert[:, :, bass.ds(token_of(i, b, c), NT)]
                nc.vector.tensor_tensor(cols, cols, ps[4 + c % 2][:, 0:HALF].rearrange("p (t e) -> p e t", t=NT), ALU.mult
                                        ).then_inc(store_step, 1)

            def apply_gelu(i, b):
                dve.wait_ge(gelu_done, i * 2 + (b + 1))
                dve.wait_ge(store_step, multiplied(i, b, CH))
                place = by_expert[:, bass.ds(i * 2 + b, 1), :]
                nc.vector.tensor_tensor(place, place, ps[6 + b][:, 0:SEQ].unsqueeze(1), ALU.mult).then_inc(store_step, 1)

            def dve_tile(i, b, first=False, last_tile=False):
                for c in range(CH):
                    if not last_tile:
                        lo_chunk_u(i + b, 1 - b, c)
                    if c == 1 and not first:
                        apply_gelu(i + (b - 1), 1 - b)
                    if first and c == 0:
                        hot_first(i, 1)
                        continue
                    dve.wait_ge(gates_done, step_of(i, b, c))
                    if not last_tile or c < CH - 1:
                        hot_first(i, CH * b + c + 1)
                    apply_gates(i + (b - 1), 1 - b, CH - 1) if c == 0 else apply_gates(i, b, c - 1)

            dve.wait_ge(choice_copied, 2)
            dve.wait_ge(store_set, 1)
            hot_first(GATES_AT, 0)
            dve_tile(GATES_AT, 0, first=True)
            dve_tile(GATES_AT, 1)
            with dve.Fori(GATES_AT + 1, PAIRS - 1) as i:
                dve_tile(i, 0)
                dve_tile(i, 1)
            dve_tile(PAIRS - 1, 0)
            dve_tile(PAIRS - 1, 1, last_tile=True)
            dve.wait_ge(gates_done, STEPS)
            apply_gates(PAIRS - 1, 1, CH - 1)
            apply_gelu(PAIRS - 1, 1)

            def split_v(i, b):
                dve.wait_ge(v_hi, i * 4 + (2 * b + 1))
                lo_part(v_hl[b][1], nat[:, b, :], v_hl[b][0]).then_inc(v_lo, 1)
                dve.wait_ge(v_hi, i * 4 + (2 * b + 2))
                lo_part(w_hl[b][1].unsqueeze(1), by_expert[:, bass.ds(i * 2 + b, 1), :], w_hl[b][0].unsqueeze(1)
                        ).then_inc(w_lo, 1)

            split_v(0, 0)
            split_v(0, 1)
            with dve.Fori(1, EXP_TILES // 2) as i:
                split_v(i, 0)
                split_v(i, 1)

            dve.wait_ge(h1_back, 48)
            dve.wait_ge(v_used, EXP_TILES)
            for t in range(TT):
                for g in range(4):
                    tile = store[:, t * D + g * 512:t * D + (g + 1) * 512]
                    nc.vector.scalar_tensor_tensor(out=tile, in0=tile, scalar=ALPHA, in1=ps[4 * t + g][:, :],
                                                   op0=ALU.mult, op1=ALU.add).then_inc(joined, 1)
            for t in range(TT):
                dve.wait_ge(joined, 4 * (t + 1))
                layer_norm(store[:, t * D:(t + 1) * D], P, store[:, TT * D:(TT + 1) * D],
                           store[:, (TT + 1) * D:(TT + 2) * D], out_ready)


_INS = ["x", "meta_tokens", "ln0_g", "ln0_b", "w_in", "q_norm_g", "kv_norm_g", "w_uq", "w_ukv", "conv_w",
        "attn_out_g", "conv_out_g", "w_o", "ln1_g", "ln1_b", "peer_w_query", "peer_sub_keys", "peer_u", "peer_v",
        "ln2_g", "ln2_b"]


def kernel(**inputs):
    import concourse.bacc as bacc
    from concourse.bass_utils import run_bass_kernel_spmd

    nc = bacc.Bacc("TRN2", target_bir_lowering=False, num_devices=1)
    arrays, args = {}, []
    for name in _INS + ["const_block"]:
        a = np.ascontiguousarray(inputs[name]) if name in inputs else constants()
        arrays[f"in_{name}"] = a
        args.append(nc.dram_tensor(f"in_{name}", a.shape, mybir.dt.from_np(a.dtype), kind="ExternalInput").ap())
    args.append(nc.dram_tensor("out", (1, SEQ, D), F32, kind="ExternalOutput").ap())
    build(nc, *args)
    return run_bass_kernel_spmd(nc, [arrays], core_ids=[0]).results[0]["out"]
```

```python
from contextlib import ExitStack

import numpy as np

import concourse.bass as bass
from concourse import mybir

ALU = mybir.AluOpType
ACT = mybir.ActivationFunctionType
AX = mybir.AxisListType
F32 = mybir.dt.float32
F32R = mybir.dt.float32r
BF16 = mybir.dt.bfloat16
U32 = mybir.dt.uint32

P = 128
D = 2048
KT = D // P
SEQ = 256
TT = SEQ // P
META = 16
L = META + SEQ
HEADS = 8
D_NOPE, D_ROPE, D_V = 128, 64, 128
D_QK = D_NOPE + D_ROPE
Q_RANK, KV_RANK = 384, 512
QT, KVT = Q_RANK // P, KV_RANK // P
CONV_DIM = 1024
CT = CONV_DIM // P
AT = HEADS * D_V // P
CONV_W = 3
CHUNK = 64
OFF_KR = Q_RANK + KV_RANK
OFF_B = OFF_KR + D_ROPE
OFF_C = OFF_B + CONV_DIM
OFF_H = OFF_C + CONV_DIM
N_KEYS = 128
TOPK = 16
EXP_TILES = N_KEYS
PICKS = TT * HEADS
CH = 4
CK = 4 * P
ALPHA = 2.0 ** 0.25
EPS = 1e-5
SCALE = float(D_QK) ** -0.5
NEG = -2.0 ** 100
THETA = 10000.0

C_ID, C_IOTA, C_KEEP = 0, P, 2 * P
C_ONES, C_FOLD, C_ROPE = C_KEEP, C_KEEP + P, C_KEEP + 2 * P
C_MASKQ = C_ROPE + L
C_MASKK = C_MASKQ + P
C_W = C_MASKK + L

G_Q, G_KV, G_ATT, G_CONV, G_CW = 0, QT, QT + KVT, QT + KVT + AT, QT + KVT + AT + CT
G_N = G_CW + CONV_W * CT


def constants():
    c = np.zeros((P, C_W), np.float32)
    r = np.arange(P)
    c[:, C_ID:C_ID + P] = np.eye(P)
    c[:, C_FOLD:C_FOLD + P] = (r[:, None] % D_ROPE) == (r[None, :] % D_ROPE)
    c[:, C_ONES:C_ONES + P] = 1.0
    inv = (1.0 / (np.float32(THETA) ** (np.arange(0, D_ROPE, 2, dtype=np.float32) / D_ROPE))).astype(np.float32)
    ang = np.arange(L, dtype=np.float32)[None, :] * inv[:, None]
    cos, sin = np.cos(ang), np.sin(ang)
    c[:, C_ROPE:C_ROPE + L] = np.concatenate([cos, cos, -sin, sin])
    c[0, C_MASKQ:C_MASKQ + CHUNK] = 1.0
    c[0, C_MASKK + L - CHUNK:C_MASKK + L] = NEG
    c[:, C_IOTA:C_IOTA + P] = np.arange(P)
    return c


class Carve:

    def __init__(self, tensor, at, end):
        self.tensor, self.at, self.end = tensor, at, end

    def take(self, n, parts=P):
        lo, self.at = self.at, self.at + n
        assert self.at <= self.end, (self.at, self.end)
        return self.tensor[0:parts, lo:lo + n]


def after(eng, sem, value):
    if not isinstance(value, int) or value > 0:
        eng.wait_ge(sem, value)


def build(nc, x, meta_tokens, ln0_g, ln0_b, w_in, q_norm_g, kv_norm_g, w_uq, w_ukv, conv_w, attn_out_g,
          conv_out_g, w_o, ln1_g, ln1_b, peer_w_query, peer_sub_keys, peer_u, peer_v, ln2_g, ln2_b,
          const_block, out):
    ctx = ExitStack()

    def sb(name, shape, dt=F32):
        return ctx.enter_context(nc.sbuf_tensor(name, shape, dt))

    def sem(name):
        return ctx.enter_context(nc.semaphore(name))

    with ctx:
        NT = 2
        STEPS = SEQ // NT
        PAIRS = EXP_TILES // 2
        PICKED_AT = 2 * PICKS
        TURNED_AT = PICKED_AT + 8
        GATES_AT = PAIRS - STEPS // (2 * CH)
        HALF = NT * P
        TURN_BANKS = (1, 2, 3, 4, 5, 7, 1, 2)
        OUT_BLOCKS = [(o, at + CH * j) for at in (AT, 0) for o in range(2) for j in range(2)]
        PAIR_CHUNKS = CH * len(OUT_BLOCKS)
        Q, B = 4, 32
        FLIPPED = 3
        FW, FM = FLIPPED * CK, FLIPPED * 4

        def channels(row, k):
            if k < FM:
                return row[:, 0:FW].rearrange("p (q m) -> p m q", m=FM)[:, k]
            return row[:, FW:].rearrange("p (q m) -> p m q", m=KT - FM)[:, k - FM]

        STEPS_AT = (0, 7, 13, 17)
        PICK_STEPS = 21
        HOT_STEP = 20
        V0 = 3

        store = sb("store", [P, EXP_TILES * SEQ])
        by_expert = store[:, :].rearrange("p (e t) -> p e t", e=EXP_TILES)
        A_COLS = 2 * KT * L
        split = sb("split", [P, A_COLS + CH * 2 * CK], F32R)
        nat = sb("nat", [P, 2, D])
        keep = sb("keep", [P, C_KEEP])
        early = sb("early", [P, C_W - C_KEEP])[:, :]
        gains = sb("gains", [P, G_N])
        smx = sb("smx", [P, 2, 8])
        stats = sb("stats", [P, TT, 4, 6])
        mv = sb("mv", [P, 2, 2])
        rstd = sb("rstd", [P, 2, 2])
        mv_meta = sb("mv_meta", [META, 2])
        mask16 = sb("mask16", [1, P + L], BF16)
        tv = sb("tv", [P, 2, TOPK])
        ti = sb("ti", [P, 2, TOPK], U32)
        tif = sb("tif", [P, 2, TOPK])
        bi = sb("bi", [P, TOPK], U32)
        bhl = sb("bhl", [P, 2, TOPK], U32)
        bhlf = sb("bhlf", [P, 2, TOPK])
        bscore = sb("bscore", [P, TOPK])
        chosen = sb("chosen", [P, 2, PICKS * TOPK])
        gate = sb("gate", [P, PICKS * TOPK])
        gsum = sb("gsum", [P, 2, PICKS])
        turnedc = sb("turnedc", [P, 3, SEQ])
        h1_spill = nc.dram_tensor("h1_spill", (P, TT * D), F32, kind="Internal").ap()

        PICK_AT = 104 * SEQ
        mixT = store[:, 112 * SEQ:].rearrange("p (k n) -> p k n", k=AT + CT)
        scores = store[:, 112 * SEQ:].rearrange("p (q c k) -> p q c k", q=PICKS, c=2)
        hot_c = Carve(store, PICK_AT, 112 * SEQ)
        sc = hot_c.take(2 * N_KEYS).rearrange("p (c k) -> p c k", c=2)
        sc2 = hot_c.take(2 * N_KEYS).rearrange("p (c k) -> p c k", c=2)
        cand, cand2 = hot_c.take(TOPK * TOPK), hot_c.take(TOPK * TOPK)
        hot = hot_c.take(2 * TOPK * TOPK).rearrange("p (c k j) -> p c k j", c=2, k=TOPK)
        carve = Carve(store, 0, PICK_AT)

        def view(n, k):
            return carve.take(n * k).rearrange("p (k n) -> p k n", k=k)

        wnat = [carve.take(D) for _ in range(4)]
        att_w = [carve.take((QT + KVT) * 2 * P) for _ in range(2)]
        metab = carve.take(D, META)
        cq, ckv = view(SEQ, QT), view(L, KVT)
        kr2, krot, cgate, ubuf, ybuf = carve.take(L), carve.take(L), carve.take(L), carve.take(L), carve.take(SEQ)
        rs = view(L, 2)
        qn, qrot, kn = view(SEQ, 2), view(SEQ, 2), view(L, 2)
        vt = carve.take(6 * P).rearrange("p (b k n) -> p b k n", b=2, k=3)
        pr = view(P + META + L, 2)
        pT = view(3 * P, 1).rearrange("p a (k n) -> p (a k) n", k=3)
        pTm = carve.take(2 * P, META).rearrange("p (k n) -> p k n", k=2)
        moT = view(SEQ, 2)
        skT = view(P, 2)
        sk = view(P, 2)
        grows = carve.take(P, G_N)
        hres = view(D, TT)
        sq_flat = store[:, PICK_AT:PICK_AT + 8 * SEQ]
        sq = sq_flat.rearrange("p (k n) -> p k n", k=8)
        sqsum = turnedc[:, 0:1, :]

        gb = nat
        ident, iota = keep[:, C_ID:C_ID + P], keep[:, C_IOTA:C_IOTA + P]
        ones = early[:, C_ONES - C_KEEP:C_ONES - C_KEEP + P]
        fold = early[:, C_FOLD - C_KEEP:C_FOLD - C_KEEP + P]
        rope = early[:, C_ROPE - C_KEEP:C_ROPE - C_KEEP + L]
        maskq, maskk = mask16[:, 0:P], mask16[:, P:P + L]

        act_hl = [split[:, s * KT * L:(s + 1) * KT * L].rearrange("p (k n) -> p k n", k=KT) for s in range(2)]
        chunk_hl = [[split[:, A_COLS + (2 * c + s) * CK:A_COLS + (2 * c + s + 1) * CK] for s in range(2)]
                    for c in range(CH)]

        def u_chunk(b, c):
            if c < FLIPPED:
                return nat[:, b, 0:FW].rearrange("p (s i m) -> p m s i", s=Q, m=FM)[:, 4 * c:4 * c + 4]
            return blocked(ps[c][:, :])

        def blocked(chunk):
            return chunk.rearrange("p (m s i) -> p m s i", m=4, s=Q)

        v_hl = [[split[:, (2 * b + s) * D:(2 * b + s + 1) * D] for s in range(2)] for b in range(2)]
        second_rows = [early[:, b * HALF:(b + 1) * HALF] for b in range(2)]
        first_rows = [chosen[:, b, :] for b in range(2)]
        w_hl = [[split[:, 4 * D + (2 * b + s) * SEQ:4 * D + (2 * b + s + 1) * SEQ] for s in range(2)] for b in range(2)]

        ps = [ctx.enter_context(nc.psum_tensor(f"ps{i}", [P, 512], F32)) for i in range(8)]

        consts_loaded = sem("consts_loaded")
        ident_loaded = sem("ident_loaded")
        x_loaded = [sem(f"x_loaded{b}") for b in range(2 * TT + 1)]
        g_loaded = sem("g_loaded")
        b_loaded = sem("b_loaded")
        gb_loaded = sem("gb_loaded")
        meta_std = sem("meta_std")
        meta_step = sem("meta_step")
        small_loaded = sem("small_loaded")
        w_loaded = [sem(f"w_loaded{s}") for s in range(3)]
        kr_loaded = sem("kr_loaded")
        att_w_loaded = [sem(f"att_w_loaded{b}") for b in range(2)]
        w2_loaded = [sem(f"w2_loaded{b}") for b in range(2)]
        wq_loaded = [sem(f"wq_loaded{b}") for b in range(2)]
        hi_done = sem("hi_done")
        lo_done = sem("lo_done")
        chunk_used = sem("chunk_used")
        stat_step = sem("stat_step")
        var_ready = sem("var_ready")
        std_ready = sem("std_ready")
        h_ready = sem("h_ready")
        turned = sem("turned")
        turned_hi = sem("turned_hi")
        turned_lo = sem("turned_lo")
        gains_turned = sem("gains_turned")
        gains_copied = sem("gains_copied")
        bank_freed = [sem(f"bank_freed{b}") for b in range(3)]
        low_copied = sem("low_copied")
        squared = sem("squared")
        head_summed = sem("head_summed")
        sums_ready = sem("sums_ready")
        ms_ready = sem("ms_ready")
        rms_ready = sem("rms_ready")
        normed = sem("normed")
        kr2_ready = sem("kr2_ready")
        folded = sem("folded")
        krot_ready = sem("krot_ready")
        mask_ready = sem("mask_ready")
        conv_step = sem("conv_step")
        mixed_hi = sem("mixed_hi")
        mixed_lo = sem("mixed_lo")
        qkv_done = sem("qkv_done")
        act_evac = sem("act_evac")
        dve_evac = sem("dve_evac")
        scored = sem("scored")
        att_step = sem("att_step")
        shifted = sem("shifted")
        exped = sem("exped")
        p_ready = sem("p_ready")
        p_turned = sem("p_turned")
        pT_copied = sem("pT_copied")
        pTm_copied = sem("pTm_copied")
        pv_done = sem("pv_done")
        o_copied = sem("o_copied")
        row_done = sem("row_done")
        res_added = sem("res_added")
        spilled = sem("spilled")
        pq_copied = sem("pq_copied")
        keys_done = sem("keys_done")
        scores_kept = sem("scores_kept")
        pick_step = sem("pick_step")
        hot_keyed = sem("hot_keyed")
        pick_passed = sem("pick_passed")
        gate_started = sem("gate_started")
        gate_step = sem("gate_step")
        gate_exped = sem("gate_exped")
        choice_turned = sem("choice_turned")
        choice_copied = sem("choice_copied")
        u_loaded = [sem(f"u_loaded{b}") for b in range(4)]
        u_flipped = sem("u_flipped")
        u_turned = sem("u_turned")
        gelu_done = sem("gelu_done")
        second_diff = sem("second_diff")
        second_sq = sem("second_sq")
        second_hot = sem("second_hot")
        first_equal = sem("first_equal")
        first_hot = sem("first_hot")
        gates_done = sem("gates_done")
        store_set = sem("store_set")
        store_step = sem("store_step")
        v_loaded = [sem(f"v_loaded{b}") for b in range(2)]
        v_hi = sem("v_hi")
        v_lo = sem("v_lo")
        w_lo = sem("w_lo")
        v_used = sem("v_used")
        h1_back = sem("h1_back")
        summed = sem("summed")
        joined = sem("joined")
        out_ready = sem("out_ready")
        stored = sem("stored")

        FIRST = QT + KVT + 1
        KR_TILE = FIRST - 1
        N_IN = FIRST + 3 * CT
        fills = [len([n for n in range(KR_TILE) if n % 3 == s]) for s in range(3)]
        uses = [len([n for n in range(FIRST) if n % 3 == s]) for s in range(3)]
        SC, SH, SB = FIRST % 3, (FIRST + 1) % 3, (FIRST + 2) % 3
        C_WO = CH * N_IN
        C_WQ = C_WO + CH * KT
        C_U = C_WQ + CH * KT
        GROUPS = D // 512
        wk = P + META

        def multiplied(i, b, k):
            return i * (2 * (CH + 1)) + ((CH + 1) * (b - 2 * GATES_AT) + k)

        def step_of(i, b, c):
            return i * (2 * CH) + (CH * (b - 2 * GATES_AT) + c)

        def token_of(i, b, c):
            return i * (2 * CH * NT) + NT * (CH * (b - 2 * GATES_AT) + c)

        block = ctx.enter_context(nc.Block())

        @block.sync
        def _(sp):
            win = w_in[0].rearrange("(k p) n -> p k n", p=P)

            def tile(slot):
                return wnat[slot].rearrange("p (k n) -> p k n", k=KT)

            sp.dma_start(metab, meta_tokens[:, :]).then_inc(x_loaded[2 * TT], 16)
            for t in range(TT):
                for half in range(2):
                    cols = slice(half * (D // 2), (half + 1) * (D // 2))
                    sp.dma_start(hres[:, t, cols], x[0, t * P:(t + 1) * P, cols]).then_inc(x_loaded[2 * t + half], 16)
                if t == 0:
                    sp.dma_start(keep[:, :], const_block[:, 0:C_KEEP]).then_inc(ident_loaded, 16)
                    sp.dma_start(gb[:, 0, :], ln0_g.partition_broadcast(P)).then_inc(g_loaded, 16)
                    sp.dma_start(gb[:, 1, :], ln0_b.partition_broadcast(P)).then_inc(b_loaded, 16)
            for n in range(FIRST):
                if n == 1:
                    sp.dma_start(early, const_block[:, C_KEEP:C_W]).then_inc(consts_loaded, 16)
                if n >= 3:
                    sp.wait_ge(lo_done, CH * (n - 2))
                if n < KR_TILE:
                    sp.dma_start(tile(n % 3), win[:, :, n * P:(n + 1) * P]).then_inc(w_loaded[n % 3], 16)
                else:
                    half = D_ROPE // 2
                    for to, frm, w in ((0, 0, D_ROPE), (D_ROPE, half, half), (D_ROPE + half, 0, half)):
                        sp.dma_start(tile(n % 3)[:, :, to:to + w],
                                     win[:, :, OFF_KR + frm:OFF_KR + frm + w]).then_inc(kr_loaded, 16)
            with sp.Fori(0, CT) as i:
                for k, (slot, off) in enumerate(((SC, OFF_C), (SH, OFF_H), (SB, OFF_B))):
                    sp.wait_ge(lo_done, i * (3 * CH) + CH * (FIRST + k - 2))
                    sp.dma_start(tile(slot), win[:, :, bass.ds(i * P + off, P)]).then_inc(w_loaded[slot], 16)
            wo = w_o[0].rearrange("(k p) n -> p k n", p=P)
            for i in range(GROUPS // 2):
                for n, (o, k) in enumerate(OUT_BLOCKS):
                    g = 2 * i + o
                    sp.wait_ge(lo_done, C_WO + i * PAIR_CHUNKS + CH * (n - 1))
                    sp.dma_start(wnat[2 + n % 2].rearrange("p (k n) -> p k n", k=CH),
                                 wo[:, k:k + CH, g * 512:(g + 1) * 512]).then_inc(w2_loaded[n % 2], 16)
            wq = [peer_w_query[0, rows].rearrange("(p m) n -> p m n", p=P) for rows in (slice(0, FW), slice(FW, D))]
            with sp.Fori(0, HEADS) as i:
                for b in range(2):
                    sp.wait_ge(lo_done, i * (2 * CH) + (C_WQ + CH * (b - 1)))
                    for h in range(2):
                        sp.dma_start(tile(2 + b)[:, 0:FM, :] if h == 0 else tile(2 + b)[:, FM:, :],
                                     wq[h][:, :, bass.ds(i * (2 * P) + b * P, P)]).then_inc(wq_loaded[b], 16)

            u = peer_u[0].rearrange("(e p) d -> e p d", p=P)
            sp.wait_ge(h_ready, 8)

            def load_u(i, b, s, first):
                e = i * 2 + b
                src = u[bass.ds(e, 1)][0] if not isinstance(e, int) else u[e]
                if s == 1:
                    if not first:
                        sp.wait_ge(u_turned, i * (2 * (CH - FLIPPED)) + ((CH - FLIPPED) * (b - 2) + CH - FLIPPED))
                    sp.dma_start(nat[:, b, FW:], src[:, FW:]).then_inc(u_loaded[2 * b + 1], 16)
                    return
                if not first:
                    sp.wait_ge(lo_done, i * (2 * CH) + (C_U + CH * (b - 2) + FLIPPED))
                blocks = src[:, 0:FW].rearrange("(s i) (r w) -> r i s w", s=Q, r=Q)
                for r in range(Q):
                    sp.dma_start(nat[r * B:(r + 1) * B, b, 0:FW].rearrange("i (s w) -> i s w", s=Q), blocks[r]
                                 ).then_inc(u_loaded[2 * b], 16)

            for b in range(2):
                for s in range(2):
                    load_u(0, b, s, True)
            sp.dma_start(h1_spill[:, :], hres.rearrange("p t n -> p (t n)")).then_inc(spilled, 16)
            with sp.Fori(1, EXP_TILES // 2) as i:
                for b in range(2):
                    for s in range(2):
                        load_u(i, b, s, False)

            v = peer_v[0].rearrange("(e p) d -> e p d", p=P)
            sp.wait_ge(u_turned, (CH - FLIPPED) * EXP_TILES)
            sp.wait_ge(lo_done, C_U + CH * EXP_TILES - CH + FLIPPED)
            sp.dma_start(nat[:, 0, :], v[0]).then_inc(v_loaded[0], 16)
            sp.dma_start(nat[:, 1, :], v[1]).then_inc(v_loaded[1], 16)

            def load_v(i):
                for b in range(2):
                    sp.wait_ge(v_lo, i * 2 + (b - 1 + V0))
                    sp.dma_start(nat[:, b, :], v[bass.ds(i * 2 + b, 1)][0]).then_inc(v_loaded[b], 16)

            late = [(store[:, t * D:(t + 1) * D], h1_spill[:, t * D:(t + 1) * D]) for t in range(TT)]
            late += [(store[:, (TT + n) * D:(TT + n + 1) * D], row[0].partition_broadcast(P))
                     for n, row in enumerate((ln2_g, ln2_b))]
            SPACING = 4
            start = PAIRS - SPACING * len(late)
            with sp.Fori(1, start) as i:
                load_v(i)
            for n, (to, src) in enumerate(late):
                sp.dma_start(to, src).then_inc(h1_back, 16)
                with sp.Fori(start + n * SPACING, start + (n + 1) * SPACING) as i:
                    load_v(i)
            for t in range(TT):
                for half in range(2):
                    sp.wait_ge(out_ready, 2 * t + half + 1)
                    cols = slice(half * (D // 2), (half + 1) * (D // 2))
                    sp.dma_start(out[0, t * P:(t + 1) * P, cols],
                                 store[:, t * D + half * (D // 2):t * D + (half + 1) * (D // 2)]).then_inc(stored, 16)
            sp.wait_ge(stored, 16 * 2 * TT)

        @block.gpsimd
        def _(pool):
            def load_gb(g, b):
                pool.dma_start(gb[:, 0, :], g.partition_broadcast(P)).then_inc(gb_loaded, 16)
                pool.dma_start(gb[:, 1, :], b.partition_broadcast(P)).then_inc(gb_loaded, 16)

            for at, rows, src in ((G_Q, QT, q_norm_g[0]), (G_KV, KVT, kv_norm_g[0]), (G_ATT, AT, attn_out_g[0]),
                                  (G_CONV, CT, conv_out_g[0])):
                pool.dma_start(grows[at:at + rows, :], src.rearrange("(k p) -> k p", p=P)).then_inc(small_loaded, 16)
            pool.dma_start(grows[G_CW:G_N, :], conv_w[0].rearrange("j (k p) -> (j k) p", p=P)).then_inc(small_loaded, 16)
            pool.dma_start(sk, peer_sub_keys[0].rearrange("c k d -> k c d")).then_inc(small_loaded, 16)

            def load_head(h, slot, wait):
                if wait is not None:
                    pool.wait_ge(qkv_done, wait)
                uq = att_w[slot][:, 0:QT * 2 * P].rearrange("p (k n) -> p k n", k=QT)
                ukv = att_w[slot][:, QT * 2 * P:].rearrange("p (k n) -> p k n", k=KVT)
                srcq = w_uq[0].rearrange("(k p) n -> p k n", p=P)
                half = D_ROPE // 2
                for to, frm, w in ((0, 0, D_QK), (D_QK, D_NOPE + half, half), (D_QK + half, D_NOPE, half)):
                    pool.dma_start(uq[:, :, to:to + w], srcq[:, :, bass.ds(h * D_QK + frm, w)]
                                   ).then_inc(att_w_loaded[slot], 16)
                pool.dma_start(ukv, w_ukv[0].rearrange("(k p) n -> p k n", p=P)[
                    :, :, bass.ds(h * (D_NOPE + D_V), D_NOPE + D_V)]).then_inc(att_w_loaded[slot], 16)

            pool.wait_ge(meta_std, 1)
            full = [META, D]
            pool.wait_ge(g_loaded, 16)
            pool.wait_ge(b_loaded, 16)
            for n, (operand, op) in enumerate(((mv_meta[:, 0:1].to_broadcast(full), ALU.subtract),
                                               (gb[0:META, 0, :], ALU.mult),
                                               (mv_meta[:, 1:2].to_broadcast(full), ALU.mult),
                                               (gb[0:META, 1, :], ALU.add))):
                if n:
                    pool.wait_ge(meta_step, n)
                nc.gpsimd.tensor_tensor(metab, metab, operand, op).then_inc(meta_step, 1)

            load_head(0, 0, None)
            load_head(1, 1, None)
            pool.wait_ge(h_ready, 4)
            pool.wait_ge(meta_step, 4)
            load_gb(ln1_g[0], ln1_b[0])
            with pool.Fori(1, HEADS // 2) as i:
                load_head(i * 2, 0, i * 6 - 3)
                load_head(i * 2 + 1, 1, i * 6)

            def key_choice(q):
                pool.wait_ge(pick_step, q * PICK_STEPS + HOT_STEP)
                for c in range(2):
                    nc.gpsimd.tensor_tensor(hot[:, c], hot[:, c], tif[:, c, :].unsqueeze(1).to_broadcast([P, TOPK, TOPK]),
                                            ALU.mult).then_inc(hot_keyed, 1)

            with pool.Fori(0, PICKS) as q:
                key_choice(q)

            pool.wait_ge(choice_copied, 2)
            nc.gpsimd.memset(store[:, 2 * GATES_AT * SEQ:], 1.0).then_inc(store_set, 1)

            def second_distance(i, k, first):
                if not first:
                    pool.wait_ge(gates_done, i * (2 * CH) + (k - 1))
                full = [P, NT, P]
                nc.gpsimd.tensor_tensor(
                    second_rows[k % 2].rearrange("p (t k) -> p t k", t=NT), iota.unsqueeze(1).to_broadcast(full),
                    turnedc[:, 1, bass.ds(i * (2 * CH * NT) + k * NT, NT)].unsqueeze(2).to_broadcast(full),
                    ALU.subtract).then_inc(second_diff, 1)

            def gate_first(i, k):
                pool.wait_ge(first_equal, i * (2 * CH) + (k + 1))
                rows = first_rows[k % 2].rearrange("p (t k) -> p t k", t=NT)
                gates = turnedc[:, 2, bass.ds(i * (2 * CH * NT) + k * NT, NT)]
                nc.gpsimd.tensor_tensor(rows, rows, gates.unsqueeze(2).to_broadcast([P, NT, P]), ALU.mult
                                        ).then_inc(first_hot, 1)

            for k in range(2 * CH):
                second_distance(0, k, k < 2)
                gate_first(0, k)
            with pool.Fori(1, PAIRS - GATES_AT) as i:
                for k in range(2 * CH):
                    second_distance(i, k, False)
                    gate_first(i, k)

        @block.tensor
        def _(pe):
            def mm(o, lhsT, rhs, k, n):
                return nc.tensor.matmul(o, lhsT, rhs, start=(k == 0), stop=(k == n - 1))

            def mm3(o, stat, mov, k, n):
                nc.tensor.matmul(o, stat[0], mov[0], start=(k == 0), stop=False)
                nc.tensor.matmul(o, stat[0], mov[1], start=False, stop=False)
                return nc.tensor.matmul(o, stat[1], mov[0], start=False, stop=(k == n - 1))

            def parts(pair, cut):
                return [cut(a) for a in pair]

            def turn(n, ready, base):
                t, g = n // 4, n % 4
                first_part = CH // 2 if base == 0 else FLIPPED
                pe.wait_ge(h_ready, ready + 2 * t + (1 if g < first_part else 2))
                if n >= 6:
                    pe.wait_ge(turned_lo, base + 3)
                for j in range(4):
                    k = 4 * g + j
                    piece = hres[:, t, k * P:(k + 1) * P] if base == 0 else channels(hres[:, t, :], k)
                    last = nc.tensor.transpose(ps[TURN_BANKS[n]][:, j * P:(j + 1) * P], piece, ident)
                last.then_inc(turned, 1)

            pe.wait_ge(ident_loaded, 16)
            for n in range(6):
                turn(n, 0, 0)

            def turn_small():
                pe.wait_ge(small_loaded, 16 * 6)
                nc.tensor.transpose(ps[7][:, 256:256 + G_N], grows, ident[0:G_N, 0:G_N]).then_inc(gains_turned, 1)
                for c in range(2):
                    nc.tensor.transpose(ps[7][:, c * P:(c + 1) * P], sk[:, c, :], ident).then_inc(gains_turned, 1)

            def turn_meta():
                pe.wait_ge(meta_step, 4)
                for k in range(KT):
                    last = nc.tensor.transpose(ps[3][:, k * META:(k + 1) * META], metab[:, k * P:(k + 1) * P],
                                               ident[0:META, 0:META])
                last.then_inc(turned, 1)

            def tile_chunks(o, chunk0, lo, hi_, turning=None):
                for c in range(CH):
                    if turning is not None:
                        if c in (1, 2):
                            turn(5 + c, *turning)
                        pe.wait_ge(turned_lo, turning[1] + 2 * (c + 1))
                    pe.wait_ge(lo_done, chunk0 + (c + 1))
                    for j in range(4):
                        k = 4 * c + j
                        last = mm3(o, parts(chunk_hl[c], lambda a: a[:, j * P:(j + 1) * P]),
                                   parts(act_hl, lambda a: a[:, k, lo:hi_]), k, KT)
                    last.then_inc(chunk_used, 1)

            def project(slot, chunk0, first, turning=None):
                tile_chunks(ps[slot][:, 0:L - first], chunk0, first, L, turning)

            def low_sums():
                pe.wait_ge(consts_loaded, 16)
                pe.wait_ge(squared, QT)
                for k in range(QT):
                    last = mm(ps[3][:, 0:SEQ], ones, sq[:, k, :], k, QT)
                last.then_inc(sums_ready, 1)
                pe.wait_ge(squared, QT + KVT)
                for k in range(KVT):
                    mm(ps[4][:, META:L], ones, sq[:, QT + k, :], k, KVT)
                for k in range(KVT):
                    last = mm(ps[4][:, 0:META], ones, rs[:, 1, k * META:(k + 1) * META], k, KVT)
                last.then_inc(sums_ready, 1)

            def fold_rope():
                pe.wait_ge(kr2_ready, 1)
                nc.tensor.matmul(ps[5][:, 0:L], fold, kr2, start=True, stop=True).then_inc(folded, 1)

            for n in range(FIRST):
                if n >= 3:
                    pe.wait_ge(bank_freed[n % 3], n // 3)
                if n == QT - 1:
                    turn_meta()
                if n == QT:
                    pe.wait_ge(turned_lo, 9)
                project(n % 3, CH * n, META if n < QT else 0, (0, 0) if n == 0 else None)
                if n == 0:
                    turn_small()

            def conv_tiles(i, first):
                for k, slot in enumerate((SC, SH, SB)):
                    pe.wait_ge(bank_freed[slot], i + uses[slot])
                    project(slot, i * (3 * CH) + CH * (FIRST + k), META if k == 2 else 0)
                    if first and k == 0:
                        low_sums()
                    if first and k == 1:
                        fold_rope()

            conv_tiles(0, True)
            with pe.Fori(1, CT) as i:
                conv_tiles(i, False)

            def conv_sums():
                pe.wait_ge(squared, QT + KVT + 1)
                for k in range(CT):
                    last = mm(ps[3][:, 0:SEQ], ones, sq[:, k, :], k, CT)
                last.then_inc(sums_ready, 1)

            def queries_keys(h, b, i):
                pe.wait_ge(att_w_loaded[b], i * 64 + 64)
                after(pe, act_evac, h * 2)
                after(pe, dve_evac, h * 3)
                uq = att_w[b][:, 0:QT * 2 * P].rearrange("p (k n) -> p k n", k=QT)
                ukv = att_w[b][:, QT * 2 * P:].rearrange("p (k n) -> p k n", k=KVT)
                for half in range(2):
                    for k in range(QT):
                        last = mm(ps[7 * half][:, 0:SEQ], uq[:, k, half * P:(half + 1) * P], cq[:, k, :], k, QT)
                last.then_inc(qkv_done, 1)
                for k in range(KVT):
                    last = mm(ps[1][:, 0:L], ukv[:, k, 0:P], ckv[:, k, :], k, KVT)
                last.then_inc(qkv_done, 1)

            def values(h, b):
                ukv = att_w[b][:, QT * 2 * P:].rearrange("p (k n) -> p k n", k=KVT)
                for blk, (c0, w) in enumerate(((META, P), (META + P, P), (0, META))):
                    for k in range(KVT):
                        last = mm(ps[2][0:w, blk * P:(blk + 1) * P], ckv[:, k, c0:c0 + w],
                                  ukv[:, k, P:2 * P], k, KVT)
                last.then_inc(qkv_done, 1)

            def score(h, b):
                pe.wait_ge(act_evac, h * 2 + 2)
                pe.wait_ge(dve_evac, h * 3 + 1)
                after(pe, exped, h * 2)
                for t in range(TT):
                    o = ps[3][:, 0:wk] if t == 0 else ps[3][:, wk:wk + L]
                    w = wk if t == 0 else L
                    mm(o, qn[:, b, t * P:(t + 1) * P], kn[:, b, 0:w], 0, 3)
                    mm(o, qrot[:, b, t * P:(t + 1) * P], krot[:, 0:w], 1, 3)
                    mm(o, maskq, maskk[:, L - w:L], 2, 3).then_inc(scored, 1)

            def turn_softmax(h, b):
                pe.wait_ge(p_ready, h * 2 + 2)
                after(pe, pT_copied, h)
                after(pe, pTm_copied, h)
                for n, c0 in enumerate((META, wk + META, wk + META + P)):
                    last = nc.tensor.transpose(ps[4][:, n * P:(n + 1) * P], pr[:, b, c0:c0 + P], ident)
                last.then_inc(p_turned, 1)
                for n, c0 in enumerate((0, wk)):
                    last = nc.tensor.transpose(ps[5][0:META, n * P:(n + 1) * P], pr[:, b, c0:c0 + META], ident)
                last.then_inc(p_turned, 1)

            def attend(h, b):
                pe.wait_ge(pT_copied, h + 1)
                pe.wait_ge(pTm_copied, h + 1)
                pe.wait_ge(dve_evac, h * 3 + 3)
                after(pe, o_copied, h)
                mm(ps[6][:, 0:P], vt[:, b, 0, :], pT[:, 0, :], 0, 2)
                mm(ps[6][:, 0:P], vt[0:META, b, 2, :], pTm[:, 0, :], 1, 2)
                mm(ps[6][:, P:SEQ], vt[:, b, 0, :], pT[:, 1, :], 0, 3)
                mm(ps[6][:, P:SEQ], vt[:, b, 1, :], pT[:, 2, :], 1, 3)
                mm(ps[6][:, P:SEQ], vt[0:META, b, 2, :], pTm[:, 1, :], 2, 3).then_inc(pv_done, 1)

            pe.wait_ge(normed, 2)
            pe.wait_ge(krot_ready, 1)
            pe.wait_ge(mask_ready, 1)
            for slot in (SC, SH, SB):
                pe.wait_ge(bank_freed[slot], uses[slot] + CT)

            def pair(i, last):
                h = i * 2
                score(h, 0)
                queries_keys(h + 1, 1, i)
                turn_softmax(h, 0)
                values(h + 1, 1)
                attend(h, 0)
                score(h + 1, 1)
                if not last:
                    queries_keys(h + 2, 0, i + 1)
                    turn_softmax(h + 1, 1)
                    values(h + 2, 0)
                else:
                    pe.wait_ge(mixed_lo, 1)
                    for n in range(CH):
                        out_chunk(0, n)
                    turn_softmax(h + 1, 1)
                    out_chunk(0, CH)
                attend(h + 1, 1)

            def out_chunk(i, n, tiles=range(TT)):
                pe.wait_ge(lo_done, C_WO + i * PAIR_CHUNKS + n + 1)
                c, (o, tile) = n % CH, OUT_BLOCKS[n // CH]
                tile += c
                for t in tiles:
                    last = mm3(ps[2 * o + t][:, :], parts(act_hl, lambda a: a[:, tile, t * P:(t + 1) * P]),
                               parts(chunk_hl[c], lambda a: a), (tile - AT) % KT, KT)
                if TT - 1 in tiles:
                    last.then_inc(chunk_used, 1)
                return last

            queries_keys(0, 0, 0)
            values(0, 0)
            conv_sums()
            pe.wait_ge(ms_ready, 3)
            pair(0, False)
            with pe.Fori(1, HEADS // 2 - 1) as i:
                pair(i, False)
            pair(HEADS // 2 - 1, True)
            out_chunk(0, CH + 1)
            pe.wait_ge(head_summed, HEADS)
            nc.tensor.matmul(ps[7][:, 0:SEQ], ones, sqsum[:, 0, :], start=True, stop=True).then_inc(sums_ready, 1)
            for n in range(CH + 2, PAIR_CHUNKS):
                o, tile = OUT_BLOCKS[n // CH]
                if o == 0 and n % CH == 0 and tile < AT:
                    pe.wait_ge(mixed_lo, 2 + tile // CH)
                out_chunk(0, n)
            for n in range(PAIR_CHUNKS - CH):
                if n % (PAIR_CHUNKS // 4) == 0 and n < PAIR_CHUNKS // 2:
                    pe.wait_ge(res_added, TT * (n // (PAIR_CHUNKS // 4) + 1))
                out_chunk(1, n)
            for t in range(TT):
                for n in range(PAIR_CHUNKS - CH, PAIR_CHUNKS):
                    last = out_chunk(1, n, (t,))
                if t == 0:
                    last.then_inc(row_done, 1)

            pe.wait_ge(res_added, TT * GROUPS)
            for n in range(6):
                turn(n, 4, 9)
            pe.wait_ge(gains_copied, 2)

            def query(i, b, turning=None):
                after(pe, pq_copied, i * 2 + (b - 1))
                tile_chunks(ps[6 + b][:, 0:SEQ], i * (2 * CH) + (C_WQ + CH * b), 0, SEQ, turning)

            def key_scores(i, b):
                pe.wait_ge(pq_copied, i * 2 + (b + 1))
                after(pe, scores_kept, i * 2 + (b - 1))
                for t in range(TT):
                    last = nc.tensor.matmul(ps[4 + b][:, t * P:(t + 1) * P], moT[:, b, t * P:(t + 1) * P],
                                            skT[:, b, :], start=True, stop=True)
                last.then_inc(keys_done, 1)

            query(0, 0, (4, 9))
            query(0, 1)
            key_scores(0, 0)
            with pe.Fori(1, HEADS) as i:
                query(i, 0)
                key_scores(i - 1, 1)
                query(i, 1)
                key_scores(i, 0)

            def turn_u(i, b, c):
                pe.wait_ge(u_loaded[2 * b + 1], i * 16 + 16)
                for j in range(4):
                    last = nc.tensor.transpose(ps[c][:, j * P:(j + 1) * P], channels(nat[:, b, :], 4 * c + j), ident)
                last.then_inc(u_turned, 1)

            def gates(i, b, c, first):
                s, o = step_of(i, b, c), c % 2
                pe.wait_ge(second_hot, s + 1)
                pe.wait_ge(first_hot, s + 1)
                if not first:
                    pe.wait_ge(store_step, multiplied(i, b, c - 1 if c >= 2 else c - 2))
                for t in range(NT):
                    last = nc.tensor.matmul(ps[4 + o][:, t * P:(t + 1) * P], second_rows[o][:, t * P:(t + 1) * P],
                                            first_rows[o][:, t * P:(t + 1) * P], start=True, stop=True)
                last.then_inc(gates_done, 1)

            def dot_u(i, b, last_tile=False, with_gates=False, first=False):
                for c in range(CH):
                    pe.wait_ge(lo_done, i * (2 * CH) + (C_U + CH * b + c + 1))
                    if not last_tile and c >= FLIPPED:
                        turn_u(i + b, 1 - b, c)
                    if c == 0:
                        if with_gates and not first:
                            pe.wait_ge(store_step, multiplied(i - 1, b, CH + 1))
                        else:
                            after(pe, gelu_done, i * 2 + (b - 1))
                    for j in range(4):
                        k = 4 * c + j
                        last = mm3(ps[6 + b][:, 0:SEQ], parts(chunk_hl[c], lambda a: a[:, j * P:(j + 1) * P]),
                                   parts(act_hl, lambda a: a[:, k, 0:SEQ]), k, KT)
                    last.then_inc(chunk_used, 1)
                    if with_gates:
                        gates(i, b, c, first and b == 0 and c < 2)

            for c in range(FLIPPED, CH):
                turn_u(0, 0, c)
            key_scores(HEADS - 1, 1)
            dot_u(0, 0)
            dot_u(0, 1)
            with pe.Fori(1, TURNED_AT) as i:
                dot_u(i, 0)
                dot_u(i, 1)

            pe.wait_ge(gate_step, 4)
            pe.wait_ge(scores_kept, 2 * HEADS)
            for c in range(2):
                for t in range(TT):
                    last = nc.tensor.transpose(ps[4][:, (c * TT + t) * P:(c * TT + t + 1) * P],
                                               chosen[:, c, t * P:(t + 1) * P], ident)
            last.then_inc(choice_turned, 1)
            for t in range(TT):
                last = nc.tensor.transpose(ps[5][:, t * P:(t + 1) * P], gate[:, t * P:(t + 1) * P], ident)
            last.then_inc(choice_turned, 1)

            with pe.Fori(TURNED_AT, GATES_AT) as i:
                dot_u(i, 0)
                dot_u(i, 1)
            pe.wait_ge(choice_copied, 2)
            dot_u(GATES_AT, 0, with_gates=True, first=True)
            dot_u(GATES_AT, 1, with_gates=True, first=True)
            with pe.Fori(GATES_AT + 1, PAIRS - 1) as i:
                dot_u(i, 0, with_gates=True)
                dot_u(i, 1, with_gates=True)
            dot_u(PAIRS - 1, 0, with_gates=True)
            dot_u(PAIRS - 1, 1, last_tile=True, with_gates=True)

            pe.wait_ge(store_step, multiplied(PAIRS - 1, 1, CH))

            def product(b, t, g, start=False, stop=False):
                w = parts(w_hl[b], lambda a: a[:, t * P:(t + 1) * P])
                vv = parts(v_hl[b], lambda a: a[:, g * 512:(g + 1) * 512])
                o = ps[4 * t + g][:, :]
                nc.tensor.matmul(o, w[0], vv[0], start=start, stop=False)
                nc.tensor.matmul(o, w[0], vv[1], start=False, stop=False)
                return nc.tensor.matmul(o, w[1], vv[0], start=False, stop=stop)

            def split_done(i, b):
                pe.wait_ge(w_lo, i * 2 + (b + 1))
                pe.wait_ge(v_lo, i * 2 + (b + 1 + V0))

            def times_v(i, b):
                split_done(i, b)
                for t in range(TT):
                    for g in range(4):
                        last = product(b, t, g)
                last.then_inc(v_used, 1)

            pe.wait_ge(w_lo, 1)
            for g in range(4):
                pe.wait_ge(v_lo, g + 1)
                for t in range(TT):
                    if g == 3 and t == TT - 1:
                        pe.wait_ge(store_step, multiplied(PAIRS, 0, 0))
                    last = product(0, t, g, start=True)
            last.then_inc(v_used, 1)
            times_v(0, 1)
            with pe.Fori(1, PAIRS - 1) as i:
                times_v(i, 0)
                times_v(i, 1)
            split_done(PAIRS - 1, 0)
            for t, g in ((0, 0), (0, 1), (0, 2), (0, 3), (1, 0), (1, 1)):
                product(0, t, g)
            split_done(PAIRS - 1, 1)
            for g in range(4):
                product(1, 0, g, stop=True).then_inc(summed, 1)
            for g in range(4):
                if g >= 2:
                    product(0, 1, g)
                product(1, 1, g, stop=True).then_inc(summed, 1)

        @block.scalar
        def _(act):
            def std(n):
                act.wait_ge(var_ready, n)
                nc.scalar.activation(rstd[:, n % 2, 0:1], mv[:, n % 2, 1:2], ACT.Sqrt).then_inc(std_ready, 1)

            def hi_turned(n, base):
                t, g = n // 4, n % 4
                act.wait_ge(turned, base + n + 1)
                lo = (META if base == 0 else 0) + t * P
                nc.scalar.copy(act_hl[0][:, 4 * g:4 * g + 4, lo:lo + P],
                               ps[TURN_BANKS[n]][:, :].rearrange("p (k n) -> p k n", k=4)).then_inc(turned_hi, 1)

            def hi_chunk(c, chunk0, src):
                after(act, chunk_used, chunk0 + (c + 1 - CH))
                nc.scalar.copy(chunk_hl[c][0], src[:, c * CK:(c + 1) * CK]).then_inc(hi_done, 1)

            def hi_chunks(chunk0, src, loaded, count):
                act.wait_ge(loaded, count)
                for c in range(CH):
                    hi_chunk(c, chunk0, src)

            std(1)
            std(2)
            hi_chunks(0, wnat[0], w_loaded[0], 16)
            std(3)
            for n in range(8):
                hi_turned(n, 0)

            def hi_first(n):
                hi_chunks(CH * n, wnat[n % 3], kr_loaded if n == KR_TILE else w_loaded[n % 3],
                          48 if n == KR_TILE else 16 * (n // 3 + 1))

            for n in range(KR_TILE):
                if n == QT - 1:
                    act.wait_ge(turned, 9)
                    nc.scalar.copy(act_hl[0][:, :, 0:META], ps[3][:, 0:KT * META].rearrange("p (k n) -> p k n", k=KT)
                                   ).then_inc(turned_hi, 1)
                hi_first(n + 1)
                act.wait_ge(chunk_used, CH * (n + 1))
                b = ps[n % 3]
                if n < QT:
                    nc.scalar.copy(cq[:, n, :], b[:, 0:SEQ]).then_inc(low_copied, 1)
                    nc.scalar.activation(sq[:, n, :], b[:, 0:SEQ], ACT.Square).then_inc(squared, 1)
                else:
                    k = n - QT
                    nc.scalar.copy(ckv[:, k, :], b[:, 0:L]).then_inc(low_copied, 1)
                    nc.scalar.activation(rs[:, 1, k * META:(k + 1) * META], b[:, 0:META], ACT.Square)
                    nc.scalar.activation(sq[:, n, :], b[:, META:L], ACT.Square).then_inc(squared, 1)
                act.wait_ge(squared, n + 1)
                act.sem_inc(bank_freed[n % 3], 1)
                if n == 0:
                    act.wait_ge(gains_turned, 3)
                    nc.scalar.copy(gains[:, :], ps[7][:, 256:256 + G_N]).then_inc(gains_copied, 1)
                    nc.scalar.copy(skT, ps[7][:, 0:2 * P].rearrange("p (c n) -> p c n", c=2)).then_inc(gains_copied, 1)

            def rms(n, w):
                s = n % 2
                act.wait_ge(ms_ready, n + 1)
                nc.scalar.activation(rs[:, s, 0:w], rs[:, s, 0:w], ACT.Sqrt).then_inc(rms_ready, 1)

            def conv_hi(i, k, slot):
                hi_chunks(i * (3 * CH) + CH * (FIRST + k), wnat[slot], w_loaded[slot], i * 16 + 16 * (fills[slot] + 1))

            def keep_c(i):
                act.wait_ge(chunk_used, i * (3 * CH) + CH * (FIRST + 1))
                act.wait_ge(bank_freed[SH], i + uses[SH])
                nc.scalar.copy(cgate, ps[SC][:, 0:L]).then_inc(bank_freed[SC], 1)

            conv_hi(0, 0, SC)
            conv_hi(0, 1, SH)
            keep_c(0)
            conv_hi(0, 2, SB)
            rms(0, SEQ)
            rms(1, L)
            act.wait_ge(folded, 1)
            nc.scalar.copy(krot, ps[5][:, 0:L]).then_inc(krot_ready, 1)
            with act.Fori(1, CT) as i:
                conv_hi(i, 0, SC)
                conv_hi(i, 1, SH)
                keep_c(i)
                conv_hi(i, 2, SB)
            act.wait_ge(bank_freed[SB], uses[SB] + CT)
            nc.scalar.activation(sq, mixT[:, AT:AT + CT, :], ACT.Square).then_inc(squared, 1)
            hi_chunks(C_WO, wnat[2], w2_loaded[0], 16)

            def head(h, b):
                act.wait_ge(qkv_done, h * 3 + 1)
                nc.scalar.copy(qn[:, b, :], ps[0][:, 0:SEQ]).then_inc(act_evac, 1)
                act.wait_ge(qkv_done, h * 3 + 2)
                nc.scalar.copy(kn[:, b, :], ps[1][:, 0:L]).then_inc(act_evac, 1)

            def softmax_exp(h, b):
                for t in range(TT):
                    lo, w = (0, wk) if t == 0 else (wk, L)
                    act.wait_ge(shifted, h * 2 + 2)
                    nc.scalar.activation(pr[:, b, lo:lo + w], ps[3][:, lo:lo + w], ACT.Exp,
                                         bias=smx[:, b, 2 + t:3 + t], scale=SCALE,
                                         accum_out=smx[:, b, 4 + t:5 + t]).then_inc(exped, 1)

            def output(h, b):
                act.wait_ge(p_turned, h * 2 + 1)
                nc.scalar.copy(pT, ps[4][:, 0:3 * P].rearrange("p (k n) -> p k n", k=3)).then_inc(pT_copied, 1)
                act.wait_ge(pv_done, h + 1)
                nc.scalar.copy(mixT[:, bass.ds(h, 1), :], ps[6][:, 0:SEQ].unsqueeze(1))
                nc.scalar.activation(sq[:, bass.ds(h, 1), :], ps[6][:, 0:SEQ].unsqueeze(1), ACT.Square
                                     ).then_inc(o_copied, 1)

            def pair(i, last):
                h = i * 2
                softmax_exp(h, 0)
                if last:
                    act.wait_ge(normed, 3)
                    nc.scalar.copy(act_hl[0][:, AT:AT + CT, 0:SEQ], mixT[:, AT:AT + CT, :]).then_inc(mixed_hi, 1)
                head(h + 1, 1)
                output(h, 0)
                softmax_exp(h + 1, 1)
                if not last:
                    head(h + 2, 0)
                else:
                    act.wait_ge(w2_loaded[1], 16)
                    hi_chunk(0, C_WO + CH, wnat[3])
                output(h + 1, 1)

            head(0, 0)
            rms(2, SEQ)
            pair(0, False)
            with act.Fori(1, HEADS // 2 - 1) as i:
                pair(i, False)
            pair(HEADS // 2 - 1, True)

            def block_hi(i, n):
                hi_chunks(C_WO + i * PAIR_CHUNKS + CH * n, wnat[2 + n % 2], w2_loaded[n % 2],
                          16 * (len(OUT_BLOCKS) * i // 2 + n // 2 + 1))

            for c in range(1, CH):
                hi_chunk(c, C_WO + CH, wnat[3])
            block_hi(0, 2)
            rms(3, SEQ)
            block_hi(0, 3)
            for half in range(2):
                act.wait_ge(normed, 4 + half)
                tiles = slice(half * (AT // 2), (half + 1) * (AT // 2))
                nc.scalar.copy(act_hl[0][:, tiles, 0:SEQ], mixT[:, tiles, :]).then_inc(mixed_hi, 1)
            for n in range(4, len(OUT_BLOCKS)):
                block_hi(0, n)
            for n in range(len(OUT_BLOCKS)):
                block_hi(1, n)

            def query_hi(i, b):
                hi_chunks(i * (2 * CH) + (C_WQ + CH * b), wnat[2 + b], wq_loaded[b], i * 32 + 32)

            def keep_query(i, b):
                act.wait_ge(chunk_used, i * (2 * CH) + (C_WQ + CH * (b + 1)))
                after(act, keys_done, i * 2 + (b - 1))
                nc.scalar.copy(moT[:, b, :], ps[6 + b][:, 0:SEQ]).then_inc(pq_copied, 1)

            def hi_chunk_u(i, b, c):
                if c < FLIPPED:
                    act.wait_ge(u_flipped, i * (2 * FLIPPED) + (FLIPPED * b + c + 1))
                else:
                    act.wait_ge(u_turned, i * (2 * (CH - FLIPPED)) + ((CH - FLIPPED) * b + c + 1 - FLIPPED))
                act.wait_ge(chunk_used, i * (2 * CH) + (C_U + CH * b + c + 1 - CH))
                nc.scalar.copy(blocked(chunk_hl[c][0]), u_chunk(b, c)).then_inc(hi_done, 1)

            def hi_u(i, b):
                for c in range(CH):
                    hi_chunk_u(i, b, c)

            query_hi(0, 0)
            std(4)
            std(5)
            for n in range(8):
                hi_turned(n, 9)
            query_hi(0, 1)
            keep_query(0, 0)
            with act.Fori(1, HEADS) as i:
                query_hi(i, 0)
                keep_query(i - 1, 1)
                query_hi(i, 1)
                keep_query(i, 0)
            hi_u(0, 0)
            keep_query(HEADS - 1, 1)

            def gelu(i, b, in_place=False):
                act.wait_ge(chunk_used, i * (2 * CH) + (C_U + CH * (b + 1)))
                to = ps[6 + b][:, 0:SEQ].unsqueeze(1) if in_place else by_expert[:, bass.ds(i * 2 + b, 1), :]
                nc.scalar.activation(to, ps[6 + b][:, 0:SEQ].unsqueeze(1), ACT.Gelu).then_inc(gelu_done, 1)

            def act_u(i):
                hi_u(i, 1)
                gelu(i, 0)
                hi_u(i + 1, 0)
                gelu(i, 1)

            act.wait_ge(spilled, 16)
            act_u(0)
            with act.Fori(1, PICKED_AT + 1) as i:
                act_u(i)
            act.wait_ge(gate_step, 1)
            nc.scalar.activation(gate[:, :], gate[:, :], ACT.Exp).then_inc(gate_exped, 1)
            with act.Fori(PICKED_AT + 1, TURNED_AT) as i:
                act_u(i)
            act.wait_ge(choice_turned, 1)
            nc.scalar.copy(turnedc[:, 0:2, :], ps[4][:, :].rearrange("p (c n) -> p c n", c=2)).then_inc(choice_copied, 1)
            act.wait_ge(choice_turned, 2)
            nc.scalar.copy(turnedc[:, 2, :], ps[5][:, 0:SEQ]).then_inc(choice_copied, 1)
            with act.Fori(TURNED_AT, GATES_AT) as i:
                act_u(i)

            def second_square(s, b):
                act.wait_ge(second_diff, s + 1)
                nc.scalar.activation(second_rows[b], second_rows[b], ACT.Square).then_inc(second_sq, 1)

            def second_relu(s, b):
                act.wait_ge(second_sq, s + 1)
                nc.scalar.activation(second_rows[b], second_rows[b], ACT.Relu, scale=-1.0, bias=1.0
                                     ).then_inc(second_hot, 1)

            def act_tile(i, b, last_tile=False):
                for c in range(CH):
                    s, ahead = step_of(i, b, c) + 1, not last_tile or c < CH - 1
                    if ahead:
                        second_square(s, (c + 1) % 2)
                    if not last_tile:
                        hi_chunk_u(i + b, 1 - b, c)
                    if ahead:
                        second_relu(s, (c + 1) % 2)
                if not last_tile:
                    gelu(i, b, in_place=True)

            second_square(0, 0)
            second_relu(0, 0)
            with act.Fori(GATES_AT, PAIRS - 1) as i:
                act_tile(i, 0)
                act_tile(i, 1)
            act_tile(PAIRS - 1, 0)
            act_tile(PAIRS - 1, 1, last_tile=True)

            def split_v(i, b):
                act.wait_ge(v_loaded[b], i * 16 + 16)
                after(act, v_used, i * 2 + (b - 1))
                nc.scalar.copy(v_hl[b][0], nat[:, b, :]).then_inc(v_hi, 1)
                nc.scalar.copy(w_hl[b][0].unsqueeze(1), by_expert[:, bass.ds(i * 2 + b, 1), :]).then_inc(v_hi, 1)

            def quarter(n):
                return slice(n * (D // 4), (n + 1) * (D // 4))

            act.wait_ge(v_loaded[0], 16)
            act.wait_ge(chunk_used, C_U + CH * EXP_TILES)
            nc.scalar.copy(v_hl[0][0][:, quarter(0)], nat[:, 0, quarter(0)]).then_inc(v_hi, 1)
            act.wait_ge(store_step, multiplied(PAIRS - 1, 1, CH))
            nc.scalar.copy(w_hl[0][0].unsqueeze(1), by_expert[:, 0:1, :]).then_inc(v_hi, 1)
            gelu(PAIRS - 1, 1, in_place=True)
            for n in range(1, 4):
                nc.scalar.copy(v_hl[0][0][:, quarter(n)], nat[:, 0, quarter(n)]).then_inc(v_hi, 1)
            split_v(0, 1)
            with act.Fori(1, EXP_TILES // 2) as i:
                split_v(i, 0)
                split_v(i, 1)
            std(6)
            std(7)

        @block.vector
        def _(dve):
            steps = [0]

            def link(ins):
                steps[0] += 1
                ins.then_inc(stat_step, 1)
                dve.wait_ge(stat_step, steps[0])

            norms = [0]

            def deviation(p, t):
                norms[0] += 1
                m = mv[0:p, norms[0] % 2, :]
                link(nc.vector.bn_aggr(m, stats[0:p, t, :, :].rearrange("p j s -> p (j s)")))
                nc.vector.tensor_scalar(m[:, 1:2], m[:, 1:2], EPS, None, ALU.add).then_inc(var_ready, 1)

            def centre(xb, g):
                n = norms[0]
                link(nc.vector.scalar_tensor_tensor(out=xb, in0=xb, scalar=mv[:, n % 2, 0:1], in1=g,
                                                    op0=ALU.subtract, op1=ALU.mult))

            def finish(xb, b, done, halves=(0, 1), cut=D // 2):
                n = norms[0]
                if 0 in halves:
                    dve.wait_ge(std_ready, n)
                    link(nc.vector.reciprocal(rstd[:, n % 2, 1:2], rstd[:, n % 2, 0:1]))
                for half in halves:
                    cols = slice(0, cut) if half == 0 else slice(cut, D)
                    nc.vector.scalar_tensor_tensor(out=xb[:, cols], in0=xb[:, cols], scalar=rstd[:, n % 2, 1:2],
                                                   in1=b[:, cols], op0=ALU.mult, op1=ALU.add).then_inc(done, 1)

            def lo_part(o, src, hi):
                return nc.vector.tensor_tensor(o, src, hi.bitcast(F32), ALU.subtract)

            def lo_turned(n, base):
                t, g = n // 4, n % 4
                dve.wait_ge(turned_hi, base + n + 1)
                lo = (META if base == 0 else 0) + t * P
                lo_part(act_hl[1][:, 4 * g:4 * g + 4, lo:lo + P], ps[TURN_BANKS[n]][:, :].rearrange("p (k n) -> p k n", k=4),
                        act_hl[0][:, 4 * g:4 * g + 4, lo:lo + P]).then_inc(turned_lo, 1)

            def lo_chunk(c, chunk0, src):
                dve.wait_ge(hi_done, chunk0 + (c + 1))
                lo_part(chunk_hl[c][1], src[:, c * CK:(c + 1) * CK], chunk_hl[c][0]).then_inc(lo_done, 1)

            def lo_chunks(chunk0, src):
                for c in range(CH):
                    lo_chunk(c, chunk0, src)

            link(nc.vector.memset(mv[:, :, :], 1.0))
            dve.wait_ge(x_loaded[2 * TT], 16)
            for j in range(4):
                last = nc.vector.bn_stats(stats[0:META, 1, j, :], metab[:, j * 512:(j + 1) * 512])
            link(last)
            deviation(META, 1)
            nc.vector.tensor_copy(mv_meta[:, 0:1], mv[0:META, norms[0] % 2, 0:1])

            def finish_turned(xb, b, base, chunk0, src):
                first_part = CH // 2 if base == 0 else FLIPPED
                for c in range(CH):
                    if c in (0, first_part):
                        finish(xb, b, h_ready, (min(c, 1),), first_part * CK)
                    lo_chunk(c, chunk0, src)
                    lo_turned(c, base)
                    lo_turned(4 + c, base)

            for t in range(TT):
                for j in range(4):
                    dve.wait_ge(x_loaded[2 * t + j // 2], 16)
                    last = nc.vector.bn_stats(stats[:, t, j, :], hres[:, t, j * 512:(j + 1) * 512])
                link(last)
                deviation(P, t)
                dve.wait_ge(g_loaded, 16)
                centre(hres[:, t, :], gb[:, 0, :])
                dve.wait_ge(b_loaded, 16)
                if t == 0:
                    finish(hres[:, t, :], gb[:, 1, :], h_ready)
                    nc.vector.reciprocal(mv_meta[:, 1:2], rstd[0:META, 1, 0:1]).then_inc(meta_std, 1)
                else:
                    finish_turned(hres[:, t, :], gb[:, 1, :], 0, 0, wnat[0])
            for n in range(1, FIRST):
                if n == QT:
                    dve.wait_ge(turned_hi, 9)
                    lo_part(act_hl[1][:, :, 0:META], ps[3][:, 0:KT * META].rearrange("p (k n) -> p k n", k=KT),
                            act_hl[0][:, :, 0:META]).then_inc(turned_lo, 1)
                lo_chunks(CH * n, wnat[n % 3])

            def mean_squares(n, bank, w, dim):
                dve.wait_ge(sums_ready, n + 1)
                nc.vector.tensor_scalar(rs[:, n % 2, 0:w], ps[bank][:, 0:w], 1.0 / dim, EPS, ALU.mult, ALU.add
                                        ).then_inc(ms_ready, 1)

            def invert(n, w):
                dve.wait_ge(rms_ready, n + 1)
                link(nc.vector.reciprocal(rs[:, n % 2, 0:w], rs[:, n % 2, 0:w]))

            def rms_scale(n, w, tiles, gain, piece=None):
                if piece is None:
                    invert(n, w)
                for k, tile in enumerate(tiles):
                    last = nc.vector.scalar_tensor_tensor(out=tile, in0=tile, scalar=gains[:, gain + k:gain + k + 1],
                                                          in1=rs[:, n % 2, 0:w], op0=ALU.mult, op1=ALU.mult)
                    if (k + 1) % (piece or len(tiles)) == 0:
                        last.then_inc(normed, 1)

            def conv_lo(i, k, slot):
                lo_chunks(i * (3 * CH) + CH * (FIRST + k), wnat[slot])

            def convolve(i):
                dve.wait_ge(chunk_used, i * (3 * CH) + CH * (FIRST + 2))
                dve.wait_ge(bank_freed[SC], i + (uses[SC] + 1))
                nc.vector.tensor_tensor(ubuf, ps[SH][:, 0:L], cgate, ALU.mult).then_inc(bank_freed[SH], 1)
                dve.wait_ge(bank_freed[SH], i + (uses[SH] + 1))
                lo = META - CONV_W + 1
                nc.vector.tensor_scalar(ybuf, ubuf[:, lo:lo + SEQ], gains[:, bass.ds(i + G_CW, 1)], None,
                                        ALU.mult).then_inc(conv_step, 1)
                for j in range(1, CONV_W):
                    dve.wait_ge(conv_step, i * CONV_W + j)
                    nc.vector.scalar_tensor_tensor(out=ybuf, in0=ubuf[:, lo + j:lo + j + SEQ],
                                                   scalar=gains[:, bass.ds(i + (G_CW + j * CT), 1)], in1=ybuf,
                                                   op0=ALU.mult, op1=ALU.add).then_inc(conv_step, 1)

            def gate_conv(i):
                dve.wait_ge(conv_step, i * CONV_W + CONV_W)
                dve.wait_ge(chunk_used, i * (3 * CH) + CH * (FIRST + 3))
                nc.vector.tensor_tensor(mixT[:, bass.ds(i + AT, 1), :], ps[SB][:, 0:SEQ].unsqueeze(1),
                                        ybuf.unsqueeze(1), ALU.mult).then_inc(bank_freed[SB], 1)

            conv_lo(0, 0, SC)
            dve.wait_ge(consts_loaded, 16)
            dve.wait_ge(chunk_used, CH * FIRST)
            nc.vector.tensor_tensor(kr2, ps[KR_TILE % 3][:, 0:L], rope, ALU.mult).then_inc(kr2_ready, 1)
            nc.vector.tensor_copy(mask16[:, :], early[0:1, C_MASKQ - C_KEEP:C_MASKK - C_KEEP + L]).then_inc(mask_ready, 1)
            dve.wait_ge(kr2_ready, 1)
            dve.sem_inc(bank_freed[KR_TILE % 3], 1)
            conv_lo(0, 1, SH)
            mean_squares(0, 3, SEQ, Q_RANK)
            mean_squares(1, 4, L, KV_RANK)
            conv_lo(0, 2, SB)
            dve.wait_ge(low_copied, QT + KVT)
            dve.wait_ge(gains_copied, 2)
            convolve(0)
            conv_lo(1, 0, SC)
            gate_conv(0)
            rms_scale(0, SEQ, [cq[:, k, :] for k in range(QT)], G_Q)
            conv_lo(1, 1, SH)
            rms_scale(1, L, [ckv[:, k, :] for k in range(KVT)], G_KV)
            conv_lo(1, 2, SB)
            convolve(1)
            with dve.Fori(2, CT) as i:
                conv_lo(i, 0, SC)
                gate_conv(i - 1)
                conv_lo(i, 1, SH)
                conv_lo(i, 2, SB)
                convolve(i)
            gate_conv(CT - 1)
            lo_chunks(C_WO, wnat[2])

            def rotate_query(h, b):
                dve.wait_ge(qkv_done, h * 3 + 1)
                nc.vector.tensor_tensor(qrot[:, b, :], ps[7][:, 0:SEQ], rope[:, META:L], ALU.mult
                                        ).then_inc(dve_evac, 1)

            def keep_values(h, b):
                dve.wait_ge(qkv_done, h * 3 + 3)
                nc.vector.tensor_copy(vt[:, b, 0:2, :], ps[2][:, 0:2 * P].rearrange("p (k n) -> p k n", k=2)
                                      ).then_inc(dve_evac, 1)
                nc.vector.tensor_copy(vt[0:META, b, 2, :], ps[2][0:META, 2 * P:3 * P]).then_inc(dve_evac, 1)

            def softmax(h, b):
                dve.wait_ge(scored, h * 2 + 2)
                for t in range(TT):
                    lo, w = (0, wk) if t == 0 else (wk, L)
                    nc.vector.tensor_reduce(smx[:, b, t:t + 1], ps[3][:, lo:lo + w], AX.X, ALU.max
                                            ).then_inc(att_step, 1)
                for t in range(TT):
                    dve.wait_ge(att_step, h * 4 + (t + 1))
                    nc.vector.tensor_scalar(smx[:, b, 2 + t:3 + t], smx[:, b, t:t + 1], -SCALE, None, ALU.mult
                                            ).then_inc(shifted, 1)
                for t in range(TT):
                    lo, w = (0, wk) if t == 0 else (wk, L)
                    dve.wait_ge(exped, h * 2 + (t + 1))
                    nc.vector.reciprocal(smx[:, b, 6 + t:7 + t], smx[:, b, 4 + t:5 + t]).then_inc(att_step, 1)
                    dve.wait_ge(att_step, h * 4 + (t + 3))
                    nc.vector.tensor_scalar(pr[:, b, lo:lo + w], pr[:, b, lo:lo + w], smx[:, b, 6 + t:7 + t], None,
                                            ALU.mult).then_inc(p_ready, 1)

            def turned_meta(h):
                dve.wait_ge(p_turned, h * 2 + 2)
                nc.vector.tensor_copy(pTm, ps[5][0:META, 0:2 * P].rearrange("p (k n) -> p k n", k=2)
                                      ).then_inc(pTm_copied, 1)

            def sum_heads(h):
                dve.wait_ge(o_copied, h + 1)
                dve.wait_ge(head_summed, h)
                nc.vector.tensor_tensor(sqsum, sqsum, sq[:, bass.ds(h, 1), :], ALU.add).then_inc(head_summed, 1)

            def pair(i, first=False, last=False):
                h = i * 2
                softmax(h, 0)
                if first:
                    rms_scale(2, SEQ, [mixT[:, AT + k, :] for k in range(CT)], G_CONV)
                if last:
                    dve.wait_ge(mixed_hi, 1)
                    lo_part(act_hl[1][:, AT:AT + CT, 0:SEQ], mixT[:, AT:AT + CT, :], act_hl[0][:, AT:AT + CT, 0:SEQ]
                            ).then_inc(mixed_lo, 1)
                rotate_query(h + 1, 1)
                turned_meta(h)
                keep_values(h + 1, 1)
                if not first:
                    sum_heads(h - 1)
                softmax(h + 1, 1)
                if not last:
                    rotate_query(h + 2, 0)
                    turned_meta(h + 1)
                    keep_values(h + 2, 0)
                else:
                    lo_chunk(0, C_WO + CH, wnat[3])
                    turned_meta(h + 1)
                if first:
                    dve.wait_ge(o_copied, 1)
                    nc.vector.tensor_copy(sqsum, sq[:, 0:1, :]).then_inc(head_summed, 1)
                else:
                    sum_heads(h)

            rotate_query(0, 0)
            keep_values(0, 0)
            mean_squares(2, 3, SEQ, CONV_DIM)
            pair(0, first=True)
            with dve.Fori(1, HEADS // 2 - 1) as i:
                pair(i)
            pair(HEADS // 2 - 1, last=True)
            sum_heads(HEADS - 1)

            def add_residual(i, o, tiles=range(TT)):
                for t in tiles:
                    if tiles == (0,):
                        dve.wait_ge(row_done, 1)
                    else:
                        dve.wait_ge(chunk_used, C_WO + i * PAIR_CHUNKS + (3 + o) * (PAIR_CHUNKS // 4))
                    cols = slice((2 * i + o) * 512, (2 * i + o + 1) * 512)
                    nc.vector.scalar_tensor_tensor(
                        out=hres[:, t, cols], in0=hres[:, t, cols], scalar=ALPHA, in1=ps[2 * o + t][:, :],
                        op0=ALU.mult, op1=ALU.add).then_inc(res_added, 1)

            def row_stats(g, t):
                dve.wait_ge(res_added, g * TT + t + 1)
                return nc.vector.bn_stats(stats[:, t, g, :], hres[:, t, g * 512:(g + 1) * 512])

            def block_lo(i, n):
                lo_chunks(C_WO + i * PAIR_CHUNKS + CH * n, wnat[2 + n % 2])

            for c in range(1, CH):
                lo_chunk(c, C_WO + CH, wnat[3])
            mean_squares(3, 7, SEQ, AT * P)
            block_lo(0, 2)
            invert(3, SEQ)
            for half in range(2):
                rms_scale(3, SEQ, [mixT[:, half * (AT // 2) + k, :] for k in range(AT // 2)], G_ATT + half * (AT // 2),
                          AT // 2)
                if half == 0:
                    block_lo(0, 3)
            for half in range(2):
                dve.wait_ge(mixed_hi, 2 + half)
                tiles = slice(half * (AT // 2), (half + 1) * (AT // 2))
                lo_part(act_hl[1][:, tiles, 0:SEQ], mixT[:, tiles, :], act_hl[0][:, tiles, 0:SEQ]).then_inc(mixed_lo, 1)
            for n in range(4, len(OUT_BLOCKS)):
                block_lo(0, n)
                if n == 6:
                    add_residual(0, 0)
            for n in range(len(OUT_BLOCKS)):
                block_lo(1, n)
                if n == 0:
                    add_residual(0, 1)
                if n in (1, 2):
                    for t in range(TT):
                        row_stats(n - 1, t)
                if n == 6:
                    add_residual(1, 0)
            for t in range(TT):
                row_stats(2, t)
            dve.wait_ge(gb_loaded, 32)
            add_residual(1, 1, (0,))
            link(row_stats(GROUPS - 1, 0))
            deviation(P, 0)
            centre(hres[:, 0, :], gb[:, 0, :])
            add_residual(1, 1, (1,))
            finish(hres[:, 0, :], gb[:, 1, :], h_ready, cut=FW)
            link(row_stats(GROUPS - 1, 1))
            deviation(P, 1)
            centre(hres[:, 1, :], gb[:, 0, :])
            finish_turned(hres[:, 1, :], gb[:, 1, :], 9, C_WQ, wnat[2])

            def query_lo(i, b):
                lo_chunks(i * (2 * CH) + (C_WQ + CH * b), wnat[2 + b])

            by_tile = scores.rearrange("p (t h) c k -> p t (h c k)", t=TT)

            def keep_scores(i, b):
                dve.wait_ge(keys_done, i * 2 + (b + 1))
                nc.vector.tensor_copy(by_tile[:, :, bass.ds(i * (2 * N_KEYS) + b * N_KEYS, N_KEYS)],
                                      ps[4 + b][:, 0:SEQ].rearrange("p (t n) -> p t n", t=TT)
                                      ).then_inc(scores_kept, 1)

            def lo_chunk_u(i, b, c):
                dve.wait_ge(hi_done, i * (2 * CH) + (C_U + CH * b + c + 1))
                lo_part(blocked(chunk_hl[c][1]), u_chunk(b, c), blocked(chunk_hl[c][0])).then_inc(lo_done, 1)

            assert FLIPPED == 3

            def flip_u(i, b, c, n=1):
                dve.wait_ge(u_loaded[2 * b], i * (16 * Q) + 16 * Q)
                blocks = nat[:, b, 0:FW].bitcast(U32).rearrange("p (s j m) -> p s m j", s=Q, m=FM)[
                    :, :, 4 * c:4 * (c + n)]
                nc.vector.transpose(blocks, blocks).then_inc(u_flipped, n)

            def lo_u(i, b, last_tile=False):
                for c in range(CH):
                    lo_chunk_u(i, b, c)
                    if not last_tile:
                        if c == 2:
                            flip_u(i + b, 1 - b, 0)
                        elif c == 3:
                            flip_u(i + b, 1 - b, 1, 2)

            query_lo(0, 1)
            query_lo(1, 0)
            keep_scores(0, 0)
            with dve.Fori(1, HEADS - 1) as i:
                query_lo(i, 1)
                keep_scores(i - 1, 1)
                query_lo(i + 1, 0)
                keep_scores(i, 0)
            query_lo(HEADS - 1, 1)
            keep_scores(HEADS - 2, 1)
            for c in range(FLIPPED):
                flip_u(0, 0, c)
            lo_u(0, 0)
            keep_scores(HEADS - 1, 0)
            keep_scores(HEADS - 1, 1)
            dve.wait_ge(scores_kept, 2 * HEADS)


            def picking(q):
                n = [0]

                def did(ins):
                    n[0] += 1
                    ins.then_inc(pick_step, 1)

                def need():
                    dve.wait_ge(pick_step, q * PICK_STEPS + n[0])
                    dve.sem_inc(pick_passed, 1)

                def lo(part, c):
                    lo_chunk_u(q * 2 + (part + 1) // 2, (part + 1) % 2, c)

                def flip(part, c, n=1):
                    flip_u(q * 2 + (part + 2) // 2, part % 2, c, n)

                both_keys = range(2)
                did(nc.vector.tensor_copy(sc.unsqueeze(1), scores[:, bass.ds(q, 1), :, :]))
                lo(0, 0)
                need()
                for c in both_keys:
                    did(nc.vector.max(tv[:, c, 0:8], sc[:, c, :]))
                lo(0, 1)
                need()
                for c in both_keys:
                    did(nc.vector.max_index(ti[:, c, 0:8], tv[:, c, 0:8], sc[:, c, :]))
                    did(nc.vector.match_replace(sc2[:, c, :], tv[:, c, 0:8], sc[:, c, :], -3.0e38))
                lo(0, 2)
                flip(0, 0)
                lo(0, 3)
                flip(0, 1, 2)
                assert n[0] == STEPS_AT[1]

                need()
                for c in both_keys:
                    did(nc.vector.max(tv[:, c, 8:16], sc2[:, c, :]))
                lo(1, 0)
                need()
                for c in both_keys:
                    did(nc.vector.max_index(ti[:, c, 8:16], tv[:, c, 8:16], sc2[:, c, :]))
                grid = cand.rearrange("p (a b) -> p a b", a=TOPK)
                did(nc.vector.tensor_tensor(grid, tv[:, 0, :].unsqueeze(2).to_broadcast([P, TOPK, TOPK]),
                                            tv[:, 1, :].unsqueeze(1).to_broadcast([P, TOPK, TOPK]), ALU.add))
                lo(1, 1)
                need()
                did(nc.vector.max(bscore[:, 0:8], cand))
                lo(1, 2)
                flip(1, 0)
                lo(1, 3)
                flip(1, 1, 2)
                assert n[0] == STEPS_AT[2]

                need()
                did(nc.vector.max_index(bi[:, 0:8], bscore[:, 0:8], cand))
                did(nc.vector.match_replace(cand2, bscore[:, 0:8], cand, -3.0e38))
                lo(2, 0)
                need()
                did(nc.vector.max(bscore[:, 8:16], cand2))
                lo(2, 1)
                need()
                did(nc.vector.max_index(bi[:, 8:16], bscore[:, 8:16], cand2))
                lo(2, 2)
                flip(2, 0)
                lo(2, 3)
                flip(2, 1, 2)
                assert n[0] == STEPS_AT[3]

                need()
                nc.vector.tensor_copy(tif[:, :, :], ti[:, :, :])
                nc.vector.tensor_copy(gate[:, bass.ds(q * TOPK, TOPK)], bscore[:, :])
                nc.vector.tensor_scalar(bhl[:, 0, :], bi[:, :], 4, None, ALU.logical_shift_right)
                did(nc.vector.tensor_scalar(bhl[:, 1, :], bi[:, :], TOPK - 1, None, ALU.bitwise_and))
                lo(3, 0)
                need()
                did(nc.vector.tensor_copy(bhlf[:, :, :], bhl[:, :, :]))
                lo(3, 1)
                need()
                hot3 = hot.rearrange("p c k j -> p (c k) j")
                pairs = [P, 2 * TOPK, TOPK]
                did(nc.vector.tensor_tensor(
                    hot3, iota[:, 0:TOPK].unsqueeze(1).to_broadcast(pairs),
                    bhlf[:, :, :].rearrange("p c k -> p (c k)").unsqueeze(2).to_broadcast(pairs), ALU.is_equal))
                lo(3, 2)
                flip(3, 0)
                lo(3, 3)
                flip(3, 1, 2)
                dve.wait_ge(hot_keyed, q * 2 + 2)
                did(nc.vector.tensor_reduce(chosen[:, :, bass.ds(q * TOPK, TOPK)], hot, AX.X, ALU.add))
                assert n[0] == PICK_STEPS

            picking(0)
            with dve.Fori(1, PICKS) as q:
                picking(q)

            dve.wait_ge(pick_step, PICKS * PICK_STEPS)

            def dve_u(i):
                lo_u(i, 1)
                lo_u(i + 1, 0)

            g3 = gate[:, :].rearrange("p (q k) -> p q k", k=TOPK)
            full = [P, PICKS, TOPK]
            nc.vector.tensor_copy(gsum[:, 0, :], g3[:, :, 0]).then_inc(gate_started, 1)
            dve.wait_ge(gate_started, 1)
            nc.vector.tensor_tensor(g3, g3, gsum[:, 0, :].unsqueeze(2).to_broadcast(full), ALU.subtract
                                    ).then_inc(gate_step, 1)
            with dve.Fori(PICKED_AT, PICKED_AT + 2) as i:
                dve_u(i)
            dve.wait_ge(gate_exped, 1)
            nc.vector.tensor_reduce(gsum[:, 1, :], g3, AX.X, ALU.add).then_inc(gate_step, 1)
            dve.wait_ge(gate_step, 2)
            nc.vector.reciprocal(gsum[:, 0, :], gsum[:, 1, :]).then_inc(gate_step, 1)
            dve.wait_ge(gate_step, 3)
            nc.vector.tensor_tensor(g3, g3, gsum[:, 0, :].unsqueeze(2).to_broadcast(full), ALU.mult
                                    ).then_inc(gate_step, 1)
            with dve.Fori(PICKED_AT + 2, GATES_AT) as i:
                dve_u(i)

            def hot_first(i, k):
                full = [P, NT, P]
                keys = turnedc[:, 0, bass.ds(i * (2 * CH * NT) + (k * NT - GATES_AT * (2 * CH * NT)), NT)]
                nc.vector.tensor_tensor(first_rows[k % 2].rearrange("p (t k) -> p t k", t=NT),
                                        iota.unsqueeze(1).to_broadcast(full), keys.unsqueeze(2).to_broadcast(full),
                                        ALU.is_equal).then_inc(first_equal, 1)

            def apply_gates(i, b, c):
                after(dve, store_step, multiplied(i, b, c))
                cols = by_expert[:, :, bass.ds(token_of(i, b, c), NT)]
                nc.vector.tensor_tensor(cols, cols, ps[4 + c % 2][:, 0:HALF].rearrange("p (t e) -> p e t", t=NT), ALU.mult
                                        ).then_inc(store_step, 1)

            def apply_gelu(i, b):
                dve.wait_ge(gelu_done, i * 2 + (b + 1))
                dve.wait_ge(store_step, multiplied(i, b, CH))
                place = by_expert[:, bass.ds(i * 2 + b, 1), :]
                nc.vector.tensor_tensor(place, place, ps[6 + b][:, 0:SEQ].unsqueeze(1), ALU.mult).then_inc(store_step, 1)

            def dve_tile(i, b, first=False, last_but_one=False, last_tile=False):
                for c in range(CH):
                    if not first or c > 0:
                        dve.wait_ge(gates_done, step_of(i, b, c))
                    if not last_tile or c < CH - 1:
                        hot_first(i, CH * b + c + 1)
                    if c > 0:
                        apply_gates(i, b, c - 1)
                    elif not first:
                        apply_gates(i + (b - 1), 1 - b, CH - 1)
                    if not last_tile:
                        lo_chunk_u(i + b, 1 - b, c)
                    if c > 0 and not last_tile and not last_but_one:
                        flip_u(i + 1, b, c - 1)
                    if c == 0 and not first:
                        apply_gelu(i + (b - 1), 1 - b)

            dve.wait_ge(choice_copied, 2)
            dve.wait_ge(store_set, 1)
            hot_first(GATES_AT, 0)
            dve_tile(GATES_AT, 0, first=True)
            dve_tile(GATES_AT, 1)
            with dve.Fori(GATES_AT + 1, PAIRS - 1) as i:
                dve_tile(i, 0)
                dve_tile(i, 1)
            dve_tile(PAIRS - 1, 0, last_but_one=True)
            dve_tile(PAIRS - 1, 1, last_tile=True)
            dve.wait_ge(gates_done, STEPS)
            apply_gates(PAIRS - 1, 1, CH - 1)

            for n in range(4):
                dve.wait_ge(v_hi, 1 if n == 0 else n + 2)
                cols = slice(n * (D // 4), (n + 1) * (D // 4))
                lo_part(v_hl[0][1][:, cols], nat[:, 0, cols], v_hl[0][0][:, cols]).then_inc(v_lo, 1)
                if n == 0:
                    dve.wait_ge(v_hi, 2)
                    lo_part(w_hl[0][1].unsqueeze(1), by_expert[:, 0:1, :], w_hl[0][0].unsqueeze(1)).then_inc(w_lo, 1)
                if n == 1:
                    apply_gelu(PAIRS - 1, 1)

            def split_v(i, b):
                dve.wait_ge(v_hi, i * 4 + (2 * b + 1 + V0))
                lo_part(v_hl[b][1], nat[:, b, :], v_hl[b][0]).then_inc(v_lo, 1)
                dve.wait_ge(v_hi, i * 4 + (2 * b + 2 + V0))
                lo_part(w_hl[b][1].unsqueeze(1), by_expert[:, bass.ds(i * 2 + b, 1), :], w_hl[b][0].unsqueeze(1)
                        ).then_inc(w_lo, 1)

            split_v(0, 1)
            with dve.Fori(1, EXP_TILES // 2) as i:
                split_v(i, 0)
                split_v(i, 1)

            dve.wait_ge(h1_back, 64)

            def join(n):
                dve.wait_ge(summed, n + 1)
                tile = store[:, n * 512:(n + 1) * 512]
                nc.vector.scalar_tensor_tensor(out=tile, in0=tile, scalar=ALPHA, in1=ps[n][:, :],
                                               op0=ALU.mult, op1=ALU.add).then_inc(joined, 1)

            join(0)
            for t in range(TT):
                for g in range(4):
                    n = 4 * t + g
                    if g < 3:
                        join(n + 1)
                    dve.wait_ge(joined, n + 1)
                    last = nc.vector.bn_stats(stats[:, t, g, :], store[:, n * 512:(n + 1) * 512])
                link(last)
                deviation(P, t)
                if t == 0:
                    join(4)
                row = store[:, t * D:(t + 1) * D]
                centre(row, store[:, TT * D:(TT + 1) * D])
                finish(row, store[:, (TT + 1) * D:(TT + 2) * D], out_ready)


_INS = ["x", "meta_tokens", "ln0_g", "ln0_b", "w_in", "q_norm_g", "kv_norm_g", "w_uq", "w_ukv", "conv_w",
        "attn_out_g", "conv_out_g", "w_o", "ln1_g", "ln1_b", "peer_w_query", "peer_sub_keys", "peer_u", "peer_v",
        "ln2_g", "ln2_b"]


def kernel(**inputs):
    import concourse.bacc as bacc
    from concourse.bass_utils import run_bass_kernel_spmd

    nc = bacc.Bacc("TRN2", target_bir_lowering=False, num_devices=1)
    arrays, args = {}, []
    for name in _INS + ["const_block"]:
        a = np.ascontiguousarray(inputs[name]) if name in inputs else constants()
        arrays[f"in_{name}"] = a
        args.append(nc.dram_tensor(f"in_{name}", a.shape, mybir.dt.from_np(a.dtype), kind="ExternalInput").ap())
    args.append(nc.dram_tensor("out", (1, SEQ, D), F32, kind="ExternalOutput").ap())
    build(nc, *args)
    return run_bass_kernel_spmd(nc, [arrays], core_ids=[0]).results[0]["out"]
```
